# Optimizing a Trainium2 kernel written in Bass

```python
import math
import jax, jax.numpy as jnp
from jax import lax
import numpy as np

D_MODEL = 2048
BATCH = 1
SEQ = 256
DEPTH = 1

MLA_HEADS = 8
MLA_NOPE = 128
MLA_ROPE = 64
MLA_QK = MLA_NOPE + MLA_ROPE
MLA_V = 128
MLA_Q_RANK = 768
MLA_KV_RANK = 512
MLA_WIDTH = MLA_HEADS * MLA_V
ROPE_THETA = 10000.0
Q_BLOCK = 128
MOBA_HEADS = 8
MOBA_HEAD_DIM = 128
MOBA_WIDTH = MOBA_HEADS * MOBA_HEAD_DIM
MOBA_BLOCK = 256
MOBA_TOPK = 3
MOBA_Q_CHUNK = 16
MIX_WIDTH = MLA_WIDTH + MOBA_WIDTH
IN_SPLITS = [MLA_Q_RANK, MLA_KV_RANK, MLA_ROPE, MOBA_WIDTH, MOBA_WIDTH, MOBA_WIDTH]
IN_COLS = sum(IN_SPLITS)
PEER_HEADS = 8
PEER_NKEYS = 128
PEER_EXPERTS = PEER_NKEYS * PEER_NKEYS
PEER_DKEY = 256
PEER_TOPK = 16
PEER_TOKEN_CHUNK = 128
EPS = 1e-6
NEG = -1e30

kernel_name = 'hymba_mla_moba_peer_layer'

def rmsnorm(x, g):
    xf = x.astype(jnp.float32)
    y = xf * lax.rsqrt(jnp.mean(xf * xf, axis=-1, keepdims=True) + EPS)
    return (y * g.astype(jnp.float32)).astype(x.dtype)

def rope_tables(seq):
    half = MLA_ROPE // 2
    inv_freq = ROPE_THETA ** (-jnp.arange(half, dtype=jnp.float32) / half)
    ang = jnp.arange(seq, dtype=jnp.float32)[:, None] * inv_freq[None, :]
    return jnp.cos(ang), jnp.sin(ang)

def apply_rope(x, cos, sin):
    half = x.shape[-1] // 2
    x1 = x[..., :half].astype(jnp.float32)
    x2 = x[..., half:].astype(jnp.float32)
    return jnp.concatenate([x1 * cos - x2 * sin, x2 * cos + x1 * sin], axis=-1).astype(x.dtype)

def causal_block_attention(q, k, v, scale):
    B, H, S, Dk = q.shape
    Dv = v.shape[-1]
    nblk = S // Q_BLOCK
    qb = q.reshape(B, H, nblk, Q_BLOCK, Dk).transpose(2, 0, 1, 3, 4)
    kpos = jnp.arange(S)

    def one(args):
        qi, i = args
        s = jnp.einsum('bhqd,bhkd->bhqk', qi, k).astype(jnp.float32) * scale
        qpos = i * Q_BLOCK + jnp.arange(Q_BLOCK)
        s = jnp.where(kpos[None, :] <= qpos[:, None], s, NEG)
        p = jax.nn.softmax(s, axis=-1)
        return jnp.einsum('bhqk,bhkd->bhqd', p.astype(v.dtype), v)

    out = lax.map(one, (qb, jnp.arange(nblk)))
    return out.transpose(1, 2, 0, 3, 4).reshape(B, H, S, Dv)

def mla_group(q_lat, kv_lat, k_rope, g_q, w_uq, g_kv, w_ukv):
    B, S, _ = q_lat.shape
    cos, sin = rope_tables(S)
    q = (rmsnorm(q_lat, g_q) @ w_uq).reshape(B, S, MLA_HEADS, MLA_QK).transpose(0, 2, 1, 3)
    q = jnp.concatenate([q[..., :MLA_NOPE], apply_rope(q[..., MLA_NOPE:], cos, sin)], axis=-1)
    kv = (rmsnorm(kv_lat, g_kv) @ w_ukv).reshape(B, S, MLA_HEADS, MLA_NOPE + MLA_V).transpose(0, 2, 1, 3)
    k_r = apply_rope(k_rope, cos, sin)
    k = jnp.concatenate([kv[..., :MLA_NOPE],
                         jnp.broadcast_to(k_r[:, None], (B, MLA_HEADS, S, MLA_ROPE))], axis=-1)
    v = kv[..., MLA_NOPE:]
    o = causal_block_attention(q, k, v, 1.0 / math.sqrt(MLA_QK))
    return o.transpose(0, 2, 1, 3).reshape(B, S, MLA_WIDTH)

def moba_group(q_in, k_in, v_in):
    B, S, _ = q_in.shape
    H, Dh, L, C = MOBA_HEADS, MOBA_HEAD_DIM, MOBA_BLOCK, MOBA_Q_CHUNK
    q = q_in.reshape(B, S, H, Dh).transpose(0, 2, 1, 3)
    k = k_in.reshape(B, S, H, Dh).transpose(0, 2, 1, 3)
    v = v_in.reshape(B, S, H, Dh).transpose(0, 2, 1, 3)
    scale = 1.0 / math.sqrt(Dh)
    slopes = 2.0 ** (-8.0 * (jnp.arange(H, dtype=jnp.float32) + 1.0) / H)
    nb = -(-S // L)
    pad = nb * L - S
    kp = jnp.pad(k, ((0, 0), (0, 0), (0, pad), (0, 0)))
    vp = jnp.pad(v, ((0, 0), (0, 0), (0, pad), (0, 0)))
    kb = kp.reshape(B, H, nb, L, Dh)
    vb = vp.reshape(B, H, nb, L, Dh)
    kmean = jnp.mean(kb.astype(jnp.float32), axis=3)
    pos = jnp.arange(S)
    qblk = pos // L
    gate = jnp.einsum('bhsd,bhnd->bhsn', q.astype(jnp.float32), kmean)
    gate = jnp.where(jnp.arange(nb)[None, :] < qblk[:, None], gate, NEG)
    k_sel = min(MOBA_TOPK, nb)
    _, sel = lax.top_k(gate, k_sel)
    valid = jnp.arange(k_sel)[None, :] < qblk[:, None]
    nc = S // C
    qc = q.reshape(B, H, nc, C, Dh).transpose(2, 0, 1, 3, 4)
    selc = sel.reshape(B, H, nc, C, k_sel).transpose(2, 0, 1, 3, 4)
    validc = valid.reshape(nc, C, k_sel)
    bi = jnp.arange(B)[:, None, None, None]
    hi = jnp.arange(H)[None, :, None, None]
    offs = jnp.arange(L)

    def one(args):
        qi, si, vi, ci = args
        qpos = ci * C + jnp.arange(C)
        own = (ci * C) // L
        kg = kb[bi, hi, si]
        vg = vb[bi, hi, si]
        s_past = jnp.einsum('bhcd,bhcnld->bhcnl', qi, kg).astype(jnp.float32) * scale
        kpos_past = si[..., None] * L + offs
        s_past = s_past - slopes[None, :, None, None, None] * (qpos[None, None, :, None, None] - kpos_past)
        s_past = jnp.where(vi[None, None, :, :, None], s_past, NEG).reshape(B, H, C, k_sel * L)
        ko = lax.dynamic_slice_in_dim(kp, own * L, L, axis=2)
        vo = lax.dynamic_slice_in_dim(vp, own * L, L, axis=2)
        kpos_own = own * L + offs
        s_own = jnp.einsum('bhcd,bhld->bhcl', qi, ko).astype(jnp.float32) * scale
        s_own = s_own - slopes[None, :, None, None] * (qpos[:, None] - kpos_own[None, :])
        s_own = jnp.where(kpos_own[None, :] <= qpos[:, None], s_own, NEG)
        p = jax.nn.softmax(jnp.concatenate([s_past, s_own], axis=-1), axis=-1).astype(v.dtype)
        p_past = p[..., :k_sel * L].reshape(B, H, C, k_sel, L)
        p_own = p[..., k_sel * L:]
        return (jnp.einsum('bhcnl,bhcnld->bhcd', p_past, vg)
                + jnp.einsum('bhcl,bhld->bhcd', p_own, vo))

    out = lax.map(one, (qc, selc, validc, jnp.arange(nc)))
    out = out.transpose(1, 2, 0, 3, 4).reshape(B, H, S, Dh)
    return out.transpose(0, 2, 1, 3).reshape(B, S, MOBA_WIDTH)

def peer(h, w_q, sub_k1, sub_k2, u_tab, v_tab):
    B, S, D = h.shape
    T = B * S
    H, K = PEER_HEADS, PEER_TOPK
    hf = h.reshape(T, D)
    q = (hf @ w_q).reshape(T, H, 2, PEER_DKEY // 2)
    s1 = jnp.einsum('thd,hnd->thn', q[:, :, 0], sub_k1).astype(jnp.float32)
    s2 = jnp.einsum('thd,hnd->thn', q[:, :, 1], sub_k2).astype(jnp.float32)
    v1, i1 = lax.top_k(s1, K)
    v2, i2 = lax.top_k(s2, K)
    cand = (v1[..., :, None] + v2[..., None, :]).reshape(T, H, K * K)
    cand_id = (i1[..., :, None] * PEER_NKEYS + i2[..., None, :]).reshape(T, H, K * K)
    top, slot = lax.top_k(cand, K)
    ids = jnp.take_along_axis(cand_id, slot, axis=-1).reshape(T, H * K)
    g = jax.nn.softmax(top, axis=-1).reshape(T, H * K).astype(h.dtype)
    nchunk = T // PEER_TOKEN_CHUNK

    def one(args):
        hc, ic, gc = args
        a = jax.nn.gelu(jnp.einsum('cd,ckd->ck', hc, u_tab[ic]), approximate=False) * gc
        return jnp.einsum('ck,ckd->cd', a, v_tab[ic])

    out = lax.map(one, (hf.reshape(nchunk, PEER_TOKEN_CHUNK, D),
                        ids.reshape(nchunk, PEER_TOKEN_CHUNK, H * K),
                        g.reshape(nchunk, PEER_TOKEN_CHUNK, H * K)))
    return out.reshape(B, S, D)

def setup_inputs(seed: int = 0) -> dict:
    key = jax.random.key(seed)
    ks = jax.random.split(key, 22)
    L = DEPTH

    def nrm(k, shape, scale):
        return jax.random.normal(k, shape, jnp.float32) * scale

    def gain(k, shape):
        return 1.0 + 0.02 * jax.random.normal(k, shape, jnp.float32)

    return {
        'x': nrm(ks[0], (BATCH, SEQ, D_MODEL), 1.0),
        'c': nrm(ks[1], (BATCH, D_MODEL), 1.0),
        'w_ada': nrm(ks[2], (L, D_MODEL, 6 * D_MODEL), 0.5 * D_MODEL ** -0.5),
        'b_ada': nrm(ks[3], (L, 6 * D_MODEL), 0.01),
        'g_pre_mix': gain(ks[4], (L, D_MODEL)),
        'w_in': nrm(ks[5], (L, D_MODEL, IN_COLS), D_MODEL ** -0.5),
        'g_q_lat': gain(ks[6], (L, MLA_Q_RANK)),
        'w_uq': nrm(ks[7], (L, MLA_Q_RANK, MLA_HEADS * MLA_QK), MLA_Q_RANK ** -0.5),
        'g_kv_lat': gain(ks[8], (L, MLA_KV_RANK)),
        'w_ukv': nrm(ks[9], (L, MLA_KV_RANK, MLA_HEADS * (MLA_NOPE + MLA_V)), MLA_KV_RANK ** -0.5),
        'g_out_mla': gain(ks[10], (L, MLA_WIDTH)),
        'g_out_moba': gain(ks[11], (L, MOBA_WIDTH)),
        'w_out': nrm(ks[12], (L, MIX_WIDTH, D_MODEL), MIX_WIDTH ** -0.5),
        'g_post_mix': gain(ks[13], (L, D_MODEL)),
        'g_pre_ffn': gain(ks[14], (L, D_MODEL)),
        'w_peer_q': nrm(ks[15], (L, D_MODEL, PEER_HEADS * PEER_DKEY), D_MODEL ** -0.5),
        'sub_keys_1': nrm(ks[16], (L, PEER_HEADS, PEER_NKEYS, PEER_DKEY // 2), (PEER_DKEY // 2) ** -0.5),
        'sub_keys_2': nrm(ks[17], (L, PEER_HEADS, PEER_NKEYS, PEER_DKEY // 2), (PEER_DKEY // 2) ** -0.5),
        'u_experts': nrm(ks[18], (L, PEER_EXPERTS, D_MODEL), D_MODEL ** -0.5),
        'v_experts': nrm(ks[19], (L, PEER_EXPERTS, D_MODEL), (PEER_HEADS * PEER_TOPK) ** -0.5),
        'g_post_ffn': gain(ks[20], (L, D_MODEL)),
    }

def reference(x, c, w_ada, b_ada, g_pre_mix, w_in, g_q_lat, w_uq, g_kv_lat, w_ukv,
              g_out_mla, g_out_moba, w_out, g_post_mix, g_pre_ffn, w_peer_q,
              sub_keys_1, sub_keys_2, u_experts, v_experts, g_post_ffn):
    B = x.shape[0]
    cs = jax.nn.silu(c)
    offsets = list(np.cumsum(IN_SPLITS)[:-1])
    for l in range(DEPTH):
        mod = (cs @ w_ada[l] + b_ada[l]).reshape(B, 6, 1, D_MODEL)
        shift1, scale1, gate1 = mod[:, 0], mod[:, 1], mod[:, 2]
        shift2, scale2, gate2 = mod[:, 3], mod[:, 4], mod[:, 5]
        h = rmsnorm(x, g_pre_mix[l]) * (1.0 + scale1) + shift1
        proj = h @ w_in[l]
        q_lat, kv_lat, k_rope, mq, mk, mv = jnp.split(proj, offsets, axis=-1)
        o_mla = mla_group(q_lat, kv_lat, k_rope, g_q_lat[l], w_uq[l], g_kv_lat[l], w_ukv[l])
        o_moba = moba_group(mq, mk, mv)
        o = jnp.concatenate([rmsnorm(o_mla, g_out_mla[l]), rmsnorm(o_moba, g_out_moba[l])], axis=-1)
        x = x + gate1 * rmsnorm(o @ w_out[l], g_post_mix[l])
        h2 = rmsnorm(x, g_pre_ffn[l]) * (1.0 + scale2) + shift2
        y2 = peer(h2, w_peer_q[l], sub_keys_1[l], sub_keys_2[l], u_experts[l], v_experts[l])
        x = x + gate2 * rmsnorm(y2, g_post_ffn[l])
    return x


_drawn_inputs = setup_inputs


def setup_inputs(seed=0):
    import zlib

    import numpy as np

    out = dict(_drawn_inputs(seed))
    spreads = {}
    factors = {'g_q_lat': 4.474, 'g_post_ffn': 8.0}
    for name, (base, spread) in spreads.items():
        noise = np.random.default_rng([zlib.crc32(name.encode()), seed]).standard_normal(out[name].shape)
        drawn = base * np.exp(spread * noise) if base else spread * noise
        out[name] = __import__('jax').numpy.asarray(drawn.astype(out[name].dtype))
    for name, factor in factors.items():
        out[name] = (out[name] * factor).astype(out[name].dtype)
    return out
```

```python
from contextlib import ExitStack

import numpy as np

import concourse.bass as bass
from concourse import mybir

P = 128
D = 2048
T = 256
TT = T // P
KD = D // P
QR, KVR, ROPE, HD = 768, 512, 64, 128
LAT = QR + KVR + ROPE
KQ, KKV = QR // P, KVR // P
MH = 8
W_MOBA = MH * HD
NK = 128
PH, PK = 8, 16
GROUPS = 2
GJ = NK // GROUPS
RING = 4
WRING = 5
TB = 8
EPS = 1e-6
BIG = -1e30

F32 = mybir.dt.float32
F32R = mybir.dt.float32r
U32 = mybir.dt.uint32
ACT = mybir.ActivationFunctionType
ALU = mybir.AluOpType
AX = mybir.AxisListType.X

C_ID, C_ONE, C_IOTA, C_PER = 0, 128, 256, 384
F_DIST, F_MASK, F_COS, F_SIN, F_RQ, F_DK, F_RK, C_FRONT = 0, 384, 768, 1024, 1280, 1408, 1536, 1664


def tables():
    per = np.zeros((P, C_PER), np.float32)
    per[:, C_ID:C_ID + P] = np.eye(P, dtype=np.float32)
    per[:, C_ONE:C_ONE + P] = 1.0
    per[:, C_IOTA:C_IOTA + P] = np.arange(P, dtype=np.float32)[None, :]
    fr = np.zeros((P, C_FRONT), np.float32)
    q = np.arange(T)[:, None]
    k = np.arange(T)[None, :]
    dist = np.where(k <= q, (k - q).astype(np.float32), np.float32(BIG)).astype(np.float32)
    mask = np.where(k <= q, np.float32(0), np.float32(BIG)).astype(np.float32)
    for off, m in ((F_DIST, dist), (F_MASK, mask)):
        fr[:, off:off + P] = m[0:P, 0:P]
        fr[:, off + P:off + 3 * P] = m[P:T, :]
    half = ROPE // 2
    inv = (np.float32(10000.0) ** (-np.arange(half, dtype=np.float32) / np.float32(half))).astype(np.float32)
    ang = (np.arange(T, dtype=np.float32)[:, None] * inv[None, :]).astype(np.float32)
    fr[:, F_COS:F_COS + T] = np.tile(np.cos(ang).T, (4, 1))
    fr[:, F_SIN:F_SIN + T] = np.tile(np.sin(ang).T, (4, 1))
    rot = np.zeros((ROPE, ROPE), np.float32)
    for j in range(half):
        rot[half + j, j] = -1.0
        rot[j, half + j] = 1.0
    fr[0:ROPE, F_RQ:F_RQ + ROPE] = rot
    fr[ROPE:P, F_RQ + ROPE:F_RQ + P] = rot
    eye = np.eye(ROPE, dtype=np.float32)
    fr[0:ROPE, F_DK:F_DK + P] = np.concatenate([eye, eye], 1)
    fr[0:ROPE, F_RK:F_RK + P] = np.concatenate([rot, rot], 1)
    return per, fr


def build(nc, x, c, w_ada, b_ada, g_pre_mix, w_in, g_q_lat, w_uq, g_kv_lat, w_ukv, g_out_mla,
          g_out_moba, w_out, g_post_mix, g_pre_ffn, w_peer_q, sub_keys_1, sub_keys_2, u_experts,
          v_experts, g_post_ffn, const_per, const_front, out):
    base = -(-nc.sbuf_base // 64) * 64
    zone = 16384 + 32768 + 4 * C_PER + 2048 + 3072

    def at(name, off, shape, dt=F32):
        return nc.alloc_sbuf_tensor_at(name, shape, dt, offset=base + off)

    xs = at("xs", 0, [P, TT, D])
    ring = at("ring", 16384, [P, RING, D])
    per = at("per", 49152, [P, C_PER])
    small = at("small", 49152 + 4 * C_PER, [P, 512])
    ridx = at("ridx", 49152 + 4 * C_PER + 2048, [P, 3, T])
    wring = at("wring", zone + 0, [P, WRING, D])
    acc = at("acc", zone + 40960, [P, 2, D])
    act_t = at("act_t", zone + 57344, [P, KD, T])
    lat = at("lat", zone + 73728, [P, 11, T])
    mqk = at("mqk", zone + 84992, [P, 2 * MH, T])
    mv = at("mv", zone + 101376, [P, TT, W_MOBA])
    mla = at("mla", zone + 109568, [P, 7168])
    front = at("front", zone + 138240, [P, C_FRONT])
    work = at("work", zone + 144896, [P, 2560])
    h2 = at("h2", zone + 0, [P, 2, KD, T], F32R)
    gs = at("gs", zone + 32768, [P, GJ, T])
    uv = at("uv", zone + 98304, [P, 2, 2, D], F32R)
    hot_i = at("hot_i", zone + 98304, [P, 2, TB, NK])
    hot_j = at("hot_j", zone + 98304 + 8192, [P, 2, TB, GJ])
    yacc = at("yacc", zone + 131072, [P, TT, D])
    zero = at("zero", zone + 155136, [P, P])
    am = at("am", zone + 147456, [P, 2, 2, T], F32R)

    ident, ones, iota = per[:, 0:P], per[:, P:2 * P], per[:, 2 * P:3 * P]
    col_a = small[:, 0:128]
    col_b = small[:, 128:202]
    g_pm, g_pf = col_a[:, 96:112], col_a[:, 112:128]
    col_c, g_om, g_of = col_b[:, 0:16], col_b[:, 16:32], col_b[:, 32:48]
    g_lat, g_att = col_b[:, 48:58], col_b[:, 58:74]
    mod = small[:, 208:304]
    cs = small[:, 304:320]
    sc1, sc2 = small[:, 320:336], small[:, 336:352]
    gg1, gg2 = small[:, 352:368], small[:, 368:384]
    tmpc = small[:, 384:400]
    st = small[:, 400:512]
    ssq = [st[:, 2 * n:2 * n + 2] for n in range(4)]
    rst = [st[:, 8 + 2 * n:10 + 2 * n] for n in range(4)]
    smax = st[:, 32:36].rearrange("p (b q) -> p b q", b=2)
    nmax = st[:, 36:40].rearrange("p (b q) -> p b q", b=2)
    esum = st[:, 40:44].rearrange("p (b q) -> p b q", b=2)
    erec = st[:, 44:48].rearrange("p (b q) -> p b q", b=2)

    cos, sin = front[:, F_COS:F_COS + T], front[:, F_SIN:F_SIN + T]
    rows = work[:, 0:256]
    sc = work[:, 0:768].rearrange("p (b n) -> p b n", b=2)
    pt = work[:, 768:1536].rearrange("p (b n) -> p b n", b=2)
    rb = work[:, 1536:2048].rearrange("p (g t) -> p g t", g=2)
    krope = work[:, 2048:2304]
    krt = work[:, 2304:2560]
    xn = mla[:, 0:2 * D].rearrange("p (t d) -> p t d", t=TT)
    qn = mla[:, 0:2048].rearrange("p (h t) -> p h t", h=MH)
    kn = mla[:, 2048:4096].rearrange("p (h t) -> p h t", h=MH)
    vv = mla[:, 4096:6144].rearrange("p (b n) -> p b n", b=TT)
    qr = mla[:, 6144:7168].rearrange("p (m t) -> p m t", m=MH // 2)
    sq_lat = mla[:, 0:2560].rearrange("p (k t) -> p k t", k=10)
    rt = mla[:, 4096:5120].rearrange("p (m t) -> p m t", m=MH // 2)
    subt = mv[:, :, :].rearrange("p a b -> p (a b)").rearrange("p (h n) -> p h n", h=16)
    subk = lat[:, 0:8, :].rearrange("p a b -> p (a b)").rearrange("p (h n) -> p h n", h=16)
    rs = xn
    top_v = mla[:, 4096:4352].rearrange("p (h k) -> p h k", h=16)
    top_i = mla[:, 4352:4608].bitcast(U32).rearrange("p (h k) -> p h k", h=16)
    top_f = mla[:, 4608:4864].rearrange("p (h k) -> p h k", h=16)
    pick_v = mla[:, 4864:4992].rearrange("p (h k) -> p h k", h=PH)
    pick_s = mla[:, 4992:5120].bitcast(U32).rearrange("p (h k) -> p h k", h=PH)
    slot_u = mla[:, 5120:5376].bitcast(U32).rearrange("p (s h k) -> p s h k", s=2, h=PH)
    slot_f = mla[:, 5376:5632].rearrange("p (s h k) -> p s h k", s=2, h=PH)
    rout = mla[:, 5632:6400].rearrange("p (t s n) -> p t s n", t=TT, s=3)
    rsum = mla[:, 6400:6416]
    cand = acc[:, 0, :]
    eqs = acc[:, 1, :]

    with ExitStack() as ctx:
        ps = ctx.enter_context(nc.psum_tensor("ps", [P, 8, 512], F32))

        def sem(name):
            return ctx.enter_context(nc.semaphore(name))

        ld_per, ld_front, ld_rows, ld_x, ld_sub = map(sem, ("ld_per", "ld_front", "ld_rows", "ld_x", "ld_sub"))
        w_full = [sem(f"w_full{n}") for n in range(WRING)]
        ada_full = [sem(f"ada_full{n}") for n in range(RING)]
        e_full = [sem(f"e_full{n}") for n in range(RING)]
        w_used = sem("w_used")
        ada_used = sem("ada_used")
        rows_t, rows_ev = sem("rows_t"), sem("rows_ev")
        c_exp = sem("c_exp")
        x_ssq, x_rms, x_sqrt, x_rstd, xn_ok = map(sem, ("x_ssq", "x_rms", "x_sqrt", "x_rstd", "xn_ok"))
        xt_mm, xt_ev = sem("xt_mm"), sem("xt_ev")
        mod_mm, mod_ok = sem("mod_mm"), sem("mod_ok")
        in_ev = sem("in_ev")
        sq_ok, sq_mm, sq_aff, sq_root = map(sem, ("sq_ok", "sq_mm", "sq_aff", "sq_root"))
        lat_n, uq_ev, rot_mm, rope_ok, ukv_ev = map(sem, ("lat_n", "uq_ev", "rot_mm", "rope_ok", "ukv_ev"))
        s_mm, s_add, s_max, s_exp, s_norm, pt_mm, pt_ev, o_mm, o_ev = map(sem, (
            "s_mm", "s_add", "s_max", "s_exp", "s_norm", "pt_mm", "pt_ev", "o_mm", "o_ev"))
        o_norm, diag_ok, gg_mm, gg_ev, y_ssq, y_aff, y_root, x1_ok = map(sem, (
            "o_norm", "diag_ok", "gg_mm", "gg_ev", "y_ssq", "y_aff", "y_root", "x1_ok"))
        n_ssq, n_aff, n_root, n_rstd, xn2_ok, x2t_mm, x2t_ev = map(sem, (
            "n_ssq", "n_aff", "n_root", "n_rstd", "xn2_ok", "x2t_mm", "x2t_ev"))
        sub_mm, sub_ev, pq_ev, ks_mm, ks_ev = map(sem, ("sub_mm", "sub_ev", "pq_ev", "ks_mm", "ks_ev"))
        r_max, r_exp, r_ok, rt_mm, rt_ev, h_hi, h_lo = map(sem, ("r_max", "r_exp", "r_ok", "rt_mm", "rt_ev", "h_hi", "h_lo"))
        u_tr, u_hi, u_split, u_mm, u_gelu = map(sem, ("u_tr", "u_hi", "u_split", "u_mm", "u_gelu"))
        hot_ok, g_mm, g_mul = map(sem, ("hot_ok", "g_mm", "g_mul"))
        v_hi, v_split, v_mm, y_ev = map(sem, ("v_hi", "v_split", "v_mm", "y_ev"))
        f_ssq, f_aff, f_root, f_diag, f_gg, f_out, st_out = map(sem, (
            "f_ssq", "f_aff", "f_root", "f_diag", "f_gg", "f_out", "st_out"))
        y_sum, hot_eq, zero_ok = map(sem, ("y_sum", "hot_eq", "zero_ok"))
        dve_chain, act_chain = sem("dve_chain"), sem("act_chain")
        gs_flat = gs[:, :, :].rearrange("p j t -> p (j t)")

        def column(j):
            return gs[:, bass.ds(j, 1), :].rearrange("p a t -> p (a t)")

        block = ctx.enter_context(nc.Block())

        win = w_in[0].rearrange("(k p) n -> p k n", p=P)
        wuq = w_uq[0].rearrange("(k p) n -> p k n", p=P)
        wukv = w_ukv[0].rearrange("(k p) n -> p k n", p=P)
        wout = w_out[0].rearrange("(k p) n -> p k n", p=P)
        wpq = w_peer_q[0].rearrange("(k p) n -> p k n", p=P)
        stream = []
        first = {}

        def plan(name, srcs):
            first[name] = len(stream)
            stream.extend(srcs)

        for name, c0 in (("mq", LAT), ("mk", LAT + W_MOBA), ("mv", LAT + 2 * W_MOBA)):
            plan(name, [win[:, k:k + 2, c0:c0 + W_MOBA] for k in range(0, KD, 2)])
        plan("lat", [win[:, k:k + 1, 0:LAT] for k in range(KD)])
        plan("uq", [wuq[:, k:k + 1, :] for k in range(KQ)])
        plan("ukv", [wukv[:, k:k + 1, :] for k in range(KKV)])
        plan("out", [wout[:, k:k + 1, :] for k in range(KD)])
        for cg in range(2):
            plan(f"pq{cg}", [wpq[:, k:k + 2, cg * 1024:cg * 1024 + 1024] for k in range(0, KD, 2)])

        names = list(first) + [None]
        end = {n: first[m] if m else len(stream) for n, m in zip(names, names[1:])}

        def w_loads(m):
            return sum(2 if first["uq"] <= n < end["uq"] else 1 for n in range(m % WRING, m + 1, WRING))

        def uq_nope(m):
            return wring[:, m % WRING, 0:MH * HD].rearrange("p (h c) -> p h c", c=HD)

        def uq_rope(m):
            return wring[:, m % WRING, MH * HD:MH * (HD + ROPE)].rearrange("p (h c) -> p h c", c=ROPE)

        def w_slot(m):
            _, k, n = stream[m].shape
            return wring[:, m % WRING, 0:k * n].rearrange("p (k n) -> p k n", k=k)

        uv_dram = [e[0].rearrange("(i j) d -> i j d", j=NK) for e in (u_experts, v_experts)]

        @block.sync
        def _(sp):
            sp.dma_start(per[:, :], const_per).then_inc(ld_per, 16)
            r0 = 0
            for v, n in ((b_ada, 96), (g_pre_mix, 16), (g_pre_ffn, 16)):
                sp.dma_start(rows[r0:r0 + n, 0:P], v.rearrange("a (k p) -> (a k) p", p=P)).then_inc(ld_rows, 16)
                r0 += n
            r0 = 0
            for v, n in ((c, 16), (g_post_mix, 16), (g_post_ffn, 16), (g_q_lat, KQ), (g_kv_lat, KKV),
                         (g_out_mla, MH), (g_out_moba, MH)):
                sp.dma_start(rows[r0:r0 + n, P:2 * P], v.rearrange("a (k p) -> (a k) p", p=P)).then_inc(ld_rows, 16)
                r0 += n
            sp.dma_start(xs[:, :, :], x[0].rearrange("(t p) d -> p t d", p=P)).then_inc(ld_x, 16)
            sp.dma_start(front[:, :], const_front).then_inc(ld_front, 16)
            sp.wait_ge(ada_used, 24)
            for m, src in enumerate(stream):
                if m >= WRING:
                    sp.wait_ge(w_used, m - WRING + 1)
                if m == first["out"]:
                    sp.wait_ge(w_used, end["ukv"])
                    for s, key in enumerate((sub_keys_1, sub_keys_2)):
                        sp.dma_start(subk.rearrange("p (h s) d -> p s h d", s=2)[:, s],
                                     key[0].rearrange("h n d -> n h d")).then_inc(ld_sub, 16)
                if first["uq"] <= m < end["uq"]:
                    hc = src.rearrange("p k (h c) -> p (k h) c", c=HD + ROPE)
                    sp.dma_start(uq_nope(m), hc[:, :, 0:HD]).then_inc(w_full[m % WRING], 16)
                    sp.dma_start(uq_rope(m), hc[:, :, HD:HD + ROPE]).then_inc(w_full[m % WRING], 16)
                else:
                    sp.dma_start(w_slot(m), src).then_inc(w_full[m % WRING], 16)

            sp.wait_ge(ada_used, 96)
            for g in range(GROUPS):
                for phase in range(2):
                    src = uv_dram[phase]
                    j0 = g * GJ
                    taken = (u_tr, v_split)
                    step = (2, 1)
                    for q in range(RING):
                        if phase == 1:
                            sp.wait_ge(u_tr, 2 * ((g + 1) * GJ - RING + q + 1))
                        elif g:
                            sp.wait_ge(v_split, g * GJ - RING + q + 1)
                        sp.dma_start(ring[:, q, :], src[:, j0 + q, :]).then_inc(e_full[q], 16)
                    with sp.Fori(1, GJ // RING) as it:
                        for q in range(RING):
                            sp.wait_ge(taken[phase], (it * RING + (g * GJ - RING + q + 1)) * step[phase])
                            sp.dma_start(ring[:, q, :], src[:, bass.ds(it * RING + (j0 + q), 1), :]
                                         .rearrange("p a d -> p (a d)")).then_inc(e_full[q], 16)
            sp.wait_ge(f_out, TT)
            sp.dma_start(out[0].rearrange("(t p) d -> p t d", p=P), xs[:, :, :]).then_inc(st_out, 16)
            sp.wait_ge(st_out, 16)

        @block.gpsimd
        def _(pool):
            for s in range(6):
                lo = 0
                if s == 0:
                    for q in range(RING):
                        pool.dma_start(ring[:, q, :], w_ada[0, q * P:(q + 1) * P, 0:D]).then_inc(ada_full[q], 16)
                    lo = 1
                with pool.Fori(lo, KD // RING) as it:
                    for q in range(RING):
                        pool.wait_ge(ada_used, it * RING + (s * KD + q - RING + 1))
                        pool.dma_start(ring[:, q, :], w_ada[0, bass.ds((it * RING + q) * P, P), s * D:(s + 1) * D]
                                       ).then_inc(ada_full[q], 16)

        @block.tensor
        def _(pe):
            mm = nc.tensor.matmul

            def w_wait(m):
                pe.wait_ge(w_full[m % WRING], 16 * w_loads(m))

            def half(bank, n):
                return ps[:, bank + n // 2, (n % 2) * T:(n % 2 + 1) * T]

            pe.wait_ge(ld_per, 16)
            pe.wait_ge(ld_rows, 160)
            nc.tensor.transpose(ps[:, 7, 0:P], rows[:, 0:P], ident)
            nc.tensor.transpose(ps[:, 6, 0:74], rows[0:74, P:2 * P], ident[0:74, 0:74]).then_inc(rows_t, 1)

            def x_tiles(k, src, bank, done):
                for kk in (k, k + 1):
                    for t in range(TT):
                        last = nc.tensor.transpose(ps[:, bank, (kk % 2) * T + t * P:(kk % 2) * T + t * P + P],
                                                   src[:, t, kk * P:(kk + 1) * P], ident)
                last.then_inc(done, 1)

            def mod_sum(s):
                pe.wait_ge(ada_used, 16 * (s + 1))
                for k in range(KD):
                    last = mm(ps[:, 7, P + 16 * s + k:P + 16 * s + k + 1], acc[:, s % 2, k * P:(k + 1) * P],
                              ones[:, 0:1], start=True, stop=True)
                last.then_inc(mod_mm, 1)

            pe.wait_ge(rows_ev, 1)
            pe.wait_ge(xn_ok, TT)
            for k in range(0, 14, 2):
                x_tiles(k, xn, k // 2, xt_mm)
            mod_sum(0)
            mod_sum(1)
            pe.wait_ge(xt_ev, 2)
            x_tiles(14, xn, 0, xt_mm)
            pe.wait_ge(xt_ev, KD)

            for n, name in enumerate(("mq", "mk")):
                if n:
                    pe.wait_ge(in_ev, 4 * n)
                for k in range(KD):
                    m = first[name] + k // 2
                    if k % 2 == 0:
                        w_wait(m)
                    for h in range(MH):
                        last = mm(half(0, h), w_slot(m)[:, k % 2, h * P:(h + 1) * P], act_t[:, k, :],
                                  start=k == 0 and h % 2 == 0, stop=k == KD - 1, skip_group_check=True)
                    if k % 2:
                        last.then_inc(w_used, 1)
            pe.wait_ge(in_ev, 8)
            for k in range(KD):
                m = first["mv"] + k // 2
                if k % 2 == 0:
                    w_wait(m)
                for t in range(TT):
                    for n in range(2):
                        last = mm(ps[:, 2 * t + n, :], act_t[:, k, t * P:(t + 1) * P],
                                  w_slot(m)[:, k % 2, n * 512:(n + 1) * 512], start=k == 0, stop=k == KD - 1)
                if k % 2:
                    last.then_inc(w_used, 1)
            pe.wait_ge(mod_ok, 2)
            mod_sum(2)
            mod_sum(3)
            pe.wait_ge(in_ev, 12)
            for k in range(KD):
                m = first["lat"] + k
                w_wait(m)
                for n in range(11):
                    w = P if n < 10 else ROPE
                    last = mm(half(0, n)[0:w], w_slot(m)[:, 0, n * P:n * P + w], act_t[:, k, :],
                              start=k == 0 and n % 2 == 0, stop=k == KD - 1, skip_group_check=True)
                last.then_inc(w_used, 1)
            pe.wait_ge(mod_ok, 4)
            mod_sum(4)
            mod_sum(5)
            pe.wait_ge(sq_ok, 1)
            for g, (a, b) in enumerate(((0, KQ), (KQ, KQ + KKV))):
                for k in range(a, b):
                    last = mm(ps[:, 6, g * T:(g + 1) * T], ones, sq_lat[:, k, :], start=k == a, stop=k == b - 1)
            last.then_inc(sq_mm, 1)
            pe.wait_ge(in_ev, 18)
            pe.wait_ge(lat_n, KQ)
            for k in range(KQ):
                m = first["uq"] + k
                w_wait(m)
                for h in range(MH):
                    mm(half(0, h), uq_nope(m)[:, h, :], lat[:, k, :],
                       start=k == 0 and h % 2 == 0, stop=k == KQ - 1, skip_group_check=True)
                for j in range(MH // 2):
                    last = mm(half(4, j), uq_rope(m)[:, 2 * j:2 * j + 2, :].rearrange("p h c -> p (h c)"),
                              lat[:, k, :], start=k == 0 and j % 2 == 0, stop=k == KQ - 1, skip_group_check=True)
                last.then_inc(w_used, 1)
            pe.wait_ge(ld_front, 16)
            pe.wait_ge(uq_ev, 3)
            pe.wait_ge(lat_n, 10)
            for j in range(MH // 2):
                mm(half(4, j), front[:, F_RQ:F_RQ + P], qr[:, j, :], start=True, stop=True)
            mm(ps[:, 6, 0:T], front[0:ROPE, F_DK:F_DK + P], lat[0:ROPE, 10, :], start=True, stop=True)
            mm(ps[:, 6, T:2 * T], front[0:ROPE, F_RK:F_RK + P], lat[0:ROPE, 10, :], start=True, stop=True
               ).then_inc(rot_mm, 1)
            pe.wait_ge(rope_ok, 1)
            pe.wait_ge(mod_ok, 6)
            for k in range(KKV):
                m = first["ukv"] + k
                w_wait(m)
                for h in range(MH):
                    mm(half(0, h), w_slot(m)[:, 0, h * 256:h * 256 + P], lat[:, KQ + k, :],
                       start=k == 0 and h % 2 == 0, stop=k == KKV - 1, skip_group_check=True)
                wv = w_slot(m)[:, 0, :].rearrange("p (h c) -> p h c", c=256)
                for t in range(TT):
                    for n in range(2):
                        last = mm(ps[:, 4 + 2 * t + n, :], lat[:, KQ + k, t * P:(t + 1) * P],
                                  wv[:, 4 * n:4 * n + 4, P:256], start=k == 0, stop=k == KKV - 1)
                last.then_inc(w_used, 1)

            def scores(h):
                if h == 0:
                    pe.wait_ge(ukv_ev, 4)
                if h >= 3:
                    pe.wait_ge(s_add, h - 2)
                for o, q0, kn_ in ((0, 0, P), (P, P, T)):
                    dst = ps[:, h % 3, o:o + kn_]
                    if h < MH:
                        b = ROPE * (h % 2)
                        mm(dst, qn[:, h, q0:q0 + P], kn[:, h, 0:kn_], start=True, stop=False)
                        last = mm(dst, qr[b:b + ROPE, h // 2, q0:q0 + P], krope[b:b + ROPE, 0:kn_], start=False, stop=True)
                    else:
                        last = mm(dst, mqk[:, h - MH, q0:q0 + P], mqk[:, h, 0:kn_], start=True, stop=True)
                last.then_inc(s_mm, 1)

            def weights_t(h):
                pe.wait_ge(s_norm, h + 1)
                if h >= 2:
                    pe.wait_ge(pt_ev, h - 1)
                for n in range(3):
                    last = nc.tensor.transpose(ps[:, 3 + h % 2, n * P:(n + 1) * P], sc[:, h % 2, n * P:(n + 1) * P], ident)
                last.then_inc(pt_mm, 1)

            def mix(h):
                pe.wait_ge(pt_ev, h + 1)
                if h >= 2:
                    pe.wait_ge(o_ev, h - 1)
                v = vv[:, :, h * P:(h + 1) * P] if h < MH else mv[:, :, (h - MH) * P:(h - MH + 1) * P]
                mm(ps[:, 5 + h % 2, 0:T], v[:, 0, :], pt[:, h % 2, 0:T], start=True, stop=False, skip_group_check=True)
                mm(ps[:, 5 + h % 2, P:T], v[:, 1, :], pt[:, h % 2, T:3 * P], start=False, stop=True,
                   skip_group_check=True).then_inc(o_mm, 1)

            scores(0)
            scores(1)
            for h in range(2 * MH):
                if h + 2 < 2 * MH:
                    scores(h + 2)
                weights_t(h)
                if h:
                    mix(h - 1)
            mix(2 * MH - 1)
            pe.wait_ge(diag_ok, 1)
            pe.wait_ge(s_add, 16)
            pe.wait_ge(pt_ev, 16)
            for k in range(KD):
                last = mm(ps[:, k // 4, (k % 4) * P:(k % 4 + 1) * P], ones, eqs[:, k * P:(k + 1) * P],
                          start=True, stop=True)
            last.then_inc(gg_mm, 1)
            pe.wait_ge(sq_ok, 2)
            for g in range(2):
                for k in range(MH):
                    last = mm(ps[:, 7, g * T:(g + 1) * T], ones, mqk[:, g * MH + k, :], start=k == 0, stop=k == MH - 1)
            last.then_inc(sq_mm, 1)
            pe.wait_ge(gg_ev, 1)
            pe.wait_ge(o_ev, 16)
            for k in range(KD):
                m = first["out"] + k
                w_wait(m)
                pe.wait_ge(o_norm, k + 1)
                for t in range(TT):
                    for n in range(4):
                        last = mm(ps[:, 4 * t + n, :], act_t[:, k, t * P:(t + 1) * P],
                                  w_slot(m)[:, 0, n * 512:(n + 1) * 512], start=k == 0, stop=k == KD - 1)
                last.then_inc(w_used, 1)
            pe.wait_ge(x1_ok, TT)
            pe.wait_ge(xn2_ok, TT)
            for k in range(0, KD, 2):
                x_tiles(k, xn, k // 2, x2t_mm)
            pe.wait_ge(ld_sub, 32)
            pe.wait_ge(x2t_ev, KD)
            for h in range(16):
                last = nc.tensor.transpose(ps[:, 4 + h // 4, (h % 4) * P:(h % 4 + 1) * P], subk[:, h, :], ident)
            last.then_inc(sub_mm, 1)
            for cg in range(2):
                if cg:
                    pe.wait_ge(sub_ev, 1)
                for k in range(KD):
                    m = first[f"pq{cg}"] + k // 2
                    if k % 2 == 0:
                        w_wait(m)
                    for h in range(8):
                        last = mm(half(4 * cg, h), w_slot(m)[:, k % 2, h * P:(h + 1) * P], act_t[:, k, :],
                                  start=k == 0 and h % 2 == 0, stop=k == KD - 1, skip_group_check=True)
                    if k % 2:
                        last.then_inc(w_used, 1)
            pe.wait_ge(sub_ev, 1)
            for t in range(TT):
                pe.wait_ge(pq_ev, 8)
                for h in range(16):
                    last = mm(ps[:, 4 * t + h // 4, (h % 4) * P:(h % 4 + 1) * P], mqk[:, h, t * P:(t + 1) * P],
                              subt[:, h, :], start=True, stop=True)
                last.then_inc(ks_mm, 1)
            pe.wait_ge(ks_ev, TT)
            for t in range(TT):
                pe.wait_ge(r_ok, t + 1)
                for s in range(3):
                    last = nc.tensor.transpose(ps[:, 6 + s // 2, (s % 2) * T + t * P:(s % 2) * T + (t + 1) * P],
                                               rout[:, t, s, :], ident)
            last.then_inc(rt_mm, 1)
            pe.wait_ge(rt_ev, 1)
            pe.wait_ge(h_lo, 1)

            pe.wait_ge(zero_ok, 1)

            def u_transpose(q, full, split):
                pe.wait_ge(e_full[q], full)
                for hf in range(2):
                    if split is not None:
                        pe.wait_ge(u_split, split + hf)
                    for k in range(8):
                        last = nc.tensor.transpose(ps[:, 2 * hf + k // 4, (k % 4) * P:(k % 4 + 1) * P],
                                                   ring[:, q, (8 * hf + k) * P:(8 * hf + k + 1) * P], ident)
                    last.then_inc(u_tr, 1)

            def u_scores(b, split, gelu):
                pe.wait_ge(u_split, split)
                if gelu is not None:
                    pe.wait_ge(u_gelu, gelu)
                dst = ps[:, 4 + b, 0:T]
                for k in range(KD):
                    hi, lo = uv[:, b, 0, k * P:(k + 1) * P], uv[:, b, 1, k * P:(k + 1) * P]
                    mm(dst, hi, h2[:, 0, k, :], start=k == 0, stop=False)
                    mm(dst, hi, h2[:, 1, k, :], start=False, stop=False)
                    last = mm(dst, lo, h2[:, 0, k, :], start=False, stop=k == KD - 1)
                last.then_inc(u_mm, 1)

            for g in range(GROUPS):
                n0 = g * GJ
                f0 = 16 * (2 * n0 // RING)
                for n in range(RING):
                    u_transpose(n % RING, f0 + 16, 2 * (n0 + n - 1) + 1 if n0 + n > 0 else None)
                    if n:
                        u_scores((n - 1) % 2, 2 * (n0 + n), n0 + n - 2 if n0 + n > 2 else None)
                with pe.Fori(1, GJ // RING) as it:
                    for q in range(RING):
                        u_transpose(q, it * 16 + (f0 + 16), it * (2 * RING) + (2 * (n0 + q - 1) + 1))
                        u_scores((q - 1) % 2, it * (2 * RING) + 2 * (n0 + q), it * RING + (n0 + q - 2))
                u_scores(1, 2 * (n0 + GJ), n0 + GJ - 2)

                b0 = g * (T // TB)

                def place(b, ok, mul):
                    pe.wait_ge(hot_ok, ok)
                    if mul is not None:
                        pe.wait_ge(g_mul, mul)
                    for t in range(TB):
                        last = mm(ps[:, 6 + b, t * GJ:(t + 1) * GJ], hot_i[:, b, t, :], hot_j[:, b, t, :],
                                  start=True, stop=True)
                    last.then_inc(g_mm, 1)

                for b in range(2):
                    place(b, b0 + b + 1, b0 + b - 1 if b0 + b > 1 else None)
                with pe.Fori(1, T // TB // 2) as it:
                    for b in range(2):
                        place(b, it * 2 + (b0 + b + 1), it * 2 + (b0 + b - 1))

                pe.wait_ge(g_mul, b0 + T // TB)
                pe.wait_ge(u_gelu, n0 + GJ)
                for bank in range(8):
                    mm(ps[:, bank, 0:P], zero[:, :], zero[:, :], start=True, stop=False, skip_group_check=True)

                def v_mix(q, b, ok):
                    pe.wait_ge(v_split, ok)
                    for t in range(TT):
                        hi, lo = am[:, b, 0, t * P:(t + 1) * P], am[:, b, 1, t * P:(t + 1) * P]
                        for a, part in ((hi, 0), (hi, 1), (lo, 0)):
                            for n in range(4):
                                last = mm(ps[:, 4 * t + n, :], a, uv[:, b, part, n * 512:(n + 1) * 512],
                                          start=False, stop=False, skip_group_check=True)
                    last.then_inc(v_mm, 1)

                with pe.Fori(0, GJ // RING) as it:
                    for q in range(RING):
                        v_mix(q, q % 2, it * RING + (n0 + q + 1))
                pe.wait_ge(y_sum if g else y_ev, 8)
            pe.wait_ge(f_diag, 1)
            for k in range(KD):
                last = mm(ps[:, k // 4, (k % 4) * P:(k % 4 + 1) * P], ones, gs_flat[:, k * P:(k + 1) * P],
                          start=True, stop=True)
            last.then_inc(f_gg, 1)

        @block.scalar
        def _(act):
            fn = nc.scalar.activation
            chain = [0]

            def link(ins):
                chain[0] += 1
                ins.then_inc(act_chain, 1)
                act.wait_ge(act_chain, chain[0])

            act.wait_ge(ld_x, 16)
            for t in range(TT):
                fn(xn[:, t, :], xs[:, t, :], ACT.Square, accum_out=ssq[0][:, t:t + 1]).then_inc(x_ssq, 1)
            act.wait_ge(x_rms, 1)
            fn(rst[0], ssq[0], ACT.Sqrt).then_inc(x_sqrt, 1)
            act.wait_ge(x_rstd, 1)
            for t in range(TT):
                fn(xn[:, t, :], xs[:, t, :], ACT.Copy, scale=rst[0][:, t:t + 1]).then_inc(xn_ok, 1)
            act.wait_ge(rows_ev, 1)
            fn(cs, col_c, ACT.Exp, scale=-1.0).then_inc(c_exp, 1)
            act.wait_ge(mod_ok, 2)
            for k in range(KD):
                if k % 2 == 0:
                    act.wait_ge(xt_mm, k // 2 + 1)
                bank = k // 2 if k < 14 else 0
                fn(act_t[:, k, :], ps[:, bank, (k % 2) * T:(k % 2 + 1) * T], ACT.Identity,
                   bias=mod[:, k:k + 1], scale=sc1[:, k:k + 1]).then_inc(xt_ev, 1)
            for n in range(2):
                act.wait_ge(w_used, end[("mq", "mk")[n]])
                for b in range(4):
                    fn(mqk[:, n * MH + 2 * b:n * MH + 2 * b + 2, :].rearrange("p a t -> p (a t)"), ps[:, b, :],
                       ACT.Copy, scale=HD ** -0.5 if n == 0 else 1.0).then_inc(in_ev, 1)
            act.wait_ge(w_used, end["mv"])
            for b in range(4):
                fn(mv[:, b // 2, (b % 2) * 512:(b % 2 + 1) * 512], ps[:, b, :], ACT.Copy).then_inc(in_ev, 1)
            act.wait_ge(w_used, end["lat"])
            for b in range(5):
                fn(lat[:, 2 * b:2 * b + 2, :].rearrange("p a t -> p (a t)"), ps[:, b, :], ACT.Copy).then_inc(in_ev, 1)
            fn(lat[0:ROPE, 10, :], ps[0:ROPE, 5, 0:T], ACT.Copy).then_inc(in_ev, 1)
            act.wait_ge(in_ev, 18)
            fn(sq_lat, lat[:, 0:10, :], ACT.Square).then_inc(sq_ok, 1)
            act.wait_ge(sq_aff, 1)
            fn(rb, rb, ACT.Sqrt).then_inc(sq_root, 1)
            act.wait_ge(w_used, end["uq"])
            act.wait_ge(lat_n, 10)
            s_qk = (HD + ROPE) ** -0.5
            fn(qr, ps[:, 4:6, :].rearrange("p a (b t) -> p (a b) t", b=2), ACT.Copy, scale=s_qk).then_inc(uq_ev, 1)
            for b in range(2):
                fn(qn[:, 4 * b:4 * b + 4, :].rearrange("p a t -> p (a t)"),
                   ps[:, 2 * b:2 * b + 2, :].rearrange("p a t -> p (a t)"), ACT.Copy, scale=s_qk).then_inc(uq_ev, 1)
            act.wait_ge(w_used, end["ukv"])
            act.wait_ge(rope_ok, 1)
            for b in range(2):
                fn(kn[:, 4 * b:4 * b + 4, :].rearrange("p a t -> p (a t)"),
                   ps[:, 2 * b:2 * b + 2, :].rearrange("p a t -> p (a t)"), ACT.Copy).then_inc(ukv_ev, 1)
            for t in range(TT):
                fn(vv[:, t, :], ps[:, 4 + 2 * t:6 + 2 * t, :].rearrange("p a t -> p (a t)"), ACT.Copy).then_inc(ukv_ev, 1)

            def exp(h):
                act.wait_ge(s_max, h + 1)
                b = h % 2
                fn(sc[:, b, 0:P], sc[:, b, 0:P], ACT.Exp, bias=nmax[:, b, 0:1], accum_out=esum[:, b, 0:1])
                fn(sc[:, b, P:3 * P], sc[:, b, P:3 * P], ACT.Exp, bias=nmax[:, b, 1:2],
                   accum_out=esum[:, b, 1:2]).then_inc(s_exp, 1)

            def weights_out(h):
                act.wait_ge(pt_mm, h + 1)
                if h >= 2:
                    act.wait_ge(o_mm, h - 1)
                fn(pt[:, h % 2, :], ps[:, 3 + h % 2, 0:3 * P], ACT.Copy).then_inc(pt_ev, 1)

            def mixed_out(h):
                act.wait_ge(o_mm, h + 1)
                fn(act_t[:, h, :], ps[:, 5 + h % 2, 0:T], ACT.Copy).then_inc(o_ev, 1)

            for h in range(2 * MH):
                exp(h)
                if h >= 1:
                    weights_out(h - 1)
                if h >= 2:
                    mixed_out(h - 2)
            weights_out(15)
            mixed_out(14)
            mixed_out(15)
            act.wait_ge(o_ev, 16)
            fn(mqk[:, :, :], act_t[:, :, :], ACT.Square).then_inc(sq_ok, 1)
            act.wait_ge(sq_aff, 2)
            fn(rb, rb, ACT.Sqrt).then_inc(sq_root, 1)
            act.wait_ge(gg_mm, 1)
            fn(cand, ps[:, 0:4, :].rearrange("p a n -> p (a n)"), ACT.Copy).then_inc(gg_ev, 1)
            act.wait_ge(w_used, end["out"])
            for t in range(TT):
                fn(xn[:, t, :], ps[:, 4 * t:4 * t + 4, :].rearrange("p a n -> p (a n)"), ACT.Square,
                   accum_out=ssq[1][:, t:t + 1]).then_inc(y_ssq, 1)
            act.wait_ge(y_aff, 1)
            fn(rst[1], ssq[1], ACT.Sqrt).then_inc(y_root, 1)
            act.wait_ge(y_ssq, TT)
            act.wait_ge(x1_ok, TT)
            for t in range(TT):
                fn(xn[:, t, :], xs[:, t, :], ACT.Square, accum_out=ssq[2][:, t:t + 1]).then_inc(n_ssq, 1)
            act.wait_ge(n_aff, 1)
            fn(rst[2], ssq[2], ACT.Sqrt).then_inc(n_root, 1)
            act.wait_ge(n_rstd, 1)
            for t in range(TT):
                fn(xn[:, t, :], xs[:, t, :], ACT.Copy, scale=rst[2][:, t:t + 1]).then_inc(xn2_ok, 1)
            for k in range(KD):
                if k % 2 == 0:
                    act.wait_ge(x2t_mm, k // 2 + 1)
                fn(act_t[:, k, :], ps[:, k // 2, (k % 2) * T:(k % 2 + 1) * T], ACT.Identity,
                   bias=mod[:, 48 + k:49 + k], scale=sc2[:, k:k + 1]).then_inc(x2t_ev, 1)
            for cg in range(2):
                act.wait_ge(w_used, end[f"pq{cg}"])
                for b in range(4):
                    n = 8 * cg + 2 * b
                    fn(mqk[:, n:n + 2, :].rearrange("p a t -> p (a t)"), ps[:, 4 * cg + b, :], ACT.Copy).then_inc(pq_ev, 1)
            for t in range(TT):
                act.wait_ge(ks_mm, t + 1)
                fn(rs[:, t, :], ps[:, 4 * t:4 * t + 4, :].rearrange("p a n -> p (a n)"), ACT.Copy).then_inc(ks_ev, 1)
            act.wait_ge(x2t_ev, KD)
            act.wait_ge(w_used, len(stream))
            fn(h2[:, 0, :, :], act_t[:, :, :], ACT.Copy).then_inc(h_hi, 1)
            for t in range(TT):
                act.wait_ge(r_max, t + 1)
                fn(pick_v, pick_v, ACT.Exp).then_inc(r_exp, 1)
            act.wait_ge(rt_mm, 1)
            fn(ridx[:, :, :].rearrange("p s t -> p (s t)"), ps[:, 6:8, :].rearrange("p a n -> p (a n)")[:, 0:3 * T],
               ACT.Copy).then_inc(rt_ev, 1)
            act.wait_ge(rt_ev, 1)
            act.wait_ge(h_lo, 1)

            def u_high(q, tr, free):
                for hf in range(2):
                    act.wait_ge(u_tr, tr + hf)
                    if free is not None and hf == 0:
                        act.wait_ge(u_mm, free)
                    fn(uv[:, q % 2, 0, hf * 1024:(hf + 1) * 1024],
                       ps[:, 2 * hf:2 * hf + 2, :].rearrange("p a n -> p (a n)"), ACT.Copy).then_inc(u_hi, 1)

            def gelu(b, done, j):
                act.wait_ge(u_mm, done)
                fn(column(j), ps[:, 4 + b, 0:T], ACT.Gelu).then_inc(u_gelu, 1)

            for g in range(GROUPS):
                n0 = g * GJ
                if g:
                    act.wait_ge(v_mm, n0)
                    act.wait_ge(v_split, n0)
                for n in range(RING):
                    u_high(n, 2 * (n0 + n) + 1, n0 + n - 1 if n0 + n > 1 else None)
                    if n:
                        gelu((n - 1) % 2, n0 + n, n - 1)
                with act.Fori(1, GJ // RING) as it:
                    for q in range(RING):
                        u_high(q, it * (2 * RING) + (2 * (n0 + q) + 1), it * RING + (n0 + q - 1))
                        gelu((q - 1) % 2, it * RING + (n0 + q), it * RING + (q - 1))
                gelu(1, n0 + GJ, GJ - 1)

                act.wait_ge(g_mul, (g + 1) * (T // TB))
                act.wait_ge(g_mm, (g + 1) * (T // TB))
                act.wait_ge(u_mm, n0 + GJ)

                def v_high(q, full, free, j):
                    act.wait_ge(e_full[q], full)
                    if free is not None:
                        act.wait_ge(v_mm, free)
                    fn(am[:, q % 2, 0, :], column(j), ACT.Copy)
                    fn(uv[:, q % 2, 0, :], ring[:, q, :], ACT.Copy).then_inc(v_hi, 1)

                f0 = 16 * ((2 * n0 + GJ) // RING)
                for q in range(RING):
                    v_high(q, f0 + 16, n0 + q - 1 if n0 + q > 1 else None, q)
                with act.Fori(1, GJ // RING) as it:
                    for q in range(RING):
                        v_high(q, it * 16 + (f0 + 16), it * RING + (n0 + q - 1), it * RING + q)
                act.wait_ge(v_mm, n0 + GJ)
                if g == 0:
                    for t in range(TT):
                        for n in range(4):
                            fn(yacc[:, t, n * 512:(n + 1) * 512], ps[:, 4 * t + n, :], ACT.Copy).then_inc(y_ev, 1)
                else:
                    act.wait_ge(y_sum, 8)
            for t in range(TT):
                fn(gs_flat[:, (t + 1) * D:(t + 2) * D], yacc[:, t, :], ACT.Square, accum_out=ssq[3][:, t:t + 1]).then_inc(f_ssq, 1)
            act.wait_ge(f_aff, 1)
            fn(rst[3], ssq[3], ACT.Sqrt).then_inc(f_root, 1)

        @block.vector
        def _(dve):
            tt, ts, stt = nc.vector.tensor_tensor, nc.vector.tensor_scalar, nc.vector.scalar_tensor_tensor
            chain = [0]

            def link(ins):
                chain[0] += 1
                ins.then_inc(dve_chain, 1)
                dve.wait_ge(dve_chain, chain[0])

            def rms(src, n):
                return ts(src, src, 1.0 / n, EPS, ALU.mult, ALU.add)

            nc.vector.memset(zero[:, :], 0.0).then_inc(zero_ok, 1)
            dve.wait_ge(x_ssq, TT)
            rms(ssq[0], D).then_inc(x_rms, 1)
            dve.wait_ge(x_sqrt, 1)
            nc.vector.reciprocal(rst[0], rst[0]).then_inc(x_rstd, 1)
            dve.wait_ge(rows_t, 1)
            nc.vector.tensor_copy(col_a, ps[:, 7, 0:P])
            nc.vector.tensor_copy(col_b, ps[:, 6, 0:74]).then_inc(rows_ev, 1)
            dve.wait_ge(c_exp, 1)
            link(ts(cs, cs, 1.0, None, ALU.add))
            link(nc.vector.reciprocal(cs, cs))
            link(tt(cs, cs, col_c, ALU.mult))

            def ada(s, q, full, prev, k, start):
                dve.wait_ge(ada_full[q], full)
                if prev is not None:
                    dve.wait_ge(ada_used, prev)
                if start:
                    ins = ts(acc[:, s % 2, :], ring[:, q, :], cs[:, k:k + 1], None, ALU.mult)
                else:
                    scal = cs[:, k:k + 1] if isinstance(k, int) else cs[:, bass.ds(k, 1)]
                    ins = stt(acc[:, s % 2, :], ring[:, q, :], scal, acc[:, s % 2, :], ALU.mult, ALU.add)
                ins.then_inc(ada_used, 1)

            def section(s):
                if s >= 2:
                    dve.wait_ge(mod_mm, s - 1)
                m0 = s * KD
                for q in range(RING):
                    ada(s, q, 16 * (m0 // RING + 1), m0 + q if q else None, q, q == 0)
                with dve.Fori(1, KD // RING) as it:
                    for q in range(RING):
                        ada(s, q, it * 16 + 16 * (m0 // RING + 1), it * RING + (m0 + q), it * RING + q, False)

            def mod_out(s):
                dve.wait_ge(mod_mm, s // 2 * 2 + 2)
                tt(mod[:, 16 * s:16 * s + 16], ps[:, 7, P + 16 * s:P + 16 * s + 16], col_a[:, 16 * s:16 * s + 16],
                   ALU.add).then_inc(mod_ok if s != 1 else dve_chain, 1)

            section(0)
            section(1)
            mod_out(0)
            mod_out(1)
            chain[0] += 1
            dve.wait_ge(dve_chain, chain[0])
            stt(sc1, mod[:, 16:32], 1.0, g_pm, ALU.add, ALU.mult).then_inc(mod_ok, 1)
            section(2)
            section(3)
            mod_out(2)
            mod_out(3)
            section(4)
            section(5)
            mod_out(4)
            mod_out(5)
            dve.wait_ge(mod_ok, 6)
            stt(sc2, mod[:, 64:80], 1.0, g_pf, ALU.add, ALU.mult)
            tt(gg1, mod[:, 32:48], g_om, ALU.mult)
            link(tt(gg2, mod[:, 80:96], g_of, ALU.mult))

            dve.wait_ge(sq_mm, 1)
            link(ts(rb[:, 0, :], ps[:, 6, 0:T], 1.0 / QR, EPS, ALU.mult, ALU.add))
            ts(rb[:, 1, :], ps[:, 6, T:2 * T], 1.0 / KVR, EPS, ALU.mult, ALU.add).then_inc(sq_aff, 1)
            dve.wait_ge(sq_root, 1)
            link(nc.vector.reciprocal(rb, rb))
            dve.wait_ge(in_ev, 18)
            for k in range(10):
                stt(lat[:, k, :], lat[:, k, :], g_lat[:, k:k + 1], rb[:, int(k >= KQ), :], ALU.mult, ALU.mult
                    ).then_inc(lat_n, 1)
            for k in range(KD):
                ins = ts(eqs[:, k * P:(k + 1) * P], ident, gg1[:, k:k + 1], None, ALU.mult)
            ins.then_inc(diag_ok, 1)
            dve.wait_ge(rot_mm, 1)
            dve.wait_ge(uq_ev, 3)
            cos4, sin4 = (v.unsqueeze(1).to_broadcast([P, MH // 2, T]) for v in (cos, sin))
            tt(rt, ps[:, 4:6, :].rearrange("p a (b t) -> p (a b) t", b=2), sin4, ALU.mult)
            tt(krope, ps[:, 6, 0:T], cos, ALU.mult)
            tt(krt, ps[:, 6, T:2 * T], sin, ALU.mult)
            link(tt(qr, qr, cos4, ALU.mult))
            tt(krope, krope, krt, ALU.add)
            tt(qr, qr, rt, ALU.add).then_inc(rope_ok, 1)

            def biased(h):
                b = h % 2
                dve.wait_ge(s_mm, h + 1)
                if h >= 2:
                    dve.wait_ge(pt_mm, h - 1)
                off, slope = (F_MASK, 1.0) if h < MH else (F_DIST, 2.0 ** (-(h - MH + 1.0)))
                stt(sc[:, b, :], front[:, off:off + 384], slope, ps[:, h % 3, 0:384], ALU.mult, ALU.add).then_inc(s_add, 1)
                dve.wait_ge(s_add, h + 1)
                nc.vector.reduce_max(smax[:, b, 0:1], sc[:, b, 0:P], AX)
                link(nc.vector.reduce_max(smax[:, b, 1:2], sc[:, b, P:3 * P], AX))
                ts(nmax[:, b, :], smax[:, b, :], -1.0, None, ALU.mult).then_inc(s_max, 1)

            def normed(h):
                b = h % 2
                dve.wait_ge(s_exp, h + 1)
                link(nc.vector.reciprocal(erec[:, b, :], esum[:, b, :]))
                ts(sc[:, b, 0:P], sc[:, b, 0:P], erec[:, b, 0:1], None, ALU.mult)
                ts(sc[:, b, P:3 * P], sc[:, b, P:3 * P], erec[:, b, 1:2], None, ALU.mult).then_inc(s_norm, 1)

            biased(0)
            for h in range(2 * MH):
                if h + 1 < 2 * MH:
                    biased(h + 1)
                normed(h)
            dve.wait_ge(sq_mm, 2)
            for g in range(2):
                ins = ts(rb[:, g, :], ps[:, 7, g * T:(g + 1) * T], 1.0 / (MH * HD), EPS, ALU.mult, ALU.add)
            ins.then_inc(sq_aff, 1)
            dve.wait_ge(sq_root, 2)
            link(nc.vector.reciprocal(rb, rb))
            dve.wait_ge(sq_ok, 2)
            for k in range(KD):
                stt(act_t[:, k, :], act_t[:, k, :], g_att[:, k:k + 1], rb[:, k // MH, :], ALU.mult, ALU.mult
                    ).then_inc(o_norm, 1)
            dve.wait_ge(y_ssq, TT)
            rms(ssq[1], D).then_inc(y_aff, 1)
            dve.wait_ge(y_root, 1)
            link(nc.vector.reciprocal(rst[1], rst[1]))
            dve.wait_ge(gg_ev, 1)
            for t in range(TT):
                link(stt(eqs, ps[:, 4 * t:4 * t + 4, :].rearrange("p a n -> p (a n)"), rst[1][:, t:t + 1], cand,
                         ALU.mult, ALU.mult))
                tt(xs[:, t, :], xs[:, t, :], eqs, ALU.add).then_inc(x1_ok, 1)
                dve.wait_ge(x1_ok, t + 1)
            dve.wait_ge(n_ssq, TT)
            rms(ssq[2], D).then_inc(n_aff, 1)
            dve.wait_ge(n_root, 1)
            nc.vector.reciprocal(rst[2], rst[2]).then_inc(n_rstd, 1)
            dve.wait_ge(sub_mm, 1)
            nc.vector.tensor_copy(subt.rearrange("p h n -> p (h n)"),
                                  ps[:, 4:8, :].rearrange("p a n -> p (a n)")).then_inc(sub_ev, 1)
            dve.wait_ge(h_hi, 1)
            tt(h2[:, 1, :, :], act_t[:, :, :], h2[:, 0, :, :].bitcast(F32), ALU.subtract).then_inc(h_lo, 1)

            def top16(n, vals, out_v, out_i):
                for h in range(n):
                    ins = nc.vector.max(out_v[:, h, 0:8], vals(h))
                link(ins)
                for h in range(n):
                    ins = nc.vector.max_index(out_i[:, h, 0:8], out_v[:, h, 0:8], vals(h))
                link(ins)
                for h in range(n):
                    ins = nc.vector.match_replace(vals(h), out_v[:, h, 0:8], vals(h), -3.4e38)
                link(ins)
                for h in range(n):
                    ins = nc.vector.max(out_v[:, h, 8:16], vals(h))
                link(ins)
                for h in range(n):
                    ins = nc.vector.max_index(out_i[:, h, 8:16], out_v[:, h, 8:16], vals(h))
                link(ins)

            cand4 = cand.rearrange("p (h a b) -> p h a b", h=PH, a=PK)
            eq4 = eqs.rearrange("p (h a b) -> p h a b", h=PH, a=PK)
            full = [P, PH, PK, PK]
            for t in range(TT):
                dve.wait_ge(ks_ev, t + 1)
                top16(16, lambda h: rs[:, t, h * NK:(h + 1) * NK], top_v, top_i)
                link(nc.vector.tensor_copy(top_f, top_i))
                tv = top_v.rearrange("p (h s) k -> p h s k", s=2)
                tf = top_f.rearrange("p (h s) k -> p h s k", s=2)
                link(tt(cand4, tv[:, :, 0, :].unsqueeze(3).to_broadcast(full),
                        tv[:, :, 1, :].unsqueeze(2).to_broadcast(full), ALU.add))
                top16(PH, lambda h: cand[:, h * 256:(h + 1) * 256], pick_v, pick_s)
                link(nc.vector.tensor_copy(rsum[:, 0:8].unsqueeze(2), pick_v[:, :, 0:1]))
                tt(pick_v, pick_v, rsum[:, 0:8].unsqueeze(2).to_broadcast([P, PH, PK]), ALU.subtract).then_inc(r_max, 1)
                ts(slot_u[:, 0], pick_s, 4, None, ALU.logical_shift_right)
                link(ts(slot_u[:, 1], pick_s, 15, None, ALU.bitwise_and))
                link(nc.vector.tensor_copy(slot_f, slot_u))
                for s in range(2):
                    link(tt(eq4, slot_f[:, s].unsqueeze(3).to_broadcast(full),
                            iota[:, 0:PK].unsqueeze(1).unsqueeze(1).to_broadcast(full), ALU.is_equal))
                    link(tt(eq4, eq4, tf[:, :, s, :].unsqueeze(2).to_broadcast(full), ALU.mult))
                    link(nc.vector.reduce_sum(rout[:, t, s, :].rearrange("p (h k) -> p h k", h=PH), eq4, AX))
                dve.wait_ge(r_exp, t + 1)
                link(nc.vector.reduce_sum(rsum[:, 0:8], pick_v, AX))
                link(nc.vector.reciprocal(rsum[:, 8:16], rsum[:, 0:8]))
                tt(rout[:, t, 2, :].rearrange("p (h k) -> p h k", h=PH), pick_v,
                   rsum[:, 8:16].unsqueeze(2).to_broadcast([P, PH, PK]), ALU.mult).then_inc(r_ok, 1)
                dve.wait_ge(r_ok, t + 1)
            dve.wait_ge(rt_ev, 1)

            def u_low(b, hi):
                for hf in range(2):
                    dve.wait_ge(u_hi, hi + hf)
                    tt(uv[:, b, 1, hf * 1024:(hf + 1) * 1024], ps[:, 2 * hf:2 * hf + 2, :].rearrange("p a n -> p (a n)"),
                       uv[:, b, 0, hf * 1024:(hf + 1) * 1024].bitcast(F32), ALU.subtract).then_inc(u_split, 1)

            for g in range(GROUPS):
                n0 = g * GJ
                with dve.Fori(0, GJ // RING) as it:
                    for q in range(RING):
                        u_low(q % 2, it * (2 * RING) + (2 * (n0 + q) + 1))

                b0 = g * (T // TB)

                def hots(b, t0, used):
                    if used is not None:
                        dve.wait_ge(g_mm, used)
                    ri, rj, rw = (ridx[:, s, t0].unsqueeze(2) for s in range(3))
                    tt(hot_i[:, b], iota.unsqueeze(1).to_broadcast([P, TB, NK]), ri.to_broadcast([P, TB, NK]), ALU.is_equal)
                    link_h(tt(hot_j[:, b], iota[:, n0:n0 + GJ].unsqueeze(1).to_broadcast([P, TB, GJ]),
                              rj.to_broadcast([P, TB, GJ]), ALU.is_equal))
                    tt(hot_j[:, b], hot_j[:, b], rw.to_broadcast([P, TB, GJ]), ALU.mult).then_inc(hot_ok, 1)

                def times(b, done, t0):
                    dve.wait_ge(g_mm, done)
                    view = gs[:, :, t0].rearrange("p j t -> p t j")
                    tt(view, view, ps[:, 6 + b, :].rearrange("p (t j) -> p t j", t=TB), ALU.mult).then_inc(g_mul, 1)

                def link_h(ins):
                    ins.then_inc(hot_eq, 1)
                    dve.wait_ge(hot_eq, eq_at[0])

                eq_at = [0]
                dve.wait_ge(u_mm, n0 + GJ)
                dve.wait_ge(u_gelu, n0 + GJ)
                nb = T // TB
                for b in range(2):
                    eq_at[0] = b0 + b + 1
                    hots(b, bass.ds(b * TB, TB), None)
                with dve.Fori(1, nb // 2) as it:
                    for b in range(2):
                        times(b, it * 2 + (b0 + b - 1), bass.ds(it * (2 * TB) + (b - 2) * TB, TB))
                        eq_at[0] = it * 2 + (b0 + b + 1)
                        hots(b, bass.ds(it * (2 * TB) + b * TB, TB), it * 2 + (b0 + b - 1))
                for b in range(2):
                    times(b, b0 + nb - 1 + b, bass.ds((nb - 2 + b) * TB, TB))

                def v_low(q, hi, j):
                    dve.wait_ge(v_hi, hi)
                    tt(am[:, q % 2, 1, :], column(j), am[:, q % 2, 0, :].bitcast(F32), ALU.subtract)
                    tt(uv[:, q % 2, 1, :], ring[:, q, :], uv[:, q % 2, 0, :].bitcast(F32), ALU.subtract).then_inc(v_split, 1)

                dve.wait_ge(g_mul, b0 + nb)
                with dve.Fori(0, GJ // RING) as it:
                    for q in range(RING):
                        v_low(q, it * RING + (n0 + q + 1), it * RING + q)
                if g == 0:
                    dve.wait_ge(y_ev, 8)
                else:
                    dve.wait_ge(v_mm, n0 + GJ)
                    for t in range(TT):
                        for n in range(4):
                            tt(yacc[:, t, n * 512:(n + 1) * 512], yacc[:, t, n * 512:(n + 1) * 512], ps[:, 4 * t + n, :],
                               ALU.add).then_inc(y_sum, 1)
            for k in range(KD):
                ins = ts(gs_flat[:, k * P:(k + 1) * P], ident, gg2[:, k:k + 1], None, ALU.mult)
            ins.then_inc(f_diag, 1)
            dve.wait_ge(f_ssq, TT)
            rms(ssq[3], D).then_inc(f_aff, 1)
            dve.wait_ge(f_root, 1)
            link(nc.vector.reciprocal(rst[3], rst[3]))
            dve.wait_ge(f_gg, 1)
            for t in range(TT):
                link(stt(yacc[:, t, :], yacc[:, t, :], rst[3][:, t:t + 1], ps[:, 0:4, :].rearrange("p a n -> p (a n)"),
                         ALU.mult, ALU.mult))
                tt(xs[:, t, :], xs[:, t, :], yacc[:, t, :], ALU.add).then_inc(f_out, 1)


def kernel(**inputs):
    import concourse.bacc as bacc
    from concourse.bass_utils import run_bass_kernel_spmd

    names = ["x", "c", "w_ada", "b_ada", "g_pre_mix", "w_in", "g_q_lat", "w_uq", "g_kv_lat", "w_ukv", "g_out_mla",
             "g_out_moba", "w_out", "g_post_mix", "g_pre_ffn", "w_peer_q", "sub_keys_1", "sub_keys_2", "u_experts",
             "v_experts", "g_post_ffn"]
    nc = bacc.Bacc("TRN2", target_bir_lowering=False, num_devices=1)
    arrays = {name: np.ascontiguousarray(inputs[name]) for name in names}
    arrays["const_per"], arrays["const_front"] = tables()
    args = {name: nc.dram_tensor(name, a.shape, F32, kind="ExternalInput").ap() for name, a in arrays.items()}
    out = nc.dram_tensor("out", (1, T, D), F32, kind="ExternalOutput").ap()
    build(nc, **args, out=out)
    r = run_bass_kernel_spmd(nc, [arrays], core_ids=[0])
    return r.results[0]["out"]
```

```python
from contextlib import ExitStack

import numpy as np

import concourse.bass as bass
from concourse import mybir

P = 128
D = 2048
T = 256
TT = T // P
KD = D // P
QR, KVR, ROPE, HD = 768, 512, 64, 128
LAT = QR + KVR + ROPE
KQ, KKV = QR // P, KVR // P
MH = 8
W_MOBA = MH * HD
NK = 128
PH, PK = 8, 16
GROUPS = 4
GJ = NK // GROUPS
RING = 4
WRING = 4
ROUTE_STEPS = 20
TB = 8
EPS = 1e-6
BIG = -1e30
BF16 = mybir.dt.bfloat16

F32 = mybir.dt.float32
F32R = mybir.dt.float32r
U32 = mybir.dt.uint32
ACT = mybir.ActivationFunctionType
ALU = mybir.AluOpType
AX = mybir.AxisListType.X

C_ID, C_ONE, C_IOTA, C_PER = 0, 128, 256, 384
ADA_EARLY = 70
LAT_BANKS = (4, 5, 6, 0, 1, 2)
F_DIST, F_MASK, F_COS, F_SIN, F_RQ, F_DK, F_RK, C_FRONT = 0, 384, 768, 1024, 1280, 1408, 1536, 1664


def tables():
    per = np.zeros((P, C_PER), np.float32)
    per[:, C_ID:C_ID + P] = np.eye(P, dtype=np.float32)
    per[:, C_ONE:C_ONE + P] = 1.0
    per[:, C_IOTA:C_IOTA + P] = np.arange(P, dtype=np.float32)[None, :]
    fr = np.zeros((P, C_FRONT), np.float32)
    q = np.arange(T)[:, None]
    k = np.arange(T)[None, :]
    dist = np.where(k <= q, (k - q).astype(np.float32), np.float32(BIG)).astype(np.float32)
    mask = np.where(k <= q, np.float32(0), np.float32(BIG)).astype(np.float32)
    for off, m in ((F_DIST, dist), (F_MASK, mask)):
        fr[:, off:off + P] = m[0:P, 0:P]
        fr[:, off + P:off + 3 * P] = m[P:T, :]
    half = ROPE // 2
    inv = (np.float32(10000.0) ** (-np.arange(half, dtype=np.float32) / np.float32(half))).astype(np.float32)
    ang = (np.arange(T, dtype=np.float32)[:, None] * inv[None, :]).astype(np.float32)
    fr[:, F_COS:F_COS + T] = np.tile(np.cos(ang).T, (4, 1))
    fr[:, F_SIN:F_SIN + T] = np.tile(np.sin(ang).T, (4, 1))
    rot = np.zeros((ROPE, ROPE), np.float32)
    for j in range(half):
        rot[half + j, j] = -1.0
        rot[j, half + j] = 1.0
    fr[0:ROPE, F_RQ:F_RQ + ROPE] = rot
    fr[ROPE:P, F_RQ + ROPE:F_RQ + P] = rot
    eye = np.eye(ROPE, dtype=np.float32)
    fr[0:ROPE, F_DK:F_DK + P] = np.concatenate([eye, eye], 1)
    fr[0:ROPE, F_RK:F_RK + P] = np.concatenate([rot, rot], 1)
    return per, fr


def build(nc, x, c, w_ada, b_ada, g_pre_mix, w_in, g_q_lat, w_uq, g_kv_lat, w_ukv, g_out_mla,
          g_out_moba, w_out, g_post_mix, g_pre_ffn, w_peer_q, sub_keys_1, sub_keys_2, u_experts,
          v_experts, g_post_ffn, const_per, const_front, out):
    base = -(-nc.sbuf_base // 64) * 64
    zone = 16384 + 32768 + 4 * C_PER + 2048 + 2048

    def at(name, off, shape, dt=F32):
        return nc.alloc_sbuf_tensor_at(name, shape, dt, offset=base + off)

    xs = at("xs", 0, [P, TT, D])
    ring = at("ring", 16384, [P, RING, D])
    per = at("per", 49152, [P, C_PER])
    small = at("small", 49152 + 4 * C_PER, [P, 512])
    ridx = at("ridx", 49152 + 4 * C_PER + 2048, [P, 2, T])
    wring = at("wring", zone + 0, [P, WRING, D])
    wlo = at("wlo", zone + 0, [P, WRING, D], F32R)
    whi = [at("whi0", zone + 32768, [P, D], F32R), at("whi1", zone + 142336, [P, D], F32R)]
    acc = at("acc", zone + 40960, [P, 2, D])
    act_t = at("act_t", zone + 57344, [P, KD, T])
    lat = at("lat", zone + 73728, [P, 11, T])
    mqk = at("mqk", zone + 84992, [P, 2 * MH, T])
    mv = at("mv", zone + 101376, [P, TT, W_MOBA])
    mla = at("mla", zone + 109568, [P, 7168])
    act_hi = at("act_hi", zone + 109568, [P, KD, T], F32R)
    act_lo = at("act_lo", zone + 57344, [P, KD, T], F32R)
    front = at("front", zone + 138240, [P, C_FRONT])
    work = at("work", zone + 144896, [P, 2560])
    uv = at("uv", zone + 0, [P, 2, 2, D], F32R)
    gs = at("gs", zone + 32768, [P, GJ, T])
    pw = at("pw", zone + 65536, [P, GJ, T])
    yacc = [at("yacc0", zone + 98304, [P, D]), at("yacc1", zone + 142336, [P, D])]
    wj = at("wj", zone + 106496, [P, 2, T])
    h2 = at("h2", zone + 109568, [P, 2, KD, T], F32R)
    am = at("am", zone + 150528, [P, 2, 2, T], F32R)
    zero = at("zero", zone + 155136, [P, P])
    hot_i = at("hot_i", 0, [P, 2, TB, NK], BF16)
    hot_j = at("hot_j", 4096, [P, 2, 3, TB, GJ], BF16)
    hot_e = at("hot_e", 7168, [P, 2, TB, GJ], BF16)
    w_part = at("w_part", 8192, [P, 3, T], BF16)
    w_rest = at("w_rest", 9728, [P, 3, T])
    rs = [at("rs0", zone + 142336, [P, D]), at("rs1", zone + 83456, [P, D])]
    cand = at("cand", zone + 75264, [P, D])
    rwork = at("rwork", zone + 65536, [P, 2320])

    ident, ones, iota = per[:, 0:P], per[:, P:2 * P], per[:, 2 * P:3 * P]
    col_a = small[:, 0:128]
    col_b = small[:, 128:202]
    g_pm, g_pf = col_a[:, 96:112], col_a[:, 112:128]
    col_c, g_om, g_of = col_b[:, 0:16], col_b[:, 16:32], col_b[:, 32:48]
    g_lat, g_att = col_b[:, 48:58], col_b[:, 58:74]
    mod = small[:, 208:304]
    cs = small[:, 304:320]
    sc1, sc2 = small[:, 320:336], small[:, 336:352]
    gg1, gg2 = small[:, 352:368], small[:, 368:384]
    tmpc = small[:, 384:400]
    st = small[:, 400:512]
    ssq = [st[:, 2 * n:2 * n + 2] for n in range(4)]
    rst = [st[:, 8 + 2 * n:10 + 2 * n] for n in range(4)]
    smax = st[:, 32:36].rearrange("p (b q) -> p b q", b=2)
    nmax = st[:, 36:40].rearrange("p (b q) -> p b q", b=2)
    esum = st[:, 40:44].rearrange("p (b q) -> p b q", b=2)
    erec = st[:, 44:48].rearrange("p (b q) -> p b q", b=2)

    cos, sin = front[:, F_COS:F_COS + T], front[:, F_SIN:F_SIN + T]
    rows = work[:, 0:256]
    sc = [work[:, 0:384], work[:, 384:768], front[:, F_RQ:F_RQ + 384]]
    pt = work[:, 768:1536].rearrange("p (b n) -> p b n", b=2)
    rb = work[:, 1536:2048].rearrange("p (g t) -> p g t", g=2)
    krope = work[:, 2048:2304]
    krt = work[:, 2304:2560]
    xn = mla[:, 0:2 * D].rearrange("p (t d) -> p t d", t=TT)
    qn = mla[:, 0:2048].rearrange("p (h t) -> p h t", h=MH)
    kn = mla[:, 2048:4096].rearrange("p (h t) -> p h t", h=MH)
    vv = mla[:, 4096:6144].rearrange("p (b n) -> p b n", b=TT)
    qr = mla[:, 6144:7168].rearrange("p (m t) -> p m t", m=MH // 2)
    sq_lat = mla[:, 0:2560].rearrange("p (k t) -> p k t", k=10)
    rt = mla[:, 4096:5120].rearrange("p (m t) -> p m t", m=MH // 2)
    subt = mv[:, :, :].rearrange("p a b -> p (a b)").rearrange("p (h n) -> p h n", h=16)
    subk = lat[:, 0:8, :].rearrange("p a b -> p (a b)").rearrange("p (h n) -> p h n", h=16)
    top_v = rwork[:, 0:256].rearrange("p (h k) -> p h k", h=16)
    top_i = rwork[:, 256:512].bitcast(U32).rearrange("p (h k) -> p h k", h=16)
    top_f = rwork[:, 512:768].rearrange("p (h k) -> p h k", h=16)
    pick_v = rwork[:, 768:896].rearrange("p (h k) -> p h k", h=PH)
    pick_s = rwork[:, 896:1024].bitcast(U32).rearrange("p (h k) -> p h k", h=PH)
    slot_u = rwork[:, 1024:1280].bitcast(U32).rearrange("p (s h k) -> p s h k", s=2, h=PH)
    slot_f = rwork[:, 1280:1536].rearrange("p (s h k) -> p s h k", s=2, h=PH)
    rout = rwork[:, 1536:2304].rearrange("p (t s n) -> p t s n", t=TT, s=3)
    rsum = rwork[:, 2304:2320]
    gg1_all = mla[:, 4096:4096 + D]
    diag = acc[:, 1, :]
    x1_tmp = mqk[:, :, :].rearrange("p (b a) t -> p b (a t)", b=TT)

    with ExitStack() as ctx:
        ps = ctx.enter_context(nc.psum_tensor("ps", [P, 8, 512], F32))

        def sem(name):
            return ctx.enter_context(nc.semaphore(name))

        ld_per, ld_front, ld_rows, ld_x, ld_sub = map(sem, ("ld_per", "ld_front", "ld_rows", "ld_x", "ld_sub"))
        w_full = [sem(f"w_full{n}") for n in range(WRING)]
        ada_full = [sem(f"ada_full{n}") for n in range(RING)]
        e_full = [sem(f"e_full{n}") for n in range(RING)]
        w_hi, w_split = sem("w_hi"), sem("w_split")
        act_split, h2_split, sq_head = sem("act_split"), sem("h2_split"), sem("sq_head")
        y_tmp, xn2b_ok = sem("y_tmp"), sem("xn2b_ok")
        w_used = sem("w_used")
        ada_used = sem("ada_used")
        rows_t, rows_ev = sem("rows_t"), sem("rows_ev")
        c_exp = sem("c_exp")
        x_ssq, x_rms, x_sqrt, x_rstd, xn_ok = map(sem, ("x_ssq", "x_rms", "x_sqrt", "x_rstd", "xn_ok"))
        xt_mm, xt_ev = sem("xt_mm"), sem("xt_ev")
        mod_mm, mod_ok = sem("mod_mm"), sem("mod_ok")
        in_ev = sem("in_ev")
        sq_ok, sq_mm, sq_aff, sq_root = map(sem, ("sq_ok", "sq_mm", "sq_aff", "sq_root"))
        lat_n, uq_ev, rot_mm, rope_ok, ukv_ev = map(sem, ("lat_n", "uq_ev", "rot_mm", "rope_ok", "ukv_ev"))
        s_mm, s_add, s_max, s_exp, s_norm, pt_mm, pt_ev, o_mm, o_ev = map(sem, (
            "s_mm", "s_add", "s_max", "s_exp", "s_norm", "pt_mm", "pt_ev", "o_mm", "o_ev"))
        o_norm, diag_ok, gg_mm, gg_ev, y_ssq, y_aff, y_root, x1_ok = map(sem, (
            "o_norm", "diag_ok", "gg_mm", "gg_ev", "y_ssq", "y_aff", "y_root", "x1_ok"))
        n_ssq, n_aff, n_root, n_rstd, xn2_ok, x2t_mm, x2t_ev = map(sem, (
            "n_ssq", "n_aff", "n_root", "n_rstd", "xn2_ok", "x2t_mm", "x2t_ev"))
        sub_mm, sub_ev, pq_ev, ks_mm, ks_ev = map(sem, ("sub_mm", "sub_ev", "pq_ev", "ks_mm", "ks_ev"))
        r_max, r_exp, r_ok, rt_mm, rt_ev = map(sem, ("r_max", "r_exp", "r_ok", "rt_mm", "rt_ev"))
        u_tr, u_hi, u_split, u_mm, u_gelu = map(sem, ("u_tr", "u_hi", "u_split", "u_mm", "u_gelu"))
        hot_ok, g_mm, g_ev = map(sem, ("hot_ok", "g_mm", "g_ev"))
        v_prod, v_hi, v_split, v_mm, y_ev = map(sem, ("v_prod", "v_hi", "v_split", "v_mm", "y_ev"))
        x1_st, x1_ld = map(sem, ("x1_st", "x1_ld"))
        f_ssq, f_aff, f_root, f_diag, f_gg, f_out, st_out = map(sem, (
            "f_ssq", "f_aff", "f_root", "f_diag", "f_gg", "f_out", "st_out"))
        hot_eq, zero_ok = map(sem, ("hot_eq", "zero_ok"))
        dve_chain, act_chain = sem("dve_chain"), sem("act_chain")
        gs_flat = gs[:, :, :].rearrange("p j t -> p (j t)")
        x1_dram = nc.dram_tensor("x1_dram", (P, TT, D), F32, kind="Internal").ap()

        def column(tile, j):
            return tile[:, bass.ds(j, 1), :].rearrange("p a t -> p (a t)")

        block = ctx.enter_context(nc.Block())

        win = w_in[0].rearrange("(k p) n -> p k n", p=P)
        wuq = w_uq[0].rearrange("(k p) n -> p k n", p=P)
        wukv = w_ukv[0].rearrange("(k p) n -> p k n", p=P)
        wout = w_out[0].rearrange("(k p) n -> p k n", p=P)
        wpq = w_peer_q[0].rearrange("(k p) n -> p k n", p=P)
        stream = []
        first = {}

        def plan(name, srcs):
            first[name] = len(stream)
            stream.extend(srcs)

        for name, c0 in (("mq", LAT), ("mk", LAT + W_MOBA), ("mv", LAT + 2 * W_MOBA)):
            plan(name, [win[:, k:k + 2, c0:c0 + W_MOBA] for k in range(0, KD, 2)])
        plan("lat", [win[:, k:k + 1, 0:LAT] for k in range(KD)])
        plan("uq", [wuq[:, k:k + 1, :] for k in range(KQ)])
        plan("ukv", [wukv[:, k:k + 1, :] for k in range(KKV)])
        plan("out", [wout[:, k:k + 1, :] for k in range(KD)])
        for cg in range(2):
            plan(f"pq{cg}", [wpq[:, k:k + 2, cg * 1024:cg * 1024 + 1024] for k in range(0, KD, 2)])

        names = list(first) + [None]
        end = {n: first[m] if m else len(stream) for n, m in zip(names, names[1:])}

        chunks = [m for m in range(len(stream)) if not first["uq"] <= m < end["ukv"]]
        nth = {m: i for i, m in enumerate(chunks)}

        def width(m):
            _, k, n = stream[m].shape
            return k * n

        def part(m, lo, off, n):
            return wlo[:, m % WRING, off:off + n] if lo else whi[nth[m] % 2][:, off:off + n]

        def w_loads(m):
            return sum(2 if first["uq"] <= n < end["uq"] else 1 for n in range(m % WRING, m + 1, WRING))

        def uq_nope(m):
            return wring[:, m % WRING, 0:MH * HD].rearrange("p (h c) -> p h c", c=HD)

        def uq_rope(m):
            return wring[:, m % WRING, MH * HD:MH * (HD + ROPE)].rearrange("p (h c) -> p h c", c=ROPE)

        def w_slot(m):
            _, k, n = stream[m].shape
            return wring[:, m % WRING, 0:k * n].rearrange("p (k n) -> p k n", k=k)

        def head_sq(h):
            return lat[:, h, :] if h < MH else mqk[:, h - MH, :]

        uv_dram = [e[0].rearrange("(i j) d -> i j d", j=NK) for e in (u_experts, v_experts)]

        @block.sync
        def _(sp):
            sp.dma_start(per[:, :], const_per).then_inc(ld_per, 16)
            r0 = 0
            for v, n in ((b_ada, 96), (g_pre_mix, 16), (g_pre_ffn, 16)):
                sp.dma_start(rows[r0:r0 + n, 0:P], v.rearrange("a (k p) -> (a k) p", p=P)).then_inc(ld_rows, 16)
                r0 += n
            r0 = 0
            for v, n in ((c, 16), (g_post_mix, 16), (g_post_ffn, 16), (g_q_lat, KQ), (g_kv_lat, KKV),
                         (g_out_mla, MH), (g_out_moba, MH)):
                sp.dma_start(rows[r0:r0 + n, P:2 * P], v.rearrange("a (k p) -> (a k) p", p=P)).then_inc(ld_rows, 16)
                r0 += n
            sp.dma_start(xs[:, :, :], x[0].rearrange("(t p) d -> p t d", p=P)).then_inc(ld_x, 16)
            sp.wait_ge(ada_used, 28)
            for m, src in enumerate(stream):
                if m >= WRING:
                    sp.wait_ge(w_used, m - WRING + 1)
                if m == end["lat"] + WRING - 1:
                    sp.wait_ge(w_used, end["lat"])
                    sp.dma_start(front[:, :], const_front).then_inc(ld_front, 16)
                if m == end["ukv"] + WRING:
                    sp.wait_ge(sq_mm, 2)
                    for s, key in enumerate((sub_keys_1, sub_keys_2)):
                        sp.dma_start(subk.rearrange("p (h s) d -> p s h d", s=2)[:, s],
                                     key[0].rearrange("h n d -> n h d")).then_inc(ld_sub, 16)
                if first["uq"] <= m < end["uq"]:
                    hc = src.rearrange("p k (h c) -> p (k h) c", c=HD + ROPE)
                    sp.dma_start(uq_nope(m), hc[:, :, 0:HD]).then_inc(w_full[m % WRING], 16)
                    sp.dma_start(uq_rope(m), hc[:, :, HD:HD + ROPE]).then_inc(w_full[m % WRING], 16)
                else:
                    sp.dma_start(w_slot(m), src).then_inc(w_full[m % WRING], 16)

            sp.wait_ge(ada_used, 96)
            sp.wait_ge(x1_ok, TT)
            sp.dma_start(x1_dram, xs[:, :, :]).then_inc(x1_st, 16)
            for g in range(GROUPS):
                for phase in range(2):
                    src = uv_dram[phase]
                    j0 = g * GJ
                    taken = (u_tr, v_split)
                    step = (2, 1)
                    for q in range(RING):
                        if phase == 1:
                            sp.wait_ge(u_tr, 2 * ((g + 1) * GJ - RING + q + 1))
                        elif g:
                            sp.wait_ge(v_split, g * GJ - RING + q + 1)
                        sp.dma_start(ring[:, q, :], src[:, j0 + q, :]).then_inc(e_full[q], 16)
                    with sp.Fori(1, GJ // RING) as it:
                        for q in range(RING):
                            sp.wait_ge(taken[phase], (it * RING + (g * GJ - RING + q + 1)) * step[phase])
                            sp.dma_start(ring[:, q, :], src[:, bass.ds(it * RING + (j0 + q), 1), :]
                                         .rearrange("p a d -> p (a d)")).then_inc(e_full[q], 16)
                    if g == GROUPS - 1 and phase:
                        sp.wait_ge(x1_st, 16)
                        sp.wait_ge(g_mm, GROUPS * (T // TB))
                        sp.dma_start(xs[:, :, :], x1_dram).then_inc(x1_ld, 16)
            sp.wait_ge(f_out, TT)
            sp.dma_start(out[0].rearrange("(t p) d -> p t d", p=P), xs[:, :, :]).then_inc(st_out, 16)
            sp.wait_ge(st_out, 16)

        @block.gpsimd
        def _(pool):
            for s in range(6):
                lo = 0
                if s == 0:
                    for q in range(RING):
                        pool.dma_start(ring[:, q, :], w_ada[0, q * P:(q + 1) * P, 0:D]).then_inc(ada_full[q], 16)
                    lo = 1
                if s == 4:
                    with pool.Fori(0, 2) as it:
                        for q in range(RING):
                            pool.wait_ge(ada_used, it * RING + (s * KD + q - RING + 1))
                            pool.dma_start(ring[:, q, :], w_ada[0, bass.ds((it * RING + q) * P, P), s * D:(s + 1) * D]
                                           ).then_inc(ada_full[q], 16)
                    for k in range(8, 12):
                        if k == ADA_EARLY - s * KD + RING:
                            pool.wait_ge(ukv_ev, 4)
                            for h in range(2 * MH):
                                pool.wait_ge(o_ev, h + 1)
                                nc.gpsimd.tensor_tensor(head_sq(h), act_t[:, h, :], act_t[:, h, :], ALU.mult
                                                        ).then_inc(sq_head, 1)
                        pool.wait_ge(ada_used, s * KD + k - RING + 1)
                        pool.dma_start(ring[:, k % RING, :], w_ada[0, k * P:(k + 1) * P, s * D:(s + 1) * D]
                                       ).then_inc(ada_full[k % RING], 16)
                    lo = 3
                with pool.Fori(lo, KD // RING) as it:
                    for q in range(RING):
                        pool.wait_ge(ada_used, it * RING + (s * KD + q - RING + 1))
                        pool.dma_start(ring[:, q, :], w_ada[0, bass.ds((it * RING + q) * P, P), s * D:(s + 1) * D]
                                       ).then_inc(ada_full[q], 16)

        @block.tensor
        def _(pe):
            mm = nc.tensor.matmul

            def w_wait(m):
                pe.wait_ge(w_full[m % WRING], 16 * w_loads(m))

            def half(bank, n):
                return ps[:, bank + n // 2, (n % 2) * T:(n % 2 + 1) * T]

            pe.wait_ge(ld_per, 16)
            pe.wait_ge(ld_rows, 160)
            nc.tensor.transpose(ps[:, 7, 0:P], rows[:, 0:P], ident)
            nc.tensor.transpose(ps[:, 6, 0:74], rows[0:74, P:2 * P], ident[0:74, 0:74]).then_inc(rows_t, 1)

            def x_tiles(k, src, bank, done):
                for kk in (k, k + 1):
                    for t in range(TT):
                        last = nc.tensor.transpose(ps[:, bank, (kk % 2) * T + t * P:(kk % 2) * T + t * P + P],
                                                   src[:, t, kk * P:(kk + 1) * P], ident)
                last.then_inc(done, 1)

            def mod_sum(s, bank=7):
                pe.wait_ge(ada_used, 16 * (s + 1))
                for k in range(KD):
                    last = mm(ps[:, bank, P + 16 * s + k:P + 16 * s + k + 1], acc[:, s % 2, k * P:(k + 1) * P],
                              ones[:, 0:1], start=True, stop=True)
                last.then_inc(mod_mm, 1)

            pe.wait_ge(rows_ev, 1)
            pe.wait_ge(xn_ok, TT)
            for k in range(0, 14, 2):
                x_tiles(k, xn, k // 2, xt_mm)
            mod_sum(0)
            mod_sum(1)
            pe.wait_ge(xt_ev, 2)
            x_tiles(14, xn, 0, xt_mm)
            pe.wait_ge(xt_ev, KD)

            def weight_left(m, off, w, dst, rhs, k, start):
                hi, lo = part(m, 0, off, w), part(m, 1, off, w)
                mm(dst, hi, rhs[0][:, k, :], start=start, stop=False, skip_group_check=True)
                mm(dst, hi, rhs[1][:, k, :], start=False, stop=False, skip_group_check=True)
                return mm(dst, lo, rhs[0][:, k, :], start=False, stop=k == KD - 1, skip_group_check=True)

            def weight_right(m, off, banks, k):
                for t in range(TT):
                    for a, lo in ((act_hi, 0), (act_hi, 1), (act_lo, 0)):
                        for n in range(banks):
                            last = mm(ps[:, banks * t + n, :], a[:, k, t * P:(t + 1) * P],
                                      part(m, lo, off + n * 512, 512), start=k == 0 and a is act_hi and lo == 0,
                                      stop=k == KD - 1 and a is act_lo)
                return last

            h_parts = (act_hi, act_lo)
            for n, name in enumerate(("mq", "mk")):
                for k in range(KD):
                    m = first[name] + k // 2
                    if k % 2 == 0:
                        pe.wait_ge(w_split, nth[m] + 1)
                        if n == 0:
                            pe.wait_ge(act_split, k // 2 + 1)
                    for h in range(MH):
                        last = weight_left(m, (k % 2) * W_MOBA + h * P, P, half(4 * n, h), h_parts, k,
                                           k == 0 and h % 2 == 0)
                    if k % 2:
                        last.then_inc(w_used, 1)
            pe.wait_ge(in_ev, 4)
            for k in range(KD):
                m = first["mv"] + k // 2
                if k % 2 == 0:
                    pe.wait_ge(w_split, nth[m] + 1)
                last = weight_right(m, (k % 2) * W_MOBA, 2, k)
                if k % 2:
                    last.then_inc(w_used, 1)
            pe.wait_ge(in_ev, 8)
            for k in range(KD):
                m = first["lat"] + k
                pe.wait_ge(w_split, nth[m] + 1)
                for n in range(11):
                    if k == 0 and n == 6:
                        pe.wait_ge(in_ev, 11)
                    w = P if n < 10 else ROPE
                    last = weight_left(m, n * P, w, ps[0:w, LAT_BANKS[n // 2], (n % 2) * T:(n % 2 + 1) * T], h_parts, k,
                                       k == 0 and n % 2 == 0)
                last.then_inc(w_used, 1)
            mod_sum(2)
            pe.wait_ge(in_ev, 12)
            pe.wait_ge(sq_ok, 1)
            for g, (a, b) in enumerate(((0, KQ), (KQ, KQ + KKV))):
                for k in range(a, b):
                    last = mm(ps[:, 3, g * T:(g + 1) * T], ones, sq_lat[:, k, :], start=k == a, stop=k == b - 1)
            last.then_inc(sq_mm, 1)
            pe.wait_ge(in_ev, 18)
            pe.wait_ge(lat_n, KQ)
            for k in range(KQ):
                m = first["uq"] + k
                w_wait(m)
                for h in range(MH):
                    mm(half(0, h), uq_nope(m)[:, h, :], lat[:, k, :],
                       start=k == 0 and h % 2 == 0, stop=k == KQ - 1, skip_group_check=True)
                for j in range(MH // 2):
                    last = mm(half(4, j), uq_rope(m)[:, 2 * j:2 * j + 2, :].rearrange("p h c -> p (h c)"),
                              lat[:, k, :], start=k == 0 and j % 2 == 0, stop=k == KQ - 1, skip_group_check=True)
                last.then_inc(w_used, 1)
            pe.wait_ge(ld_front, 16)
            pe.wait_ge(uq_ev, 3)
            for j in range(MH // 2):
                mm(half(4, j), front[:, F_RQ:F_RQ + P], qr[:, j, :], start=True, stop=True)
            mm(ps[:, 6, 0:T], front[0:ROPE, F_DK:F_DK + P], lat[0:ROPE, 10, :], start=True, stop=True)
            mm(ps[:, 6, T:2 * T], front[0:ROPE, F_RK:F_RK + P], lat[0:ROPE, 10, :], start=True, stop=True
               ).then_inc(rot_mm, 1)
            pe.wait_ge(rope_ok, 1)
            pe.wait_ge(mod_ok, 3)
            for k in range(KKV):
                m = first["ukv"] + k
                w_wait(m)
                for h in range(MH):
                    mm(half(0, h), w_slot(m)[:, 0, h * 256:h * 256 + P], lat[:, KQ + k, :],
                       start=k == 0 and h % 2 == 0, stop=k == KKV - 1, skip_group_check=True)
                wv = w_slot(m)[:, 0, :].rearrange("p (h c) -> p h c", c=256)
                for t in range(TT):
                    for n in range(2):
                        last = mm(ps[:, 4 + 2 * t + n, :], lat[:, KQ + k, t * P:(t + 1) * P],
                                  wv[:, 4 * n:4 * n + 4, P:256], start=k == 0, stop=k == KKV - 1)
                last.then_inc(w_used, 1)

            def scores(h):
                if h == 0:
                    pe.wait_ge(ukv_ev, 4)
                if h >= 3:
                    pe.wait_ge(s_add, h - 2)
                for o, q0, kn_ in ((0, 0, P), (P, P, T)):
                    dst = ps[:, h % 3, o:o + kn_]
                    if h < MH:
                        b = ROPE * (h % 2)
                        mm(dst, qn[:, h, q0:q0 + P], kn[:, h, 0:kn_], start=True, stop=False)
                        last = mm(dst, qr[b:b + ROPE, h // 2, q0:q0 + P], krope[b:b + ROPE, 0:kn_], start=False, stop=True)
                    else:
                        last = mm(dst, mqk[:, h - MH, q0:q0 + P], mqk[:, h, 0:kn_], start=True, stop=True)
                last.then_inc(s_mm, 1)

            def weights_t(h):
                pe.wait_ge(s_norm, h + 1)
                if h >= 2:
                    pe.wait_ge(pt_ev, h - 1)
                for n in range(3):
                    last = nc.tensor.transpose(ps[:, 3 + h % 2, n * P:(n + 1) * P], sc[h % 3][:, n * P:(n + 1) * P], ident)
                last.then_inc(pt_mm, 1)

            def mix(h):
                pe.wait_ge(pt_ev, h + 1)
                if h >= 2:
                    pe.wait_ge(o_ev, h - 1)
                v = vv[:, :, h * P:(h + 1) * P] if h < MH else mv[:, :, (h - MH) * P:(h - MH + 1) * P]
                mm(ps[:, 5 + h % 2, 0:T], v[:, 0, :], pt[:, h % 2, 0:T], start=True, stop=False, skip_group_check=True)
                mm(ps[:, 5 + h % 2, P:T], v[:, 1, :], pt[:, h % 2, T:3 * P], start=False, stop=True,
                   skip_group_check=True).then_inc(o_mm, 1)

            def head_squares(h):
                g, k = h // MH, h % MH
                pe.wait_ge(sq_head, h + 1)
                last = mm(ps[:, 7, g * T:(g + 1) * T], ones, head_sq(h), start=k == 0, stop=k == MH - 1)
                if h == 2 * MH - 1:
                    last.then_inc(sq_mm, 1)

            scores(0)
            scores(1)
            for h in range(2 * MH):
                if h + 2 < 2 * MH:
                    scores(h + 2)
                weights_t(h)
                if h:
                    mix(h - 1)
                if h == 1:
                    mod_sum(3)
                if h == 4:
                    pe.wait_ge(mod_ok, 4)
                if h >= 4:
                    head_squares(h - 4)
            mix(2 * MH - 1)
            pe.wait_ge(diag_ok, 1)
            pe.wait_ge(s_add, 16)
            pe.wait_ge(pt_ev, 16)
            for k in range(KD):
                last = mm(ps[:, k // 4, (k % 4) * P:(k % 4 + 1) * P], ones, diag[:, k * P:(k + 1) * P],
                          start=True, stop=True)
            last.then_inc(gg_mm, 1)
            for h in range(2 * MH - 4, 2 * MH):
                head_squares(h)
            pe.wait_ge(gg_ev, 1)
            pe.wait_ge(o_ev, 16)
            pe.wait_ge(sq_aff, 2)
            for k in range(KD):
                m = first["out"] + k
                pe.wait_ge(w_split, nth[m] + 1)
                pe.wait_ge(act_split, KD // 2 + k + 1)
                weight_right(m, 0, 4, k).then_inc(w_used, 1)
            pe.wait_ge(ld_sub, 32)
            pe.wait_ge(y_ssq, TT)
            pe.wait_ge(y_tmp, TT)
            for h in range(16):
                last = nc.tensor.transpose(ps[:, 4 + h // 4, (h % 4) * P:(h % 4 + 1) * P], subk[:, h, :], ident)
            last.then_inc(sub_mm, 1)
            mod_sum(4, 0)
            pe.wait_ge(mod_ok, 5)
            pe.wait_ge(xn2_ok, 1)
            pe.wait_ge(xn2b_ok, 1)
            for k in range(0, 8, 2):
                x_tiles(k, xn, k // 2, x2t_mm)
            pe.wait_ge(sub_ev, 1)
            for k in range(8, KD, 2):
                x_tiles(k, xn, k // 2, x2t_mm)
            h2_parts = (h2[:, 0, :, :], h2[:, 1, :, :])
            for cg in range(2):
                pe.wait_ge(x2t_ev, 8 * (cg + 1))
                for k in range(KD):
                    m = first[f"pq{cg}"] + k // 2
                    if k % 2 == 0:
                        pe.wait_ge(w_split, nth[m] + 1)
                        if cg == 0:
                            pe.wait_ge(h2_split, k // 2 + 1)
                    for h in range(8):
                        last = weight_left(m, (k % 2) * 1024 + h * P, P, half(4 * cg, h), h2_parts, k,
                                           k == 0 and h % 2 == 0)
                    if k % 2:
                        last.then_inc(w_used, 1)
            pe.wait_ge(pq_ev, 4)
            mod_sum(5, 0)
            pe.wait_ge(mod_ok, 7)
            for t in range(TT):
                pe.wait_ge(pq_ev, 8)
                for h in range(16):
                    last = mm(ps[:, 4 * t + h // 4, (h % 4) * P:(h % 4 + 1) * P], mqk[:, h, t * P:(t + 1) * P],
                              subt[:, h, :], start=True, stop=True)
                last.then_inc(ks_mm, 1)
            pe.wait_ge(ks_ev, TT)

            pe.wait_ge(zero_ok, 1)

            def u_transpose(q, full, split):
                pe.wait_ge(e_full[q], full)
                for hf in range(2):
                    if split is not None:
                        pe.wait_ge(u_split, split + hf)
                    for k in range(8):
                        last = nc.tensor.transpose(ps[:, 2 * hf + k // 4, (k % 4) * P:(k % 4 + 1) * P],
                                                   ring[:, q, (8 * hf + k) * P:(8 * hf + k + 1) * P], ident)
                    last.then_inc(u_tr, 1)

            def u_scores(b, split, gelu):
                pe.wait_ge(u_split, split)
                if gelu is not None:
                    pe.wait_ge(u_gelu, gelu)
                dst = ps[:, 4 + b, 0:T]
                for k in range(KD):
                    hi, lo = uv[:, b, 0, k * P:(k + 1) * P], uv[:, b, 1, k * P:(k + 1) * P]
                    mm(dst, hi, h2[:, 0, k, :], start=k == 0, stop=False)
                    mm(dst, hi, h2[:, 1, k, :], start=False, stop=False)
                    last = mm(dst, lo, h2[:, 0, k, :], start=False, stop=k == KD - 1)
                last.then_inc(u_mm, 1)

            def place(b, ok, ev):
                pe.wait_ge(hot_ok, ok)
                if ev is not None:
                    pe.wait_ge(g_ev, ev)
                for t in range(TB):
                    for part in range(3):
                        last = mm(ps[:, 6 + b, t * GJ:(t + 1) * GJ], hot_i[:, b, t, :], hot_j[:, b, part, t, :],
                                  start=part == 0, stop=part == 2)
                last.then_inc(g_mm, 1)

            def v_mix(b, ok):
                pe.wait_ge(v_split, ok)
                for t in range(TT):
                    hi, lo = am[:, b, 0, t * P:(t + 1) * P], am[:, b, 1, t * P:(t + 1) * P]
                    for a, part in ((hi, 0), (hi, 1), (lo, 0)):
                        for n in range(4):
                            last = mm(ps[:, 4 * t + n, :], a, uv[:, b, part, n * 512:(n + 1) * 512],
                                      start=False, stop=False, skip_group_check=True)
                last.then_inc(v_mm, 1)

            for g in range(GROUPS):
                n0 = g * GJ
                f0 = 16 * (2 * n0 // RING)
                if g:
                    pe.wait_ge(y_ev, 8 * g)
                def u_step(q, it):
                    u_transpose(q, it * 16 + (f0 + 16), it * (2 * RING) + (2 * (n0 + q - 1) + 1))
                    u_scores((q - 1) % 2, it * (2 * RING) + 2 * (n0 + q), it * RING + (n0 + q - 2))

                for n in range(RING):
                    u_transpose(n % RING, f0 + 16, 2 * (n0 + n - 1) + 1 if n0 + n > 0 else None)
                    if n:
                        u_scores((n - 1) % 2, 2 * (n0 + n), n0 + n - 2 if n0 + n > 2 else None)
                        if g:
                            place((n - 1) % 2, n0 + n, n0 + n - 2)
                if g == 0:
                    with pe.Fori(1, ROUTE_STEPS // RING) as it:
                        for q in range(RING):
                            u_step(q, it)
                    for t in range(TT):
                        pe.wait_ge(r_ok, t + 1)
                        for s in range(3):
                            last = nc.tensor.transpose(ps[:, 6 + s // 2, (s % 2) * T + t * P:(s % 2) * T + (t + 1) * P],
                                                       rout[:, t, s, :], ident)
                    last.then_inc(rt_mm, 1)
                    for it in range(ROUTE_STEPS // RING, GJ // RING):
                        for q in range(RING):
                            u_step(q, it)
                            m = 2 * (it * RING + q - ROUTE_STEPS)
                            if m == 0:
                                pe.wait_ge(rt_ev, 1)
                            for b in range(2):
                                place(b, m + b + 1, m + b - 1 if m else None)
                    u_scores(1, 2 * GJ, GJ - 2)
                    for m in range(2 * (GJ - ROUTE_STEPS), T // TB):
                        place(m % 2, m + 1, m - 1)
                else:
                    with pe.Fori(1, GJ // RING) as it:
                        for q in range(RING):
                            u_step(q, it)
                            place((q - 1) % 2, it * RING + (n0 + q), it * RING + (n0 + q - 2))
                    place(1, n0 + GJ, n0 + GJ - 2)
                    u_scores(1, 2 * (n0 + GJ), n0 + GJ - 2)

                pe.wait_ge(g_ev, n0 + GJ)
                pe.wait_ge(u_gelu, n0 + GJ)
                for bank in range(8):
                    mm(ps[:, bank, 0:P], zero[:, :], zero[:, :], start=True, stop=False, skip_group_check=True)
                with pe.Fori(0, GJ // RING) as it:
                    for q in range(RING):
                        v_mix(q % 2, it * RING + (n0 + q + 1))
            pe.wait_ge(y_ev, 8 * GROUPS)
            pe.wait_ge(f_diag, 1)
            for k in range(KD):
                last = mm(ps[:, k // 4, (k % 4) * P:(k % 4 + 1) * P], ones, gs_flat[:, k * P:(k + 1) * P],
                          start=True, stop=True)
            last.then_inc(f_gg, 1)

        @block.scalar
        def _(act):
            fn = nc.scalar.activation
            chain = [0]

            def link(ins):
                chain[0] += 1
                ins.then_inc(act_chain, 1)
                act.wait_ge(act_chain, chain[0])

            act.wait_ge(rows_ev, 1)
            fn(cs, col_c, ACT.Exp, scale=-1.0).then_inc(c_exp, 1)
            act.wait_ge(ld_x, 16)
            for t in range(TT):
                fn(xn[:, t, :], xs[:, t, :], ACT.Square, accum_out=ssq[0][:, t:t + 1]).then_inc(x_ssq, 1)
            act.wait_ge(x_rms, 1)
            fn(rst[0], ssq[0], ACT.Sqrt).then_inc(x_sqrt, 1)
            act.wait_ge(x_rstd, 1)
            for t in range(TT):
                fn(xn[:, t, :], xs[:, t, :], ACT.Copy, scale=rst[0][:, t:t + 1]).then_inc(xn_ok, 1)
            def w_high(m):
                act.wait_ge(w_full[m % WRING], 16 * w_loads(m))
                if nth[m] >= 2:
                    act.wait_ge(w_used, chunks[nth[m] - 2] + 1)
                n = width(m)
                fn(whi[nth[m] % 2][:, 0:n], wring[:, m % WRING, 0:n], ACT.Copy).then_inc(w_hi, 1)

            w_high(0)
            w_high(1)
            act.wait_ge(mod_ok, 2)
            for k in range(KD):
                if k % 2 == 0:
                    act.wait_ge(xt_mm, k // 2 + 1)
                bank = k // 2 if k < 14 else 0
                fn(act_t[:, k, :], ps[:, bank, (k % 2) * T:(k % 2 + 1) * T], ACT.Identity,
                   bias=mod[:, k:k + 1], scale=sc1[:, k:k + 1]).then_inc(xt_ev, 1)
            for m in range(2, end["lat"]):
                w_high(m)
                if m == end["mq"] + 1:
                    act.wait_ge(w_used, end["mq"])
                    for b in range(4):
                        fn(mqk[:, 2 * b:2 * b + 2, :].rearrange("p a t -> p (a t)"), ps[:, b, :],
                           ACT.Copy, scale=HD ** -0.5).then_inc(in_ev, 1)
                if m == end["mk"] + 1:
                    act.wait_ge(w_used, end["mk"])
                    for b in range(4):
                        fn(mqk[:, MH + 2 * b:MH + 2 * b + 2, :].rearrange("p a t -> p (a t)"), ps[:, 4 + b, :],
                           ACT.Copy).then_inc(in_ev, 1)
                if m == end["mv"]:
                    act.wait_ge(w_used, end["mv"])
                    for b in range(4):
                        fn(mv[:, b // 2, (b % 2) * 512:(b % 2 + 1) * 512], ps[:, b, :], ACT.Copy).then_inc(in_ev, 1)
            act.wait_ge(w_used, end["lat"])
            for b in range(5):
                fn(lat[:, 2 * b:2 * b + 2, :].rearrange("p a t -> p (a t)"), ps[:, LAT_BANKS[b], :], ACT.Copy
                   ).then_inc(in_ev, 1)
            fn(lat[0:ROPE, 10, :], ps[0:ROPE, LAT_BANKS[5], 0:T], ACT.Copy).then_inc(in_ev, 1)
            act.wait_ge(in_ev, 18)
            fn(sq_lat, lat[:, 0:10, :], ACT.Square).then_inc(sq_ok, 1)
            act.wait_ge(sq_aff, 1)
            fn(rb, rb, ACT.Sqrt).then_inc(sq_root, 1)
            act.wait_ge(w_used, end["uq"])
            act.wait_ge(lat_n, 10)
            s_qk = (HD + ROPE) ** -0.5
            fn(qr, ps[:, 4:6, :].rearrange("p a (b t) -> p (a b) t", b=2), ACT.Copy, scale=s_qk).then_inc(uq_ev, 1)
            for b in range(2):
                fn(qn[:, 4 * b:4 * b + 4, :].rearrange("p a t -> p (a t)"),
                   ps[:, 2 * b:2 * b + 2, :].rearrange("p a t -> p (a t)"), ACT.Copy, scale=s_qk).then_inc(uq_ev, 1)
            act.wait_ge(w_used, end["ukv"])
            act.wait_ge(rope_ok, 1)
            for b in range(2):
                fn(kn[:, 4 * b:4 * b + 4, :].rearrange("p a t -> p (a t)"),
                   ps[:, 2 * b:2 * b + 2, :].rearrange("p a t -> p (a t)"), ACT.Copy).then_inc(ukv_ev, 1)
            for t in range(TT):
                fn(vv[:, t, :], ps[:, 4 + 2 * t:6 + 2 * t, :].rearrange("p a t -> p (a t)"), ACT.Copy).then_inc(ukv_ev, 1)

            w_high(first["out"])
            def exp(h):
                act.wait_ge(s_max, h + 1)
                b = h % 2
                s = sc[h % 3]
                fn(s[:, 0:P], s[:, 0:P], ACT.Exp, bias=nmax[:, b, 0:1], accum_out=esum[:, b, 0:1])
                fn(s[:, P:3 * P], s[:, P:3 * P], ACT.Exp, bias=nmax[:, b, 1:2],
                   accum_out=esum[:, b, 1:2]).then_inc(s_exp, 1)

            def weights_out(h):
                act.wait_ge(pt_mm, h + 1)
                if h >= 2:
                    act.wait_ge(o_mm, h - 1)
                fn(pt[:, h % 2, :], ps[:, 3 + h % 2, 0:3 * P], ACT.Copy).then_inc(pt_ev, 1)

            def mixed_out(h):
                act.wait_ge(o_mm, h + 1)
                fn(act_t[:, h, :], ps[:, 5 + h % 2, 0:T], ACT.Copy).then_inc(o_ev, 1)

            for h in range(2 * MH):
                exp(h)
                if h >= 1:
                    weights_out(h - 1)
                if h >= 2:
                    mixed_out(h - 2)
            weights_out(15)
            mixed_out(14)
            mixed_out(15)
            act.wait_ge(gg_mm, 1)
            fn(gg1_all, ps[:, 0:4, :].rearrange("p a n -> p (a n)"), ACT.Copy).then_inc(gg_ev, 1)
            act.wait_ge(sq_aff, 2)
            fn(rb, rb, ACT.Sqrt).then_inc(sq_root, 1)
            act.wait_ge(pt_mm, 16)
            for m in range(first["out"] + 1, first["pq0"] + 1):
                w_high(m)
            act.wait_ge(w_used, end["out"])
            for t in range(TT):
                if t == 1:
                    act.wait_ge(y_tmp, 1)
                fn(xn[:, t, :], ps[:, 4 * t:4 * t + 4, :].rearrange("p a n -> p (a n)"), ACT.Square,
                   accum_out=ssq[1][:, t:t + 1]).then_inc(y_ssq, 1)
            act.wait_ge(y_aff, 1)
            fn(rst[1], ssq[1], ACT.Sqrt).then_inc(y_root, 1)
            w_high(first["pq0"] + 1)
            for t in range(TT):
                act.wait_ge(x1_ok, t + 1)
                fn(xn[:, t, :], xs[:, t, :], ACT.Square, accum_out=ssq[2][:, t:t + 1]).then_inc(n_ssq, 1)
            act.wait_ge(n_aff, 1)
            fn(rst[2], ssq[2], ACT.Sqrt).then_inc(n_root, 1)
            act.wait_ge(n_rstd, 1)
            fn(xn[:, 0, :], xs[:, 0, :], ACT.Copy, scale=rst[2][:, 0:1]).then_inc(xn2_ok, 1)
            act.wait_ge(mod_ok, 6)
            for k in range(KD):
                if k % 2 == 0:
                    act.wait_ge(x2t_mm, k // 2 + 1)
                fn(act_t[:, k, :], ps[:, k // 2, (k % 2) * T:(k % 2 + 1) * T], ACT.Identity,
                   bias=mod[:, 48 + k:49 + k], scale=sc2[:, k:k + 1]).then_inc(x2t_ev, 1)
            for cg in range(2):
                for m in range(first["pq0"] + 2, end["pq0"] + 2) if cg == 0 else range(end["pq0"] + 2, end["pq1"]):
                    w_high(m)
                act.wait_ge(w_used, end[f"pq{cg}"])
                for b in range(4):
                    n = 8 * cg + 2 * b
                    fn(mqk[:, n:n + 2, :].rearrange("p a t -> p (a t)"), ps[:, 4 * cg + b, :], ACT.Copy).then_inc(pq_ev, 1)
            for t in range(TT):
                act.wait_ge(ks_mm, t + 1)
                fn(rs[t][:, :], ps[:, 4 * t:4 * t + 4, :].rearrange("p a n -> p (a n)"), ACT.Copy).then_inc(ks_ev, 1)
            act.wait_ge(x1_st, 16)

            def u_high(q, tr, free):
                for hf in range(2):
                    act.wait_ge(u_tr, tr + hf)
                    if free is not None and hf == 0:
                        act.wait_ge(u_mm, free)
                    fn(uv[:, q % 2, 0, hf * 1024:(hf + 1) * 1024],
                       ps[:, 2 * hf:2 * hf + 2, :].rearrange("p a n -> p (a n)"), ACT.Copy).then_inc(u_hi, 1)

            def gelu(b, done, j):
                act.wait_ge(u_mm, done)
                fn(column(gs, j), ps[:, 4 + b, 0:T], ACT.Gelu).then_inc(u_gelu, 1)

            def placed(b, done, t0):
                act.wait_ge(g_mm, done)
                fn(pw[:, :, t0].rearrange("p j t -> p t j"),
                   ps[:, 6 + b, 0:TB * GJ].rearrange("p (t j) -> p t j", t=TB), ACT.Copy).then_inc(g_ev, 1)

            def v_high(q, full, prod, free):
                act.wait_ge(e_full[q], full)
                act.wait_ge(v_prod, prod)
                if free is not None:
                    act.wait_ge(v_mm, free)
                fn(am[:, q % 2, 0, :], wj[:, q % 2, :], ACT.Copy)
                fn(uv[:, q % 2, 0, :], ring[:, q, :], ACT.Copy).then_inc(v_hi, 1)

            for g in range(GROUPS):
                n0 = g * GJ
                if g:
                    act.wait_ge(v_mm, n0)
                    act.wait_ge(v_prod, n0)
                def step(q, it):
                    u_high(q, it * (2 * RING) + (2 * (n0 + q) + 1), it * RING + (n0 + q - 1))
                    gelu((q - 1) % 2, it * RING + (n0 + q), it * RING + (q - 1))

                for n in range(RING):
                    u_high(n, 2 * (n0 + n) + 1, n0 + n - 1 if n0 + n > 1 else None)
                    if n:
                        gelu((n - 1) % 2, n0 + n, n - 1)
                        if g:
                            placed((n - 1) % 2, n0 + n, bass.ds((n - 1) * TB, TB))
                if g == 0:
                    for n in range(RING, ROUTE_STEPS):
                        step(n % RING, n // RING)
                        for t in range(TT):
                            if n == (6, 14)[t]:
                                act.wait_ge(r_max, t + 1)
                                fn(pick_v, pick_v, ACT.Exp).then_inc(r_exp, 1)
                    for n in range(ROUTE_STEPS, GJ):
                        step(n % RING, n // RING)
                        m = 2 * (n - ROUTE_STEPS)
                        if m == 0:
                            act.wait_ge(rt_mm, 1)
                            fn(ridx[:, :, :], ps[:, 6, :].rearrange("p (s t) -> p s t", s=2), ACT.Copy)
                            fn(w_rest[:, 0, :], ps[:, 7, 0:T], ACT.Copy).then_inc(rt_ev, 1)
                        else:
                            for b in range(2):
                                placed(b, m + b - 1, bass.ds((m + b - 2) * TB, TB))
                    gelu(1, GJ, GJ - 1)
                    for m in range(2 * (GJ - 1 - ROUTE_STEPS), T // TB):
                        placed(m % 2, m + 1, bass.ds(m * TB, TB))
                else:
                    with act.Fori(1, GJ // RING) as it:
                        for q in range(RING):
                            step(q, it)
                            placed((q - 1) % 2, it * RING + (n0 + q), bass.ds(it * (RING * TB) + (q - 1) * TB, TB))
                    placed(1, n0 + GJ, bass.ds((GJ - 1) * TB, TB))
                    gelu(1, n0 + GJ, GJ - 1)

                f0 = 16 * ((2 * n0 + GJ) // RING)
                for q in range(RING):
                    v_high(q, f0 + 16, n0 + q + 1, n0 + q - 1 if n0 + q > 1 else None)
                with act.Fori(1, GJ // RING) as it:
                    for q in range(RING):
                        v_high(q, it * 16 + (f0 + 16), it * RING + (n0 + q + 1), it * RING + (n0 + q - 1))
            act.wait_ge(y_ev, 8 * GROUPS)
            for t in range(TT):
                fn(gs_flat[:, (t + 1) * D:(t + 2) * D], yacc[t][:, :], ACT.Square, accum_out=ssq[3][:, t:t + 1]).then_inc(f_ssq, 1)
            act.wait_ge(f_aff, 1)
            fn(rst[3], ssq[3], ACT.Sqrt).then_inc(f_root, 1)

        @block.vector
        def _(dve):
            tt, ts, stt = nc.vector.tensor_tensor, nc.vector.tensor_scalar, nc.vector.scalar_tensor_tensor
            chain = [0]

            def link(ins):
                chain[0] += 1
                ins.then_inc(dve_chain, 1)
                dve.wait_ge(dve_chain, chain[0])

            def rms(src, n):
                return ts(src, src, 1.0 / n, EPS, ALU.mult, ALU.add)

            nc.vector.memset(zero[:, :], 0.0).then_inc(zero_ok, 1)
            dve.wait_ge(rows_t, 1)
            nc.vector.tensor_copy(col_a, ps[:, 7, 0:P])
            nc.vector.tensor_copy(col_b, ps[:, 6, 0:74]).then_inc(rows_ev, 1)
            dve.wait_ge(c_exp, 1)
            link(ts(cs, cs, 1.0, None, ALU.add))
            link(nc.vector.reciprocal(cs, cs))
            link(tt(cs, cs, col_c, ALU.mult))

            def ada(s, q, full, prev, k, start):
                dve.wait_ge(ada_full[q], full)
                if prev is not None:
                    dve.wait_ge(ada_used, prev)
                if start:
                    ins = ts(acc[:, s % 2, :], ring[:, q, :], cs[:, k:k + 1], None, ALU.mult)
                else:
                    scal = cs[:, k:k + 1] if isinstance(k, int) else cs[:, bass.ds(k, 1)]
                    ins = stt(acc[:, s % 2, :], ring[:, q, :], scal, acc[:, s % 2, :], ALU.mult, ALU.add)
                ins.then_inc(ada_used, 1)

            def section(s):
                m0 = s * KD
                for q in range(RING):
                    ada(s, q, 16 * (m0 // RING + 1), m0 + q if q else None, q, q == 0)
                with dve.Fori(1, KD // RING) as it:
                    for q in range(RING):
                        ada(s, q, it * 16 + 16 * (m0 // RING + 1), it * RING + (m0 + q), it * RING + q, False)

            def ada_step(n):
                s, k = n // KD, n % KD
                if k == 0:
                    dve.wait_ge(gg_mm if s == 5 else mod_mm, 1 if s == 5 else s - 1)
                ada(s, n % RING, 16 * (n // RING + 1), n, k, k == 0)

            def w_low(m):
                n = width(m)
                dve.wait_ge(w_hi, nth[m] + 1)
                tt(wlo[:, m % WRING, 0:n], wring[:, m % WRING, 0:n], whi[nth[m] % 2][:, 0:n].bitcast(F32),
                   ALU.subtract).then_inc(w_split, 1)

            def act_parts(k, n, hi, lo, done):
                link(nc.vector.tensor_copy(hi[:, k:k + n, :], act_t[:, k:k + n, :]))
                tt(lo[:, k:k + n, :], act_t[:, k:k + n, :], hi[:, k:k + n, :].bitcast(F32), ALU.subtract).then_inc(done, 1)

            def mod_out(s):
                dve.wait_ge(mod_mm, max(s + 1, 2))
                bank = 7 if s < 4 else 0
                tt(mod[:, 16 * s:16 * s + 16], ps[:, bank, P + 16 * s:P + 16 * s + 16], col_a[:, 16 * s:16 * s + 16],
                   ALU.add).then_inc(mod_ok if s != 1 else dve_chain, 1)
                chain[0] += s == 1

            section(0)
            dve.wait_ge(x_ssq, TT)
            rms(ssq[0], D).then_inc(x_rms, 1)
            dve.wait_ge(x_sqrt, 1)
            nc.vector.reciprocal(rst[0], rst[0]).then_inc(x_rstd, 1)
            section(1)
            mod_out(0)
            mod_out(1)
            dve.wait_ge(dve_chain, chain[0])
            stt(sc1, mod[:, 16:32], 1.0, g_pm, ALU.add, ALU.mult).then_inc(mod_ok, 1)
            w_low(0)
            w_low(1)
            dve.wait_ge(xt_mm, KD // 2)
            for k in range(0, KD, 2):
                if k == 8:
                    w_low(2)
                dve.wait_ge(xt_ev, k + 2)
                act_parts(k, 2, act_hi, act_lo, act_split)
            n = 2 * KD
            for m in range(3, end["lat"]):
                w_low(m)
                if m % 4 != 3 if m < first["lat"] else m % 2:
                    ada_step(n)
                    n += 1
            late = (n + ADA_EARLY) // 2

            dve.wait_ge(sq_mm, 1)
            link(ts(rb[:, 0, :], ps[:, 3, 0:T], 1.0 / QR, EPS, ALU.mult, ALU.add))
            ts(rb[:, 1, :], ps[:, 3, T:2 * T], 1.0 / KVR, EPS, ALU.mult, ALU.add).then_inc(sq_aff, 1)
            dve.wait_ge(sq_root, 1)
            link(nc.vector.reciprocal(rb, rb))
            dve.wait_ge(in_ev, 18)
            for k in range(10):
                stt(lat[:, k, :], lat[:, k, :], g_lat[:, k:k + 1], rb[:, int(k >= KQ), :], ALU.mult, ALU.mult
                    ).then_inc(lat_n, 1)
            mod_out(2)
            dve.wait_ge(mod_ok, 3)
            link(tt(gg1, mod[:, 32:48], g_om, ALU.mult))
            for m in range(n, late):
                ada_step(m)
            dve.wait_ge(rot_mm, 1)
            dve.wait_ge(uq_ev, 3)
            cos4, sin4 = (v.unsqueeze(1).to_broadcast([P, MH // 2, T]) for v in (cos, sin))
            tt(rt, ps[:, 4:6, :].rearrange("p a (b t) -> p (a b) t", b=2), sin4, ALU.mult)
            tt(krope, ps[:, 6, 0:T], cos, ALU.mult)
            tt(krt, ps[:, 6, T:2 * T], sin, ALU.mult)
            link(tt(qr, qr, cos4, ALU.mult))
            tt(krope, krope, krt, ALU.add)
            tt(qr, qr, rt, ALU.add).then_inc(rope_ok, 1)
            for m in range(late, ADA_EARLY):
                ada_step(m)
            w_low(first["out"])

            def biased(h):
                b = h % 2
                dve.wait_ge(s_mm, h + 1)
                if h >= 3:
                    dve.wait_ge(pt_mm, h - 2)
                off, slope = (F_MASK, 1.0) if h < MH else (F_DIST, 2.0 ** (-(h - MH + 1.0)))
                s = sc[h % 3]
                stt(s, front[:, off:off + 384], slope, ps[:, h % 3, 0:384], ALU.mult, ALU.add).then_inc(s_add, 1)
                dve.wait_ge(s_add, h + 1)
                nc.vector.reduce_max(smax[:, b, 0:1], s[:, 0:P], AX)
                link(nc.vector.reduce_max(smax[:, b, 1:2], s[:, P:3 * P], AX))
                ts(nmax[:, b, :], smax[:, b, :], -1.0, None, ALU.mult).then_inc(s_max, 1)

            def normed(h):
                b = h % 2
                dve.wait_ge(s_exp, h + 1)
                link(nc.vector.reciprocal(erec[:, b, :], esum[:, b, :]))
                s = sc[h % 3]
                ts(s[:, 0:P], s[:, 0:P], erec[:, b, 0:1], None, ALU.mult)
                ts(s[:, P:3 * P], s[:, P:3 * P], erec[:, b, 1:2], None, ALU.mult).then_inc(s_norm, 1)

            biased(0)
            for h in range(2 * MH):
                if h + 1 < 2 * MH:
                    biased(h + 1)
                normed(h)
                if h == 2:
                    mod_out(3)
                if h == 3:
                    for k in range(KD):
                        ins = ts(diag[:, k * P:(k + 1) * P], ident, gg1[:, k:k + 1], None, ALU.mult)
                    ins.then_inc(diag_ok, 1)
            dve.wait_ge(sq_mm, 2)
            for g in range(2):
                ins = ts(rb[:, g, :], ps[:, 7, g * T:(g + 1) * T], 1.0 / (MH * HD), EPS, ALU.mult, ALU.add)
            ins.then_inc(sq_aff, 1)
            dve.wait_ge(sq_root, 2)
            link(nc.vector.reciprocal(rb, rb))

            def o_parts(k):
                link(stt(act_t[:, k, :], act_t[:, k, :], g_att[:, k:k + 1], rb[:, k // MH, :], ALU.mult, ALU.mult))
                act_parts(k, 1, act_hi, act_lo, act_split)

            n = ADA_EARLY
            for k in range(2):
                o_parts(k)
            for k in range(KD):
                w_low(first["out"] + k + 1)
                if k % 4 != 3:
                    ada_step(n)
                    n += 1
                if k + 2 < KD:
                    o_parts(k + 2)
            dve.wait_ge(gg_ev, 1)
            dve.wait_ge(w_used, end["out"])
            for t in (1, 0):
                if t == 0:
                    dve.wait_ge(y_ssq, 1)
                tt(x1_tmp[:, t, :], ps[:, 4 * t:4 * t + 4, :].rearrange("p a n -> p (a n)"), gg1_all, ALU.mult
                   ).then_inc(y_tmp, 1)
            dve.wait_ge(y_ssq, TT)
            rms(ssq[1], D).then_inc(y_aff, 1)
            dve.wait_ge(y_root, 1)
            link(nc.vector.reciprocal(rst[1], rst[1]))
            dve.wait_ge(y_tmp, TT)
            for t in range(TT):
                stt(xs[:, t, :], x1_tmp[:, t, :], rst[1][:, t:t + 1], xs[:, t, :], ALU.mult, ALU.add).then_inc(x1_ok, 1)
            dve.wait_ge(sub_mm, 1)
            nc.vector.tensor_copy(subt.rearrange("p h n -> p (h n)"),
                                  ps[:, 4:8, :].rearrange("p a n -> p (a n)")).then_inc(sub_ev, 1)
            mod_out(4)
            dve.wait_ge(mod_ok, 5)
            stt(sc2, mod[:, 64:80], 1.0, g_pf, ALU.add, ALU.mult).then_inc(mod_ok, 1)
            dve.wait_ge(n_ssq, TT)
            rms(ssq[2], D).then_inc(n_aff, 1)
            dve.wait_ge(n_root, 1)
            nc.vector.reciprocal(rst[2], rst[2]).then_inc(n_rstd, 1)
            dve.wait_ge(n_rstd, 1)
            ts(xn[:, 1, :], xs[:, 1, :], rst[2][:, 1:2], None, ALU.mult).then_inc(xn2b_ok, 1)
            w_low(first["pq0"] + 1)
            dve.wait_ge(x2t_mm, KD // 2)
            for k in range(0, KD, 2):
                if k == 8:
                    w_low(first["pq0"] + 2)
                dve.wait_ge(x2t_ev, k + 2)
                act_parts(k, 2, h2[:, 0, :, :], h2[:, 1, :, :], h2_split)
            for m in range(first["pq0"] + 3, end["pq1"]):
                w_low(m)
                if n < 6 * KD:
                    ada_step(n)
                    n += 1
            for m in range(n, 6 * KD):
                ada_step(m)
            mod_out(5)
            dve.wait_ge(mod_ok, 7)
            link(tt(gg2, mod[:, 80:96], g_of, ALU.mult))

            def top16(n, vals, out_v, out_i):
                for h in range(n):
                    ins = nc.vector.max(out_v[:, h, 0:8], vals(h))
                link(ins)
                yield
                for h in range(n):
                    ins = nc.vector.max_index(out_i[:, h, 0:8], out_v[:, h, 0:8], vals(h))
                link(ins)
                yield
                for h in range(n):
                    ins = nc.vector.match_replace(vals(h), out_v[:, h, 0:8], vals(h), -3.4e38)
                link(ins)
                yield
                for h in range(n):
                    ins = nc.vector.max(out_v[:, h, 8:16], vals(h))
                link(ins)
                yield
                for h in range(n):
                    ins = nc.vector.max_index(out_i[:, h, 8:16], out_v[:, h, 8:16], vals(h))
                link(ins)
                yield

            cand4 = cand[:, :].rearrange("p (h a b) -> p h a b", h=PH, a=PK)
            full = [P, PH, PK, PK]
            heads = [P, PH, PK]

            def routing():
                dve.wait_ge(ks_mm, TT)
                for t in range(TT):
                    dve.wait_ge(ks_ev, t + 1)
                    yield from top16(16, lambda h: rs[t][:, h * NK:(h + 1) * NK], top_v, top_i)
                    nc.vector.tensor_copy(top_f, top_i)
                    tv = top_v.rearrange("p (h s) k -> p h s k", s=2)
                    tf = top_f.rearrange("p (h s) k -> p h s k", s=2)
                    link(tt(cand4, tv[:, :, 0, :].unsqueeze(3).to_broadcast(full),
                            tv[:, :, 1, :].unsqueeze(2).to_broadcast(full), ALU.add))
                    yield from top16(PH, lambda h: cand[:, h * 256:(h + 1) * 256], pick_v, pick_s)
                    link(nc.vector.tensor_copy(rsum[:, 0:8].unsqueeze(2), pick_v[:, :, 0:1]))
                    tt(pick_v, pick_v, rsum[:, 0:8].unsqueeze(2).to_broadcast(heads), ALU.subtract).then_inc(r_max, 1)
                    ts(slot_u[:, 0], pick_s, 4, None, ALU.logical_shift_right)
                    link(ts(slot_u[:, 1], pick_s, 15, None, ALU.bitwise_and))
                    link(nc.vector.tensor_copy(slot_f, slot_u))
                    for s in range(2):
                        link(tt(cand4, slot_f[:, s].unsqueeze(3).to_broadcast(full),
                                iota[:, 0:PK].unsqueeze(1).unsqueeze(1).to_broadcast(full), ALU.is_equal))
                        yield
                        link(tt(cand4, cand4, tf[:, :, s, :].unsqueeze(2).to_broadcast(full), ALU.mult))
                        yield
                        link(nc.vector.reduce_sum(rout[:, t, s, :].rearrange("p (h k) -> p h k", h=PH), cand4, AX))
                        yield
                    dve.wait_ge(r_exp, t + 1)
                    link(nc.vector.reduce_sum(rsum[:, 0:8], pick_v, AX))
                    link(nc.vector.reciprocal(rsum[:, 8:16], rsum[:, 0:8]))
                    tt(rout[:, t, 2, :].rearrange("p (h k) -> p h k", h=PH), pick_v,
                       rsum[:, 8:16].unsqueeze(2).to_broadcast(heads), ALU.mult).then_inc(r_ok, 1)
                    dve.wait_ge(r_ok, t + 1)
                    yield

            def u_low(b, hi):
                for hf in range(2):
                    dve.wait_ge(u_hi, hi + hf)
                    tt(uv[:, b, 1, hf * 1024:(hf + 1) * 1024], ps[:, 2 * hf:2 * hf + 2, :].rearrange("p a n -> p (a n)"),
                       uv[:, b, 0, hf * 1024:(hf + 1) * 1024].bitcast(F32), ALU.subtract).then_inc(u_split, 1)

            def hots(b, j0, t0, made, used):
                if used is not None:
                    dve.wait_ge(g_mm, used)
                shape = [P, TB, GJ]
                tt(hot_e[:, b], iota[:, j0:j0 + GJ].unsqueeze(1).to_broadcast(shape),
                   ridx[:, 1, t0].unsqueeze(2).to_broadcast(shape), ALU.is_equal).then_inc(hot_eq, 1)
                tt(hot_i[:, b], iota.unsqueeze(1).to_broadcast([P, TB, NK]),
                   ridx[:, 0, t0].unsqueeze(2).to_broadcast([P, TB, NK]), ALU.is_equal)
                dve.wait_ge(hot_eq, made)
                for part in range(3):
                    ins = tt(hot_j[:, b, part], hot_e[:, b], w_part[:, part, t0].unsqueeze(2).to_broadcast(shape),
                             ALU.mult)
                ins.then_inc(hot_ok, 1)

            def product(b, j, free):
                if free is not None:
                    dve.wait_ge(v_split, free)
                tt(wj[:, b, :], column(gs, j), column(pw, j), ALU.mult).then_inc(v_prod, 1)

            def v_low(q, hi):
                dve.wait_ge(v_hi, hi)
                tt(am[:, q % 2, 1, :], wj[:, q % 2, :], am[:, q % 2, 0, :].bitcast(F32), ALU.subtract)
                tt(uv[:, q % 2, 1, :], ring[:, q, :], uv[:, q % 2, 0, :].bitcast(F32), ALU.subtract).then_inc(v_split, 1)

            for g in range(GROUPS):
                n0 = g * GJ
                if g == 0:
                    route = routing()
                    for n in range(ROUTE_STEPS):
                        u_low(n % 2, 2 * n + 1)
                        for _ in range(2):
                            next(route, None)
                    assert next(route, None) is None
                    for n in range(ROUTE_STEPS, GJ):
                        u_low(n % 2, 2 * n + 1)
                        if n == ROUTE_STEPS:
                            dve.wait_ge(rt_ev, 1)
                            for part in range(3):
                                link(nc.vector.tensor_copy(w_part[:, part, :], w_rest[:, part, :]))
                                if part < 2:
                                    link(tt(w_rest[:, part + 1, :], w_rest[:, part, :], w_part[:, part, :],
                                            ALU.subtract))
                        m = 2 * (n - ROUTE_STEPS)
                        for b in range(2):
                            hots(b, 0, bass.ds((m + b) * TB, TB), m + b + 1, m + b - 1 if m else None)
                    for m in range(2 * (GJ - ROUTE_STEPS), T // TB):
                        hots(m % 2, 0, bass.ds(m * TB, TB), m + 1, m - 1)
                else:
                    for n in range(RING):
                        u_low(n % 2, 2 * (n0 + n) + 1)
                        hots(n % 2, n0, bass.ds(n * TB, TB), n0 + n + 1, n0 + n - 1)
                    with dve.Fori(1, GJ // RING) as it:
                        for q in range(RING):
                            u_low(q % 2, it * (2 * RING) + (2 * (n0 + q) + 1))
                            hots(q % 2, n0, bass.ds(it * (RING * TB) + q * TB, TB), it * RING + (n0 + q + 1),
                                 it * RING + (n0 + q - 1))
                dve.wait_ge(g_ev, n0 + GJ)
                dve.wait_ge(u_gelu, n0 + 1)
                product(0, 0, None)
                dve.wait_ge(u_gelu, n0 + GJ)
                product(1, 1, None)
                with dve.Fori(0, GJ // RING - 1) as it:
                    for q in range(RING):
                        v_low(q, it * RING + (n0 + q + 1))
                        product(q % 2, it * RING + (q + 2), it * RING + (n0 + q + 1))
                for q in range(RING):
                    v_low(q, n0 + GJ - RING + q + 1)
                    if q < 2:
                        product(q, GJ - 2 + q, n0 + GJ - RING + q + 1)
                dve.wait_ge(v_mm, n0 + GJ)
                for t in range(TT):
                    for n in range(4):
                        y = yacc[t][:, n * 512:(n + 1) * 512]
                        ins = tt(y, y, ps[:, 4 * t + n, :], ALU.add) if g else nc.vector.tensor_copy(y, ps[:, 4 * t + n, :])
                        ins.then_inc(y_ev, 1)
            for k in range(KD):
                ins = ts(gs_flat[:, k * P:(k + 1) * P], ident, gg2[:, k:k + 1], None, ALU.mult)
            ins.then_inc(f_diag, 1)
            dve.wait_ge(f_ssq, TT)
            rms(ssq[3], D).then_inc(f_aff, 1)
            dve.wait_ge(f_root, 1)
            link(nc.vector.reciprocal(rst[3], rst[3]))
            dve.wait_ge(x1_ld, 16)
            dve.wait_ge(f_gg, 1)
            for t in range(TT):
                link(stt(yacc[t][:, :], yacc[t][:, :], rst[3][:, t:t + 1], ps[:, 0:4, :].rearrange("p a n -> p (a n)"),
                         ALU.mult, ALU.mult))
                tt(xs[:, t, :], xs[:, t, :], yacc[t][:, :], ALU.add).then_inc(f_out, 1)


def kernel(**inputs):
    import concourse.bacc as bacc
    from concourse.bass_utils import run_bass_kernel_spmd

    names = ["x", "c", "w_ada", "b_ada", "g_pre_mix", "w_in", "g_q_lat", "w_uq", "g_kv_lat", "w_ukv", "g_out_mla",
             "g_out_moba", "w_out", "g_post_mix", "g_pre_ffn", "w_peer_q", "sub_keys_1", "sub_keys_2", "u_experts",
             "v_experts", "g_post_ffn"]
    nc = bacc.Bacc("TRN2", target_bir_lowering=False, num_devices=1)
    arrays = {name: np.ascontiguousarray(inputs[name]) for name in names}
    arrays["const_per"], arrays["const_front"] = tables()
    args = {name: nc.dram_tensor(name, a.shape, F32, kind="ExternalInput").ap() for name, a in arrays.items()}
    out = nc.dram_tensor("out", (1, T, D), F32, kind="ExternalOutput").ap()
    build(nc, **args, out=out)
    r = run_bass_kernel_spmd(nc, [arrays], core_ids=[0])
    return r.results[0]["out"]
```

```python
from contextlib import ExitStack

import numpy as np

import concourse.bass as bass
from concourse import mybir

P = 128
D = 2048
T = 256
TT = T // P
KD = D // P
QR, KVR, ROPE, HD = 768, 512, 64, 128
LAT = QR + KVR + ROPE
KQ, KKV = QR // P, KVR // P
MH = 8
W_MOBA = MH * HD
NK = 128
PH, PK = 8, 16
GROUPS = 4
GJ = NK // GROUPS
RING = 4
WRING = 4
ROUTE_STEPS = 20
TB = 8
EPS = 1e-6
BIG = -1e30
BF16 = mybir.dt.bfloat16

F32 = mybir.dt.float32
F32R = mybir.dt.float32r
U32 = mybir.dt.uint32
ACT = mybir.ActivationFunctionType
ALU = mybir.AluOpType
AX = mybir.AxisListType.X

C_ID, C_ONE, C_IOTA, C_PER = 0, 128, 256, 384
F_DIST, F_MASK, F_COS, F_SIN, F_RQ, F_DK, F_RK, C_FRONT = 0, 384, 768, 1024, 1280, 1408, 1536, 1664
ADA_EARLY = 70
X_ORDER = (0, 1, 14, 15, *range(2, 14))
LAT_BANKS = (0, 1, 2, 4, 5, 6)
SET_A, SET_B = (0, 1, 2, 4), (3, 5, 6, 7)
S_BANKS, PT_BANKS, O_BANKS = (3, 5, 6), (0, 1), (2, 4)


def tables():
    per = np.zeros((P, C_PER), np.float32)
    per[:, C_ID:C_ID + P] = np.eye(P, dtype=np.float32)
    per[:, C_ONE:C_ONE + P] = 1.0
    per[:, C_IOTA:C_IOTA + P] = np.arange(P, dtype=np.float32)[None, :]
    fr = np.zeros((P, C_FRONT), np.float32)
    q = np.arange(T)[:, None]
    k = np.arange(T)[None, :]
    dist = np.where(k <= q, (k - q).astype(np.float32), np.float32(BIG)).astype(np.float32)
    mask = np.where(k <= q, np.float32(0), np.float32(BIG)).astype(np.float32)
    for off, m in ((F_DIST, dist), (F_MASK, mask)):
        fr[:, off:off + P] = m[0:P, 0:P]
        fr[:, off + P:off + 3 * P] = m[P:T, :]
    half = ROPE // 2
    inv = (np.float32(10000.0) ** (-np.arange(half, dtype=np.float32) / np.float32(half))).astype(np.float32)
    ang = (np.arange(T, dtype=np.float32)[:, None] * inv[None, :]).astype(np.float32)
    fr[:, F_COS:F_COS + T] = np.tile(np.cos(ang).T, (4, 1))
    fr[:, F_SIN:F_SIN + T] = np.tile(np.sin(ang).T, (4, 1))
    rot = np.zeros((ROPE, ROPE), np.float32)
    for j in range(half):
        rot[half + j, j] = -1.0
        rot[j, half + j] = 1.0
    fr[0:ROPE, F_RQ:F_RQ + ROPE] = rot
    fr[ROPE:P, F_RQ + ROPE:F_RQ + P] = rot
    eye = np.eye(ROPE, dtype=np.float32)
    fr[0:ROPE, F_DK:F_DK + P] = np.concatenate([eye, eye], 1)
    fr[0:ROPE, F_RK:F_RK + P] = np.concatenate([rot, rot], 1)
    return per, fr


def build(nc, x, c, w_ada, b_ada, g_pre_mix, w_in, g_q_lat, w_uq, g_kv_lat, w_ukv, g_out_mla,
          g_out_moba, w_out, g_post_mix, g_pre_ffn, w_peer_q, sub_keys_1, sub_keys_2, u_experts,
          v_experts, g_post_ffn, const_per, const_front, out):
    base = -(-nc.sbuf_base // 64) * 64
    zone = 16384 + 32768 + 4 * C_PER + 2048 + 2048

    def at(name, off, shape, dt=F32):
        return nc.alloc_sbuf_tensor_at(name, shape, dt, offset=base + off)

    xs = at("xs", 0, [P, TT, D])
    ring = at("ring", 16384, [P, RING, D])
    per = at("per", 49152, [P, C_PER])
    small = at("small", 49152 + 4 * C_PER, [P, 512])
    ridx = at("ridx", 49152 + 4 * C_PER + 2048, [P, 2, T])
    wring = at("wring", zone + 0, [P, WRING, D])
    wlo = at("wlo", zone + 0, [P, WRING, D], F32R)
    whi = [at("whi0", zone + 32768, [P, D], F32R), at("whi1", zone + 142336, [P, D], F32R)]
    acc = at("acc", zone + 40960, [P, 2, D])
    act_t = at("act_t", zone + 57344, [P, KD, T])
    lat = at("lat", zone + 73728, [P, 11, T])
    mqk = at("mqk", zone + 84992, [P, 2 * MH, T])
    mv = at("mv", zone + 101376, [P, TT, W_MOBA])
    mla = at("mla", zone + 109568, [P, 7168])
    act_hi = at("act_hi", zone + 109568, [P, KD, T], F32R)
    act_lo = at("act_lo", zone + 57344, [P, KD, T], F32R)
    front = at("front", zone + 138240, [P, C_FRONT])
    work = at("work", zone + 144896, [P, 2560])
    uv = at("uv", zone + 0, [P, 2, 2, D], F32R)
    gs = at("gs", zone + 32768, [P, GJ, T])
    pw = at("pw", zone + 65536, [P, GJ, T])
    yacc = [at("yacc0", zone + 98304, [P, D]), at("yacc1", zone + 142336, [P, D])]
    wj = at("wj", zone + 106496, [P, 2, T])
    h2 = at("h2", zone + 109568, [P, 2, KD, T], F32R)
    am = at("am", zone + 150528, [P, 2, 2, T], F32R)
    zero = at("zero", zone + 155136, [P, P])
    hot_i = at("hot_i", 0, [P, 2, TB, NK], BF16)
    hot_j = at("hot_j", 4096, [P, 2, 3, TB, GJ], BF16)
    hot_e = at("hot_e", 7168, [P, 2, TB, GJ], BF16)
    w_part = at("w_part", 8192, [P, 3, T], BF16)
    w_rest = at("w_rest", 9728, [P, 3, T])
    rs = [at("rs0", zone + 142336, [P, D]), at("rs1", zone + 83456, [P, D])]
    cand = at("cand", zone + 75264, [P, D])
    rwork = at("rwork", zone + 65536, [P, 2320])

    ident, ones, iota = per[:, 0:P], per[:, P:2 * P], per[:, 2 * P:3 * P]
    col_a = small[:, 0:128]
    col_b = small[:, 128:202]
    g_pm, g_pf = col_a[:, 96:112], col_a[:, 112:128]
    col_c, g_om, g_of = col_b[:, 0:16], col_b[:, 16:32], col_b[:, 32:48]
    g_lat, g_att = col_b[:, 48:58], col_b[:, 58:74]
    mod = small[:, 208:304]
    cs = small[:, 304:320]
    sc1, sc2 = small[:, 320:336], small[:, 336:352]
    gg1, gg2 = small[:, 352:368], small[:, 368:384]
    st = small[:, 400:512]
    ssq = [st[:, 2 * n:2 * n + 2] for n in range(4)]
    rst = [st[:, 8 + 2 * n:10 + 2 * n] for n in range(4)]
    smax = st[:, 32:36].rearrange("p (b q) -> p b q", b=2)
    nmax = st[:, 36:40].rearrange("p (b q) -> p b q", b=2)
    esum = st[:, 40:44].rearrange("p (b q) -> p b q", b=2)
    erec = st[:, 44:48].rearrange("p (b q) -> p b q", b=2)

    cos, sin = front[:, F_COS:F_COS + T], front[:, F_SIN:F_SIN + T]
    rows = work[:, 0:256]
    sc = [work[:, 0:384], work[:, 384:768], front[:, F_RQ:F_RQ + 384]]
    pt = work[:, 768:1536].rearrange("p (b n) -> p b n", b=2)
    rb = work[:, 1536:2048].rearrange("p (g t) -> p g t", g=2)
    krope = work[:, 2048:2304]
    krt = work[:, 2304:2560]
    xn = mla[:, 0:2 * D].rearrange("p (t d) -> p t d", t=TT)
    qn = mla[:, 0:2048].rearrange("p (h t) -> p h t", h=MH)
    kn = mla[:, 2048:4096].rearrange("p (h t) -> p h t", h=MH)
    vv = mla[:, 4096:6144].rearrange("p (b n) -> p b n", b=TT)
    qr = mla[:, 6144:7168].rearrange("p (m t) -> p m t", m=MH // 2)
    sq_lat = mla[:, 4096:6656].rearrange("p (k t) -> p k t", k=10)
    rt = mla[:, 4096:5120].rearrange("p (m t) -> p m t", m=MH // 2)
    subt = mv[:, :, :].rearrange("p a b -> p (a b)").rearrange("p (h n) -> p h n", h=16)
    subk = lat[:, 0:8, :].rearrange("p a b -> p (a b)").rearrange("p (h n) -> p h n", h=16)
    top_v = rwork[:, 0:256].rearrange("p (h k) -> p h k", h=16)
    top_i = rwork[:, 256:512].bitcast(U32).rearrange("p (h k) -> p h k", h=16)
    top_f = rwork[:, 512:768].rearrange("p (h k) -> p h k", h=16)
    pick_v = rwork[:, 768:896].rearrange("p (h k) -> p h k", h=PH)
    pick_s = rwork[:, 896:1024].bitcast(U32).rearrange("p (h k) -> p h k", h=PH)
    slot_u = rwork[:, 1024:1280].bitcast(U32).rearrange("p (s h k) -> p s h k", s=2, h=PH)
    slot_f = rwork[:, 1280:1536].rearrange("p (s h k) -> p s h k", s=2, h=PH)
    rout = rwork[:, 1536:2304].rearrange("p (t s n) -> p t s n", t=TT, s=3)
    rsum = rwork[:, 2304:2320]
    gg1_all = mla[:, 4096:4096 + D]
    diag = acc[:, 1, :]
    x1_tmp = mqk[:, :, :].rearrange("p (b a) t -> p b (a t)", b=TT)

    with ExitStack() as ctx:
        ps = ctx.enter_context(nc.psum_tensor("ps", [P, 8, 512], F32))

        def sem(name):
            return ctx.enter_context(nc.semaphore(name))

        ld_per, ld_front, ld_rows, ld_x, ld_sub = map(sem, ("ld_per", "ld_front", "ld_rows", "ld_x", "ld_sub"))
        w_full = [sem(f"w_full{n}") for n in range(WRING)]
        ada_full = [sem(f"ada_full{n}") for n in range(RING)]
        e_full = [sem(f"e_full{n}") for n in range(RING)]
        w_hi, w_split = sem("w_hi"), sem("w_split")
        act_split, h2_split, sq_head = sem("act_split"), sem("h2_split"), sem("sq_head")
        k_mm = sem("k_mm")
        y_tmp, xn2b_ok = sem("y_tmp"), sem("xn2b_ok")
        w_used = sem("w_used")
        ada_used = sem("ada_used")
        rows_t, rows_ev = sem("rows_t"), sem("rows_ev")
        c_exp = sem("c_exp")
        x_ssq, x_rms, x_sqrt, x_rstd, xn_ok = map(sem, ("x_ssq", "x_rms", "x_sqrt", "x_rstd", "xn_ok"))
        xt_mm, xt_ev = sem("xt_mm"), sem("xt_ev")
        mod_mm, mod_ok = sem("mod_mm"), sem("mod_ok")
        in_ev = sem("in_ev")
        sq_ok, sq_mm, sq_aff, sq_root = map(sem, ("sq_ok", "sq_mm", "sq_aff", "sq_root"))
        lat_n, uq_ev, rot_mm, rope_ok, ukv_ev = map(sem, ("lat_n", "uq_ev", "rot_mm", "rope_ok", "ukv_ev"))
        s_mm, s_add, s_max, s_exp, s_norm, pt_mm, pt_ev, o_mm, o_ev = map(sem, (
            "s_mm", "s_add", "s_max", "s_exp", "s_norm", "pt_mm", "pt_ev", "o_mm", "o_ev"))
        diag_ok, gg_mm, gg_ev, y_ssq, y_aff, y_root, x1_ok = map(sem, (
            "diag_ok", "gg_mm", "gg_ev", "y_ssq", "y_aff", "y_root", "x1_ok"))
        n_ssq, n_aff, n_root, n_rstd, xn2_ok, x2t_mm, x2t_ev = map(sem, (
            "n_ssq", "n_aff", "n_root", "n_rstd", "xn2_ok", "x2t_mm", "x2t_ev"))
        sub_mm, sub_ev, pq_ev, ks_mm, ks_ev = map(sem, ("sub_mm", "sub_ev", "pq_ev", "ks_mm", "ks_ev"))
        r_max, r_exp, r_ok, rt_mm, rt_ev = map(sem, ("r_max", "r_exp", "r_ok", "rt_mm", "rt_ev"))
        u_tr, u_hi, u_split, u_mm, u_gelu = map(sem, ("u_tr", "u_hi", "u_split", "u_mm", "u_gelu"))
        hot_ok, g_mm, g_ev = map(sem, ("hot_ok", "g_mm", "g_ev"))
        v_prod, v_hi, v_split, v_mm, y_ev = map(sem, ("v_prod", "v_hi", "v_split", "v_mm", "y_ev"))
        x1_st, x1_ld = map(sem, ("x1_st", "x1_ld"))
        f_ssq, f_aff, f_root, f_diag, f_gg, f_out, st_out = map(sem, (
            "f_ssq", "f_aff", "f_root", "f_diag", "f_gg", "f_out", "st_out"))
        hot_eq, zero_ok, hot_j_ok = map(sem, ("hot_eq", "zero_ok", "hot_j_ok"))
        v_half, v_whi, y_gated = map(sem, ("v_half", "v_whi", "y_gated"))
        dve_chain, act_chain = sem("dve_chain"), sem("act_chain")
        gs_flat = gs[:, :, :].rearrange("p j t -> p (j t)")
        x1_dram = nc.dram_tensor("x1_dram", (P, TT, D), F32, kind="Internal").ap()

        def column(tile, j):
            return tile[:, bass.ds(j, 1), :].rearrange("p a t -> p (a t)")

        block = ctx.enter_context(nc.Block())

        win = w_in[0].rearrange("(k p) n -> p k n", p=P)
        wuq = w_uq[0].rearrange("(k p) n -> p k n", p=P)
        wukv = w_ukv[0].rearrange("(k p) n -> p k n", p=P)
        wout = w_out[0].rearrange("(k p) n -> p k n", p=P)
        wpq = w_peer_q[0].rearrange("(k p) n -> p k n", p=P)
        stream = []
        first = {}

        def plan(name, srcs):
            first[name] = len(stream)
            stream.extend(srcs)

        plan("lat", [win[:, k:k + 1, 0:LAT] for k in range(KD)])
        for name, c0 in (("mq", LAT), ("mk", LAT + W_MOBA), ("mv", LAT + 2 * W_MOBA)):
            plan(name, [win[:, k:k + 2, c0:c0 + W_MOBA] for k in range(0, KD, 2)])
        plan("uq", [wuq[:, k:k + 1, :] for k in range(KQ)])
        plan("ukv", [wukv[:, k:k + 1, :] for k in range(KKV)])
        plan("out", [wout[:, k:k + 1, :] for k in range(KD)])
        for cg in range(2):
            plan(f"pq{cg}", [wpq[:, k:k + 2, cg * 1024:cg * 1024 + 1024] for k in range(0, KD, 2)])

        names = list(first) + [None]
        end = {n: first[m] if m else len(stream) for n, m in zip(names, names[1:])}

        chunks = [m for m in range(len(stream)) if not first["uq"] <= m < end["ukv"]]
        nth = {m: i for i, m in enumerate(chunks)}

        def width(m):
            _, k, n = stream[m].shape
            return k * n

        def part(m, lo, off, n):
            return wlo[:, m % WRING, off:off + n] if lo else whi[nth[m] % 2][:, off:off + n]

        def w_loads(m):
            return sum(2 if first["uq"] <= n < end["uq"] else 1 for n in range(m % WRING, m + 1, WRING))

        def uq_nope(m):
            return wring[:, m % WRING, 0:MH * HD].rearrange("p (h c) -> p h c", c=HD)

        def uq_rope(m):
            return wring[:, m % WRING, MH * HD:MH * (HD + ROPE)].rearrange("p (h c) -> p h c", c=ROPE)

        def w_slot(m):
            _, k, n = stream[m].shape
            return wring[:, m % WRING, 0:k * n].rearrange("p (k n) -> p k n", k=k)

        batches, m = {}, 0
        for n in range(ROUTE_STEPS, GJ):
            left = T // TB - m
            count = -(-left // (GJ - n))
            batches[n] = range(m, m + count)
            m += count

        def head_sq(h):
            return lat[:, h, :] if h < MH else mqk[:, h - MH, :]

        uv_dram = [e[0].rearrange("(i j) d -> i j d", j=NK) for e in (u_experts, v_experts)]

        @block.sync
        def _(sp):
            sp.dma_start(per[:, :], const_per).then_inc(ld_per, 16)
            r0 = 0
            for v, n in ((b_ada, 96), (g_pre_mix, 16), (g_pre_ffn, 16)):
                sp.dma_start(rows[r0:r0 + n, 0:P], v.rearrange("a (k p) -> (a k) p", p=P)).then_inc(ld_rows, 16)
                r0 += n
            r0 = 0
            for v, n in ((c, 16), (g_post_mix, 16), (g_post_ffn, 16), (g_q_lat, KQ), (g_kv_lat, KKV),
                         (g_out_mla, MH), (g_out_moba, MH)):
                sp.dma_start(rows[r0:r0 + n, P:2 * P], v.rearrange("a (k p) -> (a k) p", p=P)).then_inc(ld_rows, 16)
                r0 += n
            sp.dma_start(xs[:, :, :], x[0].rearrange("(t p) d -> p t d", p=P)).then_inc(ld_x, 16)
            sp.wait_ge(ada_used, 28)
            for m, src in enumerate(stream):
                if m >= WRING:
                    sp.wait_ge(w_used, m - WRING + 1)
                if m == end["mv"] + WRING - 1:
                    sp.wait_ge(w_used, end["mv"])
                    sp.dma_start(front[:, :], const_front).then_inc(ld_front, 16)
                if m == end["ukv"] + WRING:
                    sp.wait_ge(sq_mm, 2)
                    for s, key in enumerate((sub_keys_1, sub_keys_2)):
                        sp.dma_start(subk.rearrange("p (h s) d -> p s h d", s=2)[:, s],
                                     key[0].rearrange("h n d -> n h d")).then_inc(ld_sub, 16)
                if first["uq"] <= m < end["uq"]:
                    hc = src.rearrange("p k (h c) -> p (k h) c", c=HD + ROPE)
                    sp.dma_start(uq_nope(m), hc[:, :, 0:HD]).then_inc(w_full[m % WRING], 16)
                    sp.dma_start(uq_rope(m), hc[:, :, HD:HD + ROPE]).then_inc(w_full[m % WRING], 16)
                else:
                    sp.dma_start(w_slot(m), src).then_inc(w_full[m % WRING], 16)

            sp.wait_ge(ada_used, 96)
            sp.wait_ge(x1_ok, TT)
            sp.dma_start(x1_dram, xs[:, :, :]).then_inc(x1_st, 16)
            for g in range(GROUPS):
                for phase in range(2):
                    src = uv_dram[phase]
                    j0 = g * GJ
                    taken = (u_tr, v_split)
                    step = (2, 1)
                    for q in range(RING):
                        if phase == 1:
                            sp.wait_ge(u_tr, 2 * ((g + 1) * GJ - RING + q + 1))
                        elif g:
                            sp.wait_ge(v_split, g * GJ - RING + q + 1)
                        sp.dma_start(ring[:, q, :], src[:, j0 + q, :]).then_inc(e_full[q], 16)
                    with sp.Fori(1, GJ // RING) as it:
                        for q in range(RING):
                            sp.wait_ge(taken[phase], (it * RING + (g * GJ - RING + q + 1)) * step[phase])
                            sp.dma_start(ring[:, q, :], src[:, bass.ds(it * RING + (j0 + q), 1), :]
                                         .rearrange("p a d -> p (a d)")).then_inc(e_full[q], 16)
                    if g == GROUPS - 1 and phase:
                        sp.wait_ge(x1_st, 16)
                        sp.wait_ge(g_mm, GROUPS * (T // TB))
                        sp.dma_start(xs[:, :, :], x1_dram).then_inc(x1_ld, 16)
            for t in range(TT):
                sp.wait_ge(f_out, t + 1)
                sp.dma_start(out[0, t * P:(t + 1) * P, :], xs[:, t, :]).then_inc(st_out, 16)
            sp.wait_ge(st_out, 16 * TT)

        @block.gpsimd
        def _(pool):
            for s in range(6):
                lo = 0
                if s == 0:
                    for q in range(RING):
                        pool.dma_start(ring[:, q, :], w_ada[0, q * P:(q + 1) * P, 0:D]).then_inc(ada_full[q], 16)
                    lo = 1
                if s == 4:
                    with pool.Fori(0, 2) as it:
                        for q in range(RING):
                            pool.wait_ge(ada_used, it * RING + (s * KD + q - RING + 1))
                            pool.dma_start(ring[:, q, :], w_ada[0, bass.ds((it * RING + q) * P, P), s * D:(s + 1) * D]
                                           ).then_inc(ada_full[q], 16)
                    for k in range(8, 12):
                        if k == ADA_EARLY - s * KD + RING:
                            pool.wait_ge(ukv_ev, 8)
                            for h in range(2 * MH):
                                pool.wait_ge(o_ev, h + 1)
                                nc.gpsimd.tensor_tensor(head_sq(h), act_t[:, h, :], act_t[:, h, :], ALU.mult
                                                        ).then_inc(sq_head, 1)
                        pool.wait_ge(ada_used, s * KD + k - RING + 1)
                        pool.dma_start(ring[:, k % RING, :], w_ada[0, k * P:(k + 1) * P, s * D:(s + 1) * D]
                                       ).then_inc(ada_full[k % RING], 16)
                    lo = 3
                with pool.Fori(lo, KD // RING) as it:
                    for q in range(RING):
                        pool.wait_ge(ada_used, it * RING + (s * KD + q - RING + 1))
                        pool.dma_start(ring[:, q, :], w_ada[0, bass.ds((it * RING + q) * P, P), s * D:(s + 1) * D]
                                       ).then_inc(ada_full[q], 16)

            def hot_columns(b, made, used, t0):
                pool.wait_ge(hot_eq, made)
                if used is not None:
                    pool.wait_ge(g_mm, used)
                for part in range(3):
                    ins = nc.gpsimd.tensor_tensor(hot_j[:, b, part], hot_e[:, b],
                                                  w_part[:, part, t0].unsqueeze(2).to_broadcast([P, TB, GJ]), ALU.mult)
                ins.then_inc(hot_j_ok, 1)

            for b in range(2):
                hot_columns(b, b + 1, None, bass.ds(b * TB, TB))
            for g in range(GROUPS):
                m0 = g * (T // TB)
                with pool.Fori(int(g == 0), T // TB // 2) as it:
                    for b in range(2):
                        hot_columns(b, it * 2 + (m0 + b + 1), it * 2 + (m0 + b - 1), bass.ds(it * (2 * TB) + b * TB, TB))

        @block.tensor
        def _(pe):
            mm = nc.tensor.matmul

            def w_wait(m):
                pe.wait_ge(w_full[m % WRING], 16 * w_loads(m))

            def half(bank, n):
                return ps[:, bank + n // 2, (n % 2) * T:(n % 2 + 1) * T]

            pe.wait_ge(ld_per, 16)
            pe.wait_ge(ld_rows, 160)
            nc.tensor.transpose(ps[:, 7, 0:P], rows[:, 0:P], ident)
            nc.tensor.transpose(ps[:, 6, 0:74], rows[0:74, P:2 * P], ident[0:74, 0:74]).then_inc(rows_t, 1)

            def x_tiles(k, src, bank, done):
                for kk in (k, k + 1):
                    for t in range(TT):
                        last = nc.tensor.transpose(ps[:, bank, (kk % 2) * T + t * P:(kk % 2) * T + t * P + P],
                                                   src[:, t, kk * P:(kk + 1) * P], ident)
                last.then_inc(done, 1)

            def mod_sum(s, bank=7):
                pe.wait_ge(ada_used, 16 * (s + 1))
                for k in range(KD):
                    last = mm(ps[:, bank, P + 16 * s + k:P + 16 * s + k + 1], acc[:, s % 2, k * P:(k + 1) * P],
                              ones[:, 0:1], start=True, stop=True)
                last.then_inc(mod_mm, 1)

            pe.wait_ge(rows_ev, 1)
            pe.wait_ge(xn_ok, TT)
            for k in range(0, 14, 2):
                x_tiles(k, xn, k // 2, xt_mm)
            mod_sum(0)
            mod_sum(1)
            pe.wait_ge(xt_ev, 2)
            x_tiles(14, xn, 0, xt_mm)

            def weight_left(m, off, w, dst, rhs, k, start):
                hi, lo = part(m, 0, off, w), part(m, 1, off, w)
                mm(dst, hi, rhs[0][:, k, :], start=start, stop=False, skip_group_check=True)
                mm(dst, hi, rhs[1][:, k, :], start=False, stop=False, skip_group_check=True)
                return mm(dst, lo, rhs[0][:, k, :], start=False, stop=k == KD - 1, skip_group_check=True)

            def weight_right(m, off, banks, k):
                per_t = len(banks) // TT
                for t in range(TT):
                    for a, lo in ((act_hi, 0), (act_hi, 1), (act_lo, 0)):
                        for n in range(per_t):
                            last = mm(ps[:, banks[per_t * t + n], :], a[:, k, t * P:(t + 1) * P],
                                      part(m, lo, off + n * 512, 512), start=k == 0 and a is act_hi and lo == 0,
                                      stop=k == KD - 1 and a is act_lo)
                return last

            def in_set(banks, n):
                return ps[:, banks[n // 2], (n % 2) * T:(n % 2 + 1) * T]

            h_parts = (act_hi, act_lo)
            for k in range(KD):
                m = first["lat"] + k
                pe.wait_ge(w_split, nth[m] + 1)
                pe.wait_ge(act_split, k // 2 + 1)
                for n in range(11):
                    if k == 0 and n % 2 == 0:
                        pe.wait_ge(xt_ev, 2 * LAT_BANKS[n // 2] + 4)
                    w = P if n < 10 else ROPE
                    last = weight_left(m, n * P, w, in_set(LAT_BANKS, n)[0:w], h_parts, k, k == 0 and n % 2 == 0)
                last.then_inc(w_used, 1)
            for name, banks in (("mq", SET_A), ("mk", SET_B)):
                if name == "mk":
                    pe.wait_ge(in_ev, 6)
                    pe.wait_ge(sq_aff, 1)
                for k in range(KD):
                    m = first[name] + k // 2
                    if k % 2 == 0:
                        pe.wait_ge(w_split, nth[m] + 1)
                    for h in range(MH):
                        if name == "mq" and k == 0 and h % 2 == 0:
                            pe.wait_ge(in_ev, h // 2 + 1)
                        last = weight_left(m, (k % 2) * W_MOBA + h * P, P, in_set(banks, h), h_parts, k,
                                           k == 0 and h % 2 == 0)
                    if k % 2:
                        last.then_inc(w_used, 1)
                    if name == "mq" and k == 5:
                        pe.wait_ge(sq_ok, 1)
                        for g, (a, b) in enumerate(((0, KQ), (KQ, KQ + KKV))):
                            for kk in range(a, b):
                                last = mm(ps[:, 3, g * T:(g + 1) * T], ones, sq_lat[:, kk, :], start=kk == a,
                                          stop=kk == b - 1)
                        last.then_inc(sq_mm, 1)
            pe.wait_ge(in_ev, 10)
            for k in range(KD):
                m = first["mv"] + k // 2
                if k % 2 == 0:
                    pe.wait_ge(w_split, nth[m] + 1)
                last = weight_right(m, (k % 2) * W_MOBA, SET_A, k)
                if k % 2:
                    last.then_inc(w_used, 1)
            pe.wait_ge(in_ev, 14)
            pe.wait_ge(lat_n, KQ)
            for k in range(KQ):
                m = first["uq"] + k
                w_wait(m)
                for h in range(MH):
                    mm(in_set(SET_B, h), uq_nope(m)[:, h, :], lat[:, k, :],
                       start=k == 0 and h % 2 == 0, stop=k == KQ - 1, skip_group_check=True)
                if k == 0:
                    pe.wait_ge(in_ev, 16)
                for j in range(MH // 2):
                    last = mm(half(0, j), uq_rope(m)[:, 2 * j:2 * j + 2, :].rearrange("p h c -> p (h c)"),
                              lat[:, k, :], start=k == 0 and j % 2 == 0, stop=k == KQ - 1, skip_group_check=True)
                last.then_inc(w_used, 1)
            pe.wait_ge(in_ev, 18)
            mod_sum(2, 2)
            pe.wait_ge(ld_front, 16)
            pe.wait_ge(uq_ev, 1)
            for j in range(MH // 2):
                mm(half(0, j), front[:, F_RQ:F_RQ + P], qr[:, j, :], start=True, stop=True)
            mm(ps[:, 4, 0:T], front[0:ROPE, F_DK:F_DK + P], lat[0:ROPE, 10, :], start=True, stop=True)
            mm(ps[:, 4, T:2 * T], front[0:ROPE, F_RK:F_RK + P], lat[0:ROPE, 10, :], start=True, stop=True
               ).then_inc(rot_mm, 1)
            pe.wait_ge(uq_ev, 5)
            for k in range(KKV):
                m = first["ukv"] + k
                w_wait(m)
                for h in range(MH):
                    last = mm(in_set(SET_B, h), w_slot(m)[:, 0, h * 256:h * 256 + P], lat[:, KQ + k, :],
                              start=k == 0 and h % 2 == 0, stop=k == KKV - 1, skip_group_check=True)
            last.then_inc(k_mm, 1)

            def values(k):
                m = first["ukv"] + k
                wv = w_slot(m)[:, 0, :].rearrange("p (h c) -> p h c", c=256)
                for t in range(TT):
                    for n in range(2):
                        last = mm(ps[:, SET_A[2 * t + n], :], lat[:, KQ + k, t * P:(t + 1) * P],
                                  wv[:, 4 * n:4 * n + 4, P:256], start=k == 0, stop=k == KKV - 1)
                last.then_inc(w_used, 1)

            def scores(h):
                if h == 0:
                    pe.wait_ge(ukv_ev, 4)
                if h >= 3:
                    pe.wait_ge(s_add, h - 2)
                for o, q0, kn_ in ((0, 0, P), (P, P, T)):
                    dst = ps[:, S_BANKS[h % 3], o:o + kn_]
                    if h < MH:
                        b = ROPE * (h % 2)
                        mm(dst, qn[:, h, q0:q0 + P], kn[:, h, 0:kn_], start=True, stop=False)
                        last = mm(dst, qr[b:b + ROPE, h // 2, q0:q0 + P], krope[b:b + ROPE, 0:kn_], start=False, stop=True)
                    else:
                        last = mm(dst, mqk[:, h - MH, q0:q0 + P], mqk[:, h, 0:kn_], start=True, stop=True)
                last.then_inc(s_mm, 1)

            def weights_t(h):
                pe.wait_ge(s_norm, h + 1)
                if h == 0:
                    pe.wait_ge(ukv_ev, 8)
                if h >= 2:
                    pe.wait_ge(pt_ev, h - 1)
                for n in range(3):
                    last = nc.tensor.transpose(ps[:, PT_BANKS[h % 2], n * P:(n + 1) * P], sc[h % 3][:, n * P:(n + 1) * P], ident)
                last.then_inc(pt_mm, 1)

            def mix(h):
                pe.wait_ge(pt_ev, h + 1)
                if h >= 2:
                    pe.wait_ge(o_ev, h - 1)
                v = vv[:, :, h * P:(h + 1) * P] if h < MH else mv[:, :, (h - MH) * P:(h - MH + 1) * P]
                mm(ps[:, O_BANKS[h % 2], 0:T], v[:, 0, :], pt[:, h % 2, 0:T], start=True, stop=False, skip_group_check=True)
                mm(ps[:, O_BANKS[h % 2], P:T], v[:, 1, :], pt[:, h % 2, T:3 * P], start=False, stop=True,
                   skip_group_check=True).then_inc(o_mm, 1)

            def head_squares(h):
                g, k = h // MH, h % MH
                pe.wait_ge(sq_head, h + 1)
                last = mm(ps[:, 7, g * T:(g + 1) * T], ones, head_sq(h), start=k == 0, stop=k == MH - 1)
                if h == 2 * MH - 1:
                    last.then_inc(sq_mm, 1)

            pe.wait_ge(rope_ok, 1)
            pe.wait_ge(mod_ok, 3)
            values(0)
            scores(0)
            scores(1)
            for k in range(1, KKV):
                values(k)
            for h in range(2 * MH):
                if h + 2 < 2 * MH:
                    scores(h + 2)
                weights_t(h)
                if h:
                    mix(h - 1)
                if h == 1:
                    mod_sum(3)
                if h == 4:
                    pe.wait_ge(mod_ok, 4)
                if h >= 4:
                    head_squares(h - 4)
            mix(2 * MH - 1)
            for h in range(2 * MH - 4, 2 * MH):
                head_squares(h)
            pe.wait_ge(diag_ok, 1)
            pe.wait_ge(s_add, 16)
            pe.wait_ge(pt_ev, 16)
            pe.wait_ge(o_ev, 16)
            for k in range(KD):
                last = mm(ps[:, k // 4, (k % 4) * P:(k % 4 + 1) * P], ones, diag[:, k * P:(k + 1) * P],
                          start=True, stop=True)
            last.then_inc(gg_mm, 1)
            pe.wait_ge(gg_ev, 1)
            pe.wait_ge(o_ev, 16)
            pe.wait_ge(sq_aff, 2)
            for k in range(KD):
                m = first["out"] + k
                pe.wait_ge(w_split, nth[m] + 1)
                pe.wait_ge(act_split, KD // 2 + k + 1)
                weight_right(m, 0, range(8), k).then_inc(w_used, 1)
            pe.wait_ge(ld_sub, 32)
            pe.wait_ge(y_ssq, TT)
            pe.wait_ge(y_tmp, TT)
            for h in range(16):
                last = nc.tensor.transpose(ps[:, 4 + h // 4, (h % 4) * P:(h % 4 + 1) * P], subk[:, h, :], ident)
            last.then_inc(sub_mm, 1)
            mod_sum(4, 0)
            pe.wait_ge(mod_ok, 5)
            pe.wait_ge(xn2_ok, 1)
            pe.wait_ge(xn2b_ok, 1)
            for k in range(0, 8, 2):
                x_tiles(k, xn, k // 2, x2t_mm)
            pe.wait_ge(sub_ev, 1)
            for k in range(8, KD, 2):
                x_tiles(k, xn, k // 2, x2t_mm)
            h2_parts = (h2[:, 0, :, :], h2[:, 1, :, :])
            for cg in range(2):
                for k in range(KD):
                    m = first[f"pq{cg}"] + k // 2
                    if k % 2 == 0:
                        pe.wait_ge(w_split, nth[m] + 1)
                        if cg == 0:
                            pe.wait_ge(h2_split, k // 2 + 1)
                    for h in range(8):
                        if k == 0 and h % 2 == 0:
                            pe.wait_ge(x2t_ev, 8 * cg + h + 2)
                        last = weight_left(m, (k % 2) * 1024 + h * P, P, half(4 * cg, h), h2_parts, k,
                                           k == 0 and h % 2 == 0)
                    if k % 2:
                        last.then_inc(w_used, 1)
            pe.wait_ge(pq_ev, 4)
            mod_sum(5, 0)
            pe.wait_ge(mod_ok, 7)
            for t in range(TT):
                pe.wait_ge(pq_ev, 8)
                for h in range(16):
                    last = mm(ps[:, 4 * t + h // 4, (h % 4) * P:(h % 4 + 1) * P], mqk[:, h, t * P:(t + 1) * P],
                              subt[:, h, :], start=True, stop=True)
                last.then_inc(ks_mm, 1)
            pe.wait_ge(ks_ev, 1)

            pe.wait_ge(zero_ok, 1)

            def u_transpose(q, full, split):
                pe.wait_ge(e_full[q], full)
                for hf in range(2):
                    if split is not None:
                        pe.wait_ge(u_split, split + hf)
                    for k in range(8):
                        last = nc.tensor.transpose(ps[:, 2 * hf + k // 4, (k % 4) * P:(k % 4 + 1) * P],
                                                   ring[:, q, (8 * hf + k) * P:(8 * hf + k + 1) * P], ident)
                    last.then_inc(u_tr, 1)

            def u_scores(b, split, gelu, beside=()):
                pe.wait_ge(u_split, split)
                if gelu is not None:
                    pe.wait_ge(u_gelu, gelu)
                dst = ps[:, 4 + b, 0:T]
                for k in range(KD):
                    if k % 5 == 0 and k // 5 < len(beside):
                        m = beside[k // 5]
                        place(m % 2, m + 1, m - 1 if m >= 2 else None)
                    hi, lo = uv[:, b, 0, k * P:(k + 1) * P], uv[:, b, 1, k * P:(k + 1) * P]
                    mm(dst, hi, h2[:, 0, k, :], start=k == 0, stop=False)
                    mm(dst, hi, h2[:, 1, k, :], start=False, stop=False)
                    last = mm(dst, lo, h2[:, 0, k, :], start=False, stop=k == KD - 1)
                last.then_inc(u_mm, 1)

            def place(b, ok, ev):
                pe.wait_ge(hot_ok, ok)
                pe.wait_ge(hot_j_ok, ok)
                if ev is not None:
                    pe.wait_ge(g_ev, ev)
                for t in range(TB):
                    for part in range(3):
                        last = mm(ps[:, 6 + b, t * GJ:(t + 1) * GJ], hot_i[:, b, t, :], hot_j[:, b, part, t, :],
                                  start=part == 0, stop=part == 2)
                last.then_inc(g_mm, 1)

            def v_mix(b, ok, gelu=None, half_done=False):
                pe.wait_ge(v_split, ok)
                for t in range(TT):
                    if gelu is not None:
                        if t:
                            pe.wait_ge(u_gelu, gelu)
                        for n in range(4):
                            mm(ps[:, 4 * t + n, 0:P], zero[:, :], zero[:, :], start=True, stop=False,
                               skip_group_check=True)
                    hi, lo = am[:, b, 0, t * P:(t + 1) * P], am[:, b, 1, t * P:(t + 1) * P]
                    for a, part in ((hi, 0), (hi, 1), (lo, 0)):
                        for n in range(4):
                            last = mm(ps[:, 4 * t + n, :], a, uv[:, b, part, n * 512:(n + 1) * 512],
                                      start=False, stop=False, skip_group_check=True)
                    if half_done and t == 0:
                        last.then_inc(v_half, 1)
                last.then_inc(v_mm, 1)

            for g in range(GROUPS):
                n0 = g * GJ
                f0 = 16 * (2 * n0 // RING)
                if g:
                    pe.wait_ge(y_ev, 8 * g - 4)
                def u_step(q, it):
                    u_transpose(q, it * 16 + (f0 + 16), it * (2 * RING) + (2 * (n0 + q - 1) + 1))
                    u_scores((q - 1) % 2, it * (2 * RING) + 2 * (n0 + q), it * RING + (n0 + q - 2))

                for n in range(RING):
                    u_transpose(n % RING, f0 + 16, 2 * (n0 + n - 1) + 1 if n0 + n > 0 else None)
                    if n == 1:
                        if g:
                            pe.wait_ge(y_ev, 8 * g)
                        else:
                            pe.wait_ge(ks_ev, TT)
                    if n:
                        u_scores((n - 1) % 2, 2 * (n0 + n), n0 + n - 2 if n0 + n > 2 else None)
                        if g:
                            place((n - 1) % 2, n0 + n, n0 + n - 2)
                if g == 0:
                    with pe.Fori(1, ROUTE_STEPS // RING) as it:
                        for q in range(RING):
                            u_step(q, it)
                    for t in range(TT):
                        pe.wait_ge(r_ok, t + 1)
                        for s in range(3):
                            last = nc.tensor.transpose(ps[:, 6 + s // 2, (s % 2) * T + t * P:(s % 2) * T + (t + 1) * P],
                                                       rout[:, t, s, :], ident)
                    last.then_inc(rt_mm, 1)
                    pe.wait_ge(rt_ev, 1)
                    for n in range(ROUTE_STEPS, GJ):
                        u_transpose(n % RING, 16 * (n // RING + 1), 2 * n - 1)
                        u_scores((n - 1) % 2, 2 * n, n - 2, batches.get(n - 1, ()))
                    u_scores(1, 2 * GJ, GJ - 2, batches[GJ - 1])
                else:
                    with pe.Fori(1, GJ // RING) as it:
                        for q in range(RING):
                            u_step(q, it)
                            place((q - 1) % 2, it * RING + (n0 + q), it * RING + (n0 + q - 2))
                    place(1, n0 + GJ, n0 + GJ - 2)
                    u_scores(1, 2 * (n0 + GJ), n0 + GJ - 2)

                pe.wait_ge(g_ev, n0 + GJ)
                for q in range(RING):
                    v_mix(q % 2, n0 + q + 1, n0 + GJ if q == 0 else None)
                with pe.Fori(1, GJ // RING - 1) as it:
                    for q in range(RING):
                        v_mix(q % 2, it * RING + (n0 + q + 1))
                for q in range(RING):
                    v_mix(q % 2, n0 + GJ - RING + q + 1, half_done=q == RING - 1)
            pe.wait_ge(y_ev, 8 * GROUPS - 4)
            pe.wait_ge(f_diag, 1)
            for k in range(KD):
                last = mm(ps[:, k // 4, (k % 4) * P:(k % 4 + 1) * P], ones, gs_flat[:, k * P:(k + 1) * P],
                          start=True, stop=True)
            last.then_inc(f_gg, 1)

        @block.scalar
        def _(act):
            fn = nc.scalar.activation
            chain = [0]

            def link(ins):
                chain[0] += 1
                ins.then_inc(act_chain, 1)
                act.wait_ge(act_chain, chain[0])

            act.wait_ge(rows_ev, 1)
            fn(cs, col_c, ACT.Exp, scale=-1.0).then_inc(c_exp, 1)
            act.wait_ge(ld_x, 16)
            for t in range(TT):
                fn(xn[:, t, :], xs[:, t, :], ACT.Square, accum_out=ssq[0][:, t:t + 1]).then_inc(x_ssq, 1)
            act.wait_ge(x_rms, 1)
            fn(rst[0], ssq[0], ACT.Sqrt).then_inc(x_sqrt, 1)
            act.wait_ge(x_rstd, 1)
            for t in range(TT):
                fn(xn[:, t, :], xs[:, t, :], ACT.Copy, scale=rst[0][:, t:t + 1]).then_inc(xn_ok, 1)
            def w_high(m):
                act.wait_ge(w_full[m % WRING], 16 * w_loads(m))
                if nth[m] >= 2:
                    act.wait_ge(w_used, chunks[nth[m] - 2] + 1)
                n = width(m)
                fn(whi[nth[m] % 2][:, 0:n], wring[:, m % WRING, 0:n], ACT.Copy).then_inc(w_hi, 1)

            w_high(0)
            w_high(1)
            act.wait_ge(mod_ok, 2)
            for k in X_ORDER:
                if k % 2 == 0:
                    act.wait_ge(xt_mm, k // 2 + 1)
                bank = k // 2 if k < 14 else 0
                fn(act_t[:, k, :], ps[:, bank, (k % 2) * T:(k % 2 + 1) * T], ACT.Identity,
                   bias=mod[:, k:k + 1], scale=sc1[:, k:k + 1]).then_inc(xt_ev, 1)
            for m in range(2, end["mv"]):
                w_high(m)
                if m == end["lat"]:
                    act.wait_ge(w_used, end["lat"])
                    for b in range(4):
                        fn(lat[:, 2 * b:2 * b + 2, :].rearrange("p a t -> p (a t)"), ps[:, LAT_BANKS[b], :], ACT.Copy
                           ).then_inc(in_ev, 1)
                if m == end["lat"] + 1:
                    fn(lat[:, 8:10, :].rearrange("p a t -> p (a t)"), ps[:, LAT_BANKS[4], :], ACT.Copy).then_inc(in_ev, 1)
                    fn(lat[0:ROPE, 10, :], ps[0:ROPE, LAT_BANKS[5], 0:T], ACT.Copy).then_inc(in_ev, 1)
                if m == end["lat"] + 2:
                    act.wait_ge(in_ev, 6)
                    fn(sq_lat, lat[:, 0:10, :], ACT.Square).then_inc(sq_ok, 1)
                if m == end["lat"] + 4:
                    act.wait_ge(sq_aff, 1)
                    fn(rb, rb, ACT.Sqrt).then_inc(sq_root, 1)
                if m == end["mq"] + 1:
                    act.wait_ge(w_used, end["mq"])
                    for b in range(4):
                        fn(mqk[:, 2 * b:2 * b + 2, :].rearrange("p a t -> p (a t)"), ps[:, SET_A[b], :],
                           ACT.Copy, scale=HD ** -0.5).then_inc(in_ev, 1)
                if m == end["mk"] + 1:
                    act.wait_ge(w_used, end["mk"])
                    for b in range(4):
                        fn(mqk[:, MH + 2 * b:MH + 2 * b + 2, :].rearrange("p a t -> p (a t)"), ps[:, SET_B[b], :],
                           ACT.Copy).then_inc(in_ev, 1)
            act.wait_ge(w_used, end["mv"])
            for b in range(4):
                fn(mv[:, b // 2, (b % 2) * 512:(b % 2 + 1) * 512], ps[:, SET_A[b], :], ACT.Copy).then_inc(in_ev, 1)
            act.wait_ge(w_used, end["uq"])
            s_qk = (HD + ROPE) ** -0.5
            fn(qr, ps[:, 0:2, :].rearrange("p a (b t) -> p (a b) t", b=2), ACT.Copy, scale=s_qk).then_inc(uq_ev, 1)
            for b in range(4):
                fn(qn[:, 2 * b:2 * b + 2, :].rearrange("p a t -> p (a t)"), ps[:, SET_B[b], :], ACT.Copy, scale=s_qk
                   ).then_inc(uq_ev, 1)
            act.wait_ge(k_mm, 1)
            for b in range(4):
                fn(kn[:, 2 * b:2 * b + 2, :].rearrange("p a t -> p (a t)"), ps[:, SET_B[b], :], ACT.Copy
                   ).then_inc(ukv_ev, 1)

            def exp(h):
                act.wait_ge(s_max, h + 1)
                b = h % 2
                s = sc[h % 3]
                fn(s[:, 0:P], s[:, 0:P], ACT.Exp, bias=nmax[:, b, 0:1], accum_out=esum[:, b, 0:1])
                fn(s[:, P:3 * P], s[:, P:3 * P], ACT.Exp, bias=nmax[:, b, 1:2],
                   accum_out=esum[:, b, 1:2]).then_inc(s_exp, 1)

            def weights_out(h):
                act.wait_ge(pt_mm, h + 1)
                if h >= 2:
                    act.wait_ge(o_mm, h - 1)
                fn(pt[:, h % 2, :], ps[:, PT_BANKS[h % 2], 0:3 * P], ACT.Copy).then_inc(pt_ev, 1)

            def mixed_out(h):
                act.wait_ge(o_mm, h + 1)
                fn(act_t[:, h, :], ps[:, O_BANKS[h % 2], 0:T], ACT.Copy).then_inc(o_ev, 1)

            for h in range(2 * MH):
                exp(h)
                if h == 1:
                    act.wait_ge(rope_ok, 1)
                    act.wait_ge(w_used, end["ukv"])
                    for b in range(4):
                        fn(vv[:, b // 2, (b % 2) * 512:(b % 2 + 1) * 512], ps[:, SET_A[b], :], ACT.Copy
                           ).then_inc(ukv_ev, 1)
                if h == 8:
                    w_high(first["out"])
                if h >= 1:
                    weights_out(h - 1)
                if h >= 2:
                    mixed_out(h - 2)
            weights_out(15)
            mixed_out(14)
            mixed_out(15)
            act.wait_ge(pt_mm, 16)
            w_high(first["out"] + 1)
            act.wait_ge(sq_aff, 2)
            fn(rb, rb, ACT.Sqrt).then_inc(sq_root, 1)
            act.wait_ge(gg_mm, 1)
            fn(gg1_all, ps[:, 0:4, :].rearrange("p a n -> p (a n)"), ACT.Copy).then_inc(gg_ev, 1)
            for m in range(first["out"] + 2, first["pq0"] + 1):
                w_high(m)
            act.wait_ge(w_used, end["out"])
            for t in range(TT):
                if t == 1:
                    act.wait_ge(y_tmp, 1)
                fn(xn[:, t, :], ps[:, 4 * t:4 * t + 4, :].rearrange("p a n -> p (a n)"), ACT.Square,
                   accum_out=ssq[1][:, t:t + 1]).then_inc(y_ssq, 1)
            act.wait_ge(y_aff, 1)
            fn(rst[1], ssq[1], ACT.Sqrt).then_inc(y_root, 1)
            w_high(first["pq0"] + 1)
            for t in range(TT):
                act.wait_ge(x1_ok, t + 1)
                fn(xn[:, t, :], xs[:, t, :], ACT.Square, accum_out=ssq[2][:, t:t + 1]).then_inc(n_ssq, 1)
            act.wait_ge(n_aff, 1)
            fn(rst[2], ssq[2], ACT.Sqrt).then_inc(n_root, 1)
            act.wait_ge(n_rstd, 1)
            fn(xn[:, 0, :], xs[:, 0, :], ACT.Copy, scale=rst[2][:, 0:1]).then_inc(xn2_ok, 1)
            act.wait_ge(mod_ok, 6)
            for k in range(KD):
                if k % 2 == 0:
                    act.wait_ge(x2t_mm, k // 2 + 1)
                fn(act_t[:, k, :], ps[:, k // 2, (k % 2) * T:(k % 2 + 1) * T], ACT.Identity,
                   bias=mod[:, 48 + k:49 + k], scale=sc2[:, k:k + 1]).then_inc(x2t_ev, 1)
            for cg in range(2):
                for m in range(first["pq0"] + 2, end["pq0"] + 2) if cg == 0 else range(end["pq0"] + 2, end["pq1"]):
                    w_high(m)
                act.wait_ge(w_used, end[f"pq{cg}"])
                for b in range(4):
                    n = 8 * cg + 2 * b
                    fn(mqk[:, n:n + 2, :].rearrange("p a t -> p (a t)"), ps[:, 4 * cg + b, :], ACT.Copy).then_inc(pq_ev, 1)
            for t in range(TT):
                act.wait_ge(ks_mm, t + 1)
                fn(rs[t][:, :], ps[:, 4 * t:4 * t + 4, :].rearrange("p a n -> p (a n)"), ACT.Copy).then_inc(ks_ev, 1)
            act.wait_ge(x1_st, 16)

            def u_high(q, tr, free):
                for hf in range(2):
                    act.wait_ge(u_tr, tr + hf)
                    if free is not None and hf == 0:
                        act.wait_ge(u_mm, free)
                    fn(uv[:, q % 2, 0, hf * 1024:(hf + 1) * 1024],
                       ps[:, 2 * hf:2 * hf + 2, :].rearrange("p a n -> p (a n)"), ACT.Copy).then_inc(u_hi, 1)

            def gelu(b, done, j):
                act.wait_ge(u_mm, done)
                fn(column(gs, j), ps[:, 4 + b, 0:T], ACT.Gelu).then_inc(u_gelu, 1)

            def placed(b, done, t0):
                act.wait_ge(g_mm, done)
                fn(pw[:, :, t0].rearrange("p j t -> p t j"),
                   ps[:, 6 + b, 0:TB * GJ].rearrange("p (t j) -> p t j", t=TB), ACT.Copy).then_inc(g_ev, 1)

            def v_high_rows(q, full, free=None):
                act.wait_ge(e_full[q], full)
                if free is not None:
                    act.wait_ge(v_mm, free)
                fn(uv[:, q % 2, 0, :], ring[:, q, :], ACT.Copy).then_inc(v_hi, 1)

            def v_high_weights(q, prod):
                act.wait_ge(v_prod, prod)
                fn(am[:, q % 2, 0, :], wj[:, q % 2, :], ACT.Copy).then_inc(v_whi, 1)

            for g in range(GROUPS):
                n0 = g * GJ
                f0 = 16 * ((2 * n0 + GJ) // RING)
                if g:
                    act.wait_ge(v_prod, n0)

                def step(q, it):
                    u_high(q, it * (2 * RING) + (2 * (n0 + q) + 1), it * RING + (n0 + q - 1))
                    gelu((q - 1) % 2, it * RING + (n0 + q), it * RING + (q - 1))

                for n in range(RING):
                    if g and n < 2:
                        act.wait_ge(v_mm, n0 - 1 + n)
                    u_high(n, 2 * (n0 + n) + 1, n0 + n - 1 if n0 + n > 1 else None)
                    if n:
                        gelu((n - 1) % 2, n0 + n, n - 1)
                        if g:
                            placed((n - 1) % 2, n0 + n, bass.ds((n - 1) * TB, TB))
                if g == 0:
                    for n in range(RING, ROUTE_STEPS):
                        step(n % RING, n // RING)
                        for t in range(TT):
                            if n == (7, 17)[t]:
                                act.wait_ge(r_max, t + 1)
                                fn(pick_v, pick_v, ACT.Exp).then_inc(r_exp, 1)
                    act.wait_ge(rt_mm, 1)
                    fn(ridx[:, :, :], ps[:, 6, :].rearrange("p (s t) -> p s t", s=2), ACT.Copy)
                    fn(w_rest[:, 0, :], ps[:, 7, 0:T], ACT.Copy).then_inc(rt_ev, 1)
                    for n in range(ROUTE_STEPS, GJ):
                        u_high(n % RING, 2 * n + 1, n - 1)
                        for m in batches.get(n - 1, ()):
                            placed(m % 2, m + 1, bass.ds(m * TB, TB))
                        gelu((n - 1) % 2, n, n - 1)
                else:
                    with act.Fori(1, GJ // RING) as it:
                        for q in range(RING):
                            step(q, it)
                            placed((q - 1) % 2, it * RING + (n0 + q), bass.ds(it * (RING * TB) + (q - 1) * TB, TB))
                act.wait_ge(u_mm, n0 + GJ - 1)
                v_high_rows(0, f0 + 16)
                for m in batches[GJ - 1] if g == 0 else (GJ - 1,):
                    placed(m % 2, n0 + m + 1, bass.ds(m * TB, TB))
                v_high_weights(0, n0 + 1)
                gelu(1, n0 + GJ, GJ - 1)
                for q in range(1, RING):
                    v_high_rows(q, f0 + 16, n0 + q - 1 if q > 1 else None)
                    v_high_weights(q, n0 + q + 1)
                with act.Fori(1, GJ // RING) as it:
                    for q in range(RING):
                        v_high_rows(q, it * 16 + (f0 + 16), it * RING + (n0 + q - 1))
                        v_high_weights(q, it * RING + (n0 + q + 1))
            for t in range(TT):
                act.wait_ge(y_ev, 8 * GROUPS - 4 + 4 * t)
                fn(gs_flat[:, (t + 1) * D:(t + 2) * D], yacc[t][:, :], ACT.Square, accum_out=ssq[3][:, t:t + 1]).then_inc(f_ssq, 1)
            act.wait_ge(f_aff, 1)
            fn(rst[3], ssq[3], ACT.Sqrt).then_inc(f_root, 1)

        @block.vector
        def _(dve):
            tt, ts, stt = nc.vector.tensor_tensor, nc.vector.tensor_scalar, nc.vector.scalar_tensor_tensor
            chain = [0]

            def link(ins):
                chain[0] += 1
                ins.then_inc(dve_chain, 1)
                dve.wait_ge(dve_chain, chain[0])

            def rms(src, n):
                return ts(src, src, 1.0 / n, EPS, ALU.mult, ALU.add)

            nc.vector.memset(zero[:, :], 0.0).then_inc(zero_ok, 1)
            dve.wait_ge(rows_t, 1)
            nc.vector.tensor_copy(col_a, ps[:, 7, 0:P])
            nc.vector.tensor_copy(col_b, ps[:, 6, 0:74]).then_inc(rows_ev, 1)
            dve.wait_ge(c_exp, 1)
            link(ts(cs, cs, 1.0, None, ALU.add))
            link(nc.vector.reciprocal(cs, cs))
            link(tt(cs, cs, col_c, ALU.mult))

            def ada(s, q, full, prev, k, start):
                dve.wait_ge(ada_full[q], full)
                if prev is not None:
                    dve.wait_ge(ada_used, prev)
                if start:
                    ins = ts(acc[:, s % 2, :], ring[:, q, :], cs[:, k:k + 1], None, ALU.mult)
                else:
                    scal = cs[:, k:k + 1] if isinstance(k, int) else cs[:, bass.ds(k, 1)]
                    ins = stt(acc[:, s % 2, :], ring[:, q, :], scal, acc[:, s % 2, :], ALU.mult, ALU.add)
                ins.then_inc(ada_used, 1)

            def section(s):
                m0 = s * KD
                for q in range(RING):
                    ada(s, q, 16 * (m0 // RING + 1), m0 + q if q else None, q, q == 0)
                with dve.Fori(1, KD // RING) as it:
                    for q in range(RING):
                        ada(s, q, it * 16 + 16 * (m0 // RING + 1), it * RING + (m0 + q), it * RING + q, False)

            def ada_step(n):
                s, k = n // KD, n % KD
                if k == 0:
                    dve.wait_ge(gg_mm if s == 5 else mod_mm, 1 if s == 5 else s - 1)
                ada(s, n % RING, 16 * (n // RING + 1), n, k, k == 0)

            def w_low(m):
                n = width(m)
                dve.wait_ge(w_hi, nth[m] + 1)
                tt(wlo[:, m % WRING, 0:n], wring[:, m % WRING, 0:n], whi[nth[m] % 2][:, 0:n].bitcast(F32),
                   ALU.subtract).then_inc(w_split, 1)

            def act_parts(k, n, hi, lo, done):
                link(nc.vector.tensor_copy(hi[:, k:k + n, :], act_t[:, k:k + n, :]))
                tt(lo[:, k:k + n, :], act_t[:, k:k + n, :], hi[:, k:k + n, :].bitcast(F32), ALU.subtract).then_inc(done, 1)

            def mod_out(s):
                dve.wait_ge(mod_mm, max(s + 1, 2))
                bank = (7, 7, 2, 7, 0, 0)[s]
                tt(mod[:, 16 * s:16 * s + 16], ps[:, bank, P + 16 * s:P + 16 * s + 16], col_a[:, 16 * s:16 * s + 16],
                   ALU.add).then_inc(mod_ok if s != 1 else dve_chain, 1)
                chain[0] += s == 1

            section(0)
            dve.wait_ge(x_ssq, TT)
            rms(ssq[0], D).then_inc(x_rms, 1)
            dve.wait_ge(x_sqrt, 1)
            nc.vector.reciprocal(rst[0], rst[0]).then_inc(x_rstd, 1)
            section(1)
            mod_out(0)
            mod_out(1)
            dve.wait_ge(dve_chain, chain[0])
            stt(sc1, mod[:, 16:32], 1.0, g_pm, ALU.add, ALU.mult).then_inc(mod_ok, 1)
            w_low(0)
            w_low(1)
            dve.wait_ge(xt_mm, KD // 2)
            for k in range(0, KD, 2):
                if k == 8:
                    w_low(2)
                dve.wait_ge(xt_ev, k + 4 if 0 < k < 14 else KD if k else 2)
                act_parts(k, 2, act_hi, act_lo, act_split)
            n = 2 * KD
            for m in range(3, end["mv"]):
                w_low(m)
                if m == end["lat"] + 3:
                    dve.wait_ge(sq_mm, 1)
                    link(ts(rb[:, 0, :], ps[:, 3, 0:T], 1.0 / QR, EPS, ALU.mult, ALU.add))
                    ts(rb[:, 1, :], ps[:, 3, T:2 * T], 1.0 / KVR, EPS, ALU.mult, ALU.add).then_inc(sq_aff, 1)
                elif m == end["lat"] + 5:
                    dve.wait_ge(sq_root, 1)
                    link(nc.vector.reciprocal(rb, rb))
                    for k in range(10):
                        stt(lat[:, k, :], lat[:, k, :], g_lat[:, k:k + 1], rb[:, int(k >= KQ), :], ALU.mult, ALU.mult
                            ).then_inc(lat_n, 1)
                elif m % 4 != 3 if m > end["lat"] else m % 2:
                    ada_step(n)
                    n += 1
            for m in range(n, 4 * KD):
                ada_step(m)
            mod_out(2)
            dve.wait_ge(mod_ok, 3)
            link(tt(gg1, mod[:, 32:48], g_om, ALU.mult))
            dve.wait_ge(rot_mm, 1)
            dve.wait_ge(uq_ev, 1)
            cos4, sin4 = (v.unsqueeze(1).to_broadcast([P, MH // 2, T]) for v in (cos, sin))
            tt(rt, ps[:, 0:2, :].rearrange("p a (b t) -> p (a b) t", b=2), sin4, ALU.mult)
            tt(krope, ps[:, 4, 0:T], cos, ALU.mult)
            tt(krt, ps[:, 4, T:2 * T], sin, ALU.mult)
            link(tt(qr, qr, cos4, ALU.mult))
            tt(krope, krope, krt, ALU.add)
            tt(qr, qr, rt, ALU.add).then_inc(rope_ok, 1)
            for m in range(4 * KD, ADA_EARLY):
                ada_step(m)

            def biased(h):
                b = h % 2
                dve.wait_ge(s_mm, h + 1)
                if h >= 3:
                    dve.wait_ge(pt_mm, h - 2)
                off, slope = (F_MASK, 1.0) if h < MH else (F_DIST, 2.0 ** (-(h - MH + 1.0)))
                s = sc[h % 3]
                stt(s, front[:, off:off + 384], slope, ps[:, S_BANKS[h % 3], 0:384], ALU.mult, ALU.add).then_inc(s_add, 1)
                dve.wait_ge(s_add, h + 1)
                nc.vector.reduce_max(smax[:, b, 0:1], s[:, 0:P], AX)
                link(nc.vector.reduce_max(smax[:, b, 1:2], s[:, P:3 * P], AX))
                ts(nmax[:, b, :], smax[:, b, :], -1.0, None, ALU.mult).then_inc(s_max, 1)

            def normed(h):
                b = h % 2
                dve.wait_ge(s_exp, h + 1)
                link(nc.vector.reciprocal(erec[:, b, :], esum[:, b, :]))
                s = sc[h % 3]
                ts(s[:, 0:P], s[:, 0:P], erec[:, b, 0:1], None, ALU.mult)
                ts(s[:, P:3 * P], s[:, P:3 * P], erec[:, b, 1:2], None, ALU.mult).then_inc(s_norm, 1)

            biased(0)
            for h in range(2 * MH):
                if h + 1 < 2 * MH:
                    biased(h + 1)
                normed(h)
                if h == 2:
                    mod_out(3)
                if h == 9:
                    w_low(first["out"])
                if 3 <= h < 7:
                    for k in range(4 * (h - 3), 4 * (h - 2)):
                        ins = ts(diag[:, k * P:(k + 1) * P], ident, gg1[:, k:k + 1], None, ALU.mult)
                    if h == 6:
                        ins.then_inc(diag_ok, 1)
            dve.wait_ge(sq_mm, 2)
            for g in range(2):
                ins = ts(rb[:, g, :], ps[:, 7, g * T:(g + 1) * T], 1.0 / (MH * HD), EPS, ALU.mult, ALU.add)
            ins.then_inc(sq_aff, 1)
            dve.wait_ge(sq_root, 2)
            link(nc.vector.reciprocal(rb, rb))

            def o_parts(k):
                link(stt(act_t[:, k, :], act_t[:, k, :], g_att[:, k:k + 1], rb[:, k // MH, :], ALU.mult, ALU.mult))
                act_parts(k, 1, act_hi, act_lo, act_split)

            n = ADA_EARLY
            for k in range(2):
                o_parts(k)
            for k in range(KD):
                w_low(first["out"] + k + 1)
                if k % 4 != 3:
                    ada_step(n)
                    n += 1
                if k + 2 < KD:
                    o_parts(k + 2)
            dve.wait_ge(gg_ev, 1)
            dve.wait_ge(w_used, end["out"])
            for t in (1, 0):
                if t == 0:
                    dve.wait_ge(y_ssq, 1)
                tt(x1_tmp[:, t, :], ps[:, 4 * t:4 * t + 4, :].rearrange("p a n -> p (a n)"), gg1_all, ALU.mult
                   ).then_inc(y_tmp, 1)
            dve.wait_ge(y_ssq, TT)
            rms(ssq[1], D).then_inc(y_aff, 1)
            dve.wait_ge(y_root, 1)
            link(nc.vector.reciprocal(rst[1], rst[1]))
            dve.wait_ge(y_tmp, TT)
            for t in range(TT):
                stt(xs[:, t, :], x1_tmp[:, t, :], rst[1][:, t:t + 1], xs[:, t, :], ALU.mult, ALU.add).then_inc(x1_ok, 1)
            dve.wait_ge(sub_mm, 1)
            nc.vector.tensor_copy(subt.rearrange("p h n -> p (h n)"),
                                  ps[:, 4:8, :].rearrange("p a n -> p (a n)")).then_inc(sub_ev, 1)
            dve.wait_ge(n_ssq, TT)
            rms(ssq[2], D).then_inc(n_aff, 1)
            dve.wait_ge(n_root, 1)
            nc.vector.reciprocal(rst[2], rst[2]).then_inc(n_rstd, 1)
            dve.wait_ge(n_rstd, 1)
            ts(xn[:, 1, :], xs[:, 1, :], rst[2][:, 1:2], None, ALU.mult).then_inc(xn2b_ok, 1)
            mod_out(4)
            dve.wait_ge(mod_ok, 5)
            stt(sc2, mod[:, 64:80], 1.0, g_pf, ALU.add, ALU.mult).then_inc(mod_ok, 1)
            w_low(first["pq0"] + 1)
            for k in range(0, KD, 2):
                if k == 8:
                    w_low(first["pq0"] + 2)
                dve.wait_ge(x2t_ev, k + 2)
                dve.wait_ge(x2t_mm, min(k + 2, KD // 2))
                act_parts(k, 2, h2[:, 0, :, :], h2[:, 1, :, :], h2_split)
            for m in range(first["pq0"] + 3, end["pq1"]):
                w_low(m)
                if n < 6 * KD:
                    ada_step(n)
                    n += 1
            for m in range(n, 6 * KD):
                ada_step(m)
            mod_out(5)
            dve.wait_ge(mod_ok, 7)
            link(tt(gg2, mod[:, 80:96], g_of, ALU.mult))

            def top16(n, vals, out_v, out_i):
                for h in range(n):
                    ins = nc.vector.max(out_v[:, h, 0:8], vals(h))
                link(ins)
                yield
                for h in range(n):
                    ins = nc.vector.max_index(out_i[:, h, 0:8], out_v[:, h, 0:8], vals(h))
                link(ins)
                yield
                for h in range(n):
                    ins = nc.vector.match_replace(vals(h), out_v[:, h, 0:8], vals(h), -3.4e38)
                link(ins)
                yield
                for h in range(n):
                    ins = nc.vector.max(out_v[:, h, 8:16], vals(h))
                link(ins)
                yield
                for h in range(n):
                    ins = nc.vector.max_index(out_i[:, h, 8:16], out_v[:, h, 8:16], vals(h))
                link(ins)
                yield

            cand4 = cand[:, :].rearrange("p (h a b) -> p h a b", h=PH, a=PK)
            full = [P, PH, PK, PK]
            heads = [P, PH, PK]

            def routing():
                dve.wait_ge(ks_mm, TT)
                for t in range(TT):
                    dve.wait_ge(ks_ev, t + 1)
                    yield from top16(16, lambda h: rs[t][:, h * NK:(h + 1) * NK], top_v, top_i)
                    nc.vector.tensor_copy(top_f, top_i)
                    tv = top_v.rearrange("p (h s) k -> p h s k", s=2)
                    tf = top_f.rearrange("p (h s) k -> p h s k", s=2)
                    link(tt(cand4, tv[:, :, 0, :].unsqueeze(3).to_broadcast(full),
                            tv[:, :, 1, :].unsqueeze(2).to_broadcast(full), ALU.add))
                    yield from top16(PH, lambda h: cand[:, h * 256:(h + 1) * 256], pick_v, pick_s)
                    link(nc.vector.tensor_copy(rsum[:, 0:8].unsqueeze(2), pick_v[:, :, 0:1]))
                    tt(pick_v, pick_v, rsum[:, 0:8].unsqueeze(2).to_broadcast(heads), ALU.subtract).then_inc(r_max, 1)
                    ts(slot_u[:, 0], pick_s, 4, None, ALU.logical_shift_right)
                    link(ts(slot_u[:, 1], pick_s, 15, None, ALU.bitwise_and))
                    link(nc.vector.tensor_copy(slot_f, slot_u))
                    for s in range(2):
                        link(tt(cand4, slot_f[:, s].unsqueeze(3).to_broadcast(full),
                                iota[:, 0:PK].unsqueeze(1).unsqueeze(1).to_broadcast(full), ALU.is_equal))
                        yield
                        link(tt(cand4, cand4, tf[:, :, s, :].unsqueeze(2).to_broadcast(full), ALU.mult))
                        yield
                        link(nc.vector.reduce_sum(rout[:, t, s, :].rearrange("p (h k) -> p h k", h=PH), cand4, AX))
                        yield
                    dve.wait_ge(r_exp, t + 1)
                    link(nc.vector.reduce_sum(rsum[:, 0:8], pick_v, AX))
                    link(nc.vector.reciprocal(rsum[:, 8:16], rsum[:, 0:8]))
                    tt(rout[:, t, 2, :].rearrange("p (h k) -> p h k", h=PH), pick_v,
                       rsum[:, 8:16].unsqueeze(2).to_broadcast(heads), ALU.mult).then_inc(r_ok, 1)
                    dve.wait_ge(r_ok, t + 1)
                    yield

            def u_low(b, hi):
                for hf in range(2):
                    dve.wait_ge(u_hi, hi + hf)
                    tt(uv[:, b, 1, hf * 1024:(hf + 1) * 1024], ps[:, 2 * hf:2 * hf + 2, :].rearrange("p a n -> p (a n)"),
                       uv[:, b, 0, hf * 1024:(hf + 1) * 1024].bitcast(F32), ALU.subtract).then_inc(u_split, 1)

            def hots(b, j0, t0, used):
                if used is not None:
                    dve.wait_ge(g_mm, used)
                shape = [P, TB, GJ]
                tt(hot_e[:, b], iota[:, j0:j0 + GJ].unsqueeze(1).to_broadcast(shape),
                   ridx[:, 1, t0].unsqueeze(2).to_broadcast(shape), ALU.is_equal).then_inc(hot_eq, 1)
                tt(hot_i[:, b], iota.unsqueeze(1).to_broadcast([P, TB, NK]),
                   ridx[:, 0, t0].unsqueeze(2).to_broadcast([P, TB, NK]), ALU.is_equal).then_inc(hot_ok, 1)

            def product(b, j, free):
                if free is not None:
                    dve.wait_ge(v_split, free)
                tt(wj[:, b, :], column(gs, j), column(pw, j), ALU.mult).then_inc(v_prod, 1)

            def v_low_rows(q, hi):
                dve.wait_ge(v_hi, hi)
                tt(uv[:, q % 2, 1, :], ring[:, q, :], uv[:, q % 2, 0, :].bitcast(F32), ALU.subtract)

            def v_low_weights(q, hi):
                dve.wait_ge(v_whi, hi)
                tt(am[:, q % 2, 1, :], wj[:, q % 2, :], am[:, q % 2, 0, :].bitcast(F32), ALU.subtract).then_inc(v_split, 1)

            for g in range(GROUPS):
                n0 = g * GJ
                if g == 0:
                    route = routing()
                    for n in range(ROUTE_STEPS):
                        u_low(n % 2, 2 * n + 1)
                        for _ in range(1 if n % 3 == 2 else 2):
                            next(route, None)
                    assert next(route, None) is None
                    for n in range(ROUTE_STEPS, GJ):
                        u_low(n % 2, 2 * n + 1)
                        if n == ROUTE_STEPS:
                            dve.wait_ge(rt_ev, 1)
                            for part in range(3):
                                link(nc.vector.tensor_copy(w_part[:, part, :], w_rest[:, part, :]))
                                if part < 2:
                                    link(tt(w_rest[:, part + 1, :], w_rest[:, part, :], w_part[:, part, :],
                                            ALU.subtract))
                        for m in batches[n]:
                            hots(m % 2, 0, bass.ds(m * TB, TB), m - 1 if m >= 2 else None)
                else:
                    for n in range(RING):
                        u_low(n % 2, 2 * (n0 + n) + 1)
                        hots(n % 2, n0, bass.ds(n * TB, TB), n0 + n - 1)
                    with dve.Fori(1, GJ // RING) as it:
                        for q in range(RING):
                            u_low(q % 2, it * (2 * RING) + (2 * (n0 + q) + 1))
                            hots(q % 2, n0, bass.ds(it * (RING * TB) + q * TB, TB), it * RING + (n0 + q - 1))
                v_low_rows(0, n0 + 1)
                dve.wait_ge(g_ev, n0 + GJ)
                dve.wait_ge(u_gelu, n0 + 1)
                product(0, 0, None)
                v_low_weights(0, n0 + 1)
                dve.wait_ge(u_gelu, n0 + GJ)
                product(1, 1, None)
                product(0, 2, n0 + 1)
                for q in range(1, RING):
                    v_low_rows(q, n0 + q + 1)
                    v_low_weights(q, n0 + q + 1)
                    product(q % 2, q + 2, n0 + q + 1)
                with dve.Fori(1, GJ // RING - 1) as it:
                    for q in range(RING):
                        v_low_rows(q, it * RING + (n0 + q + 1))
                        v_low_weights(q, it * RING + (n0 + q + 1))
                        product(q % 2, it * RING + (q + 2), it * RING + (n0 + q + 1))
                for q in range(RING):
                    v_low_rows(q, n0 + GJ - RING + q + 1)
                    v_low_weights(q, n0 + GJ - RING + q + 1)
                    if q < 2:
                        product(q, GJ - 2 + q, n0 + GJ - RING + q + 1)
                if g == GROUPS - 1:
                    for k in range(KD):
                        ins = ts(gs_flat[:, k * P:(k + 1) * P], ident, gg2[:, k:k + 1], None, ALU.mult)
                    ins.then_inc(f_diag, 1)
                for t in range(TT):
                    if t == 0:
                        dve.wait_ge(v_half, g + 1)
                    else:
                        dve.wait_ge(v_mm, n0 + GJ)
                    for n in range(4):
                        y = yacc[t][:, n * 512:(n + 1) * 512]
                        ins = tt(y, y, ps[:, 4 * t + n, :], ALU.add) if g else nc.vector.tensor_copy(y, ps[:, 4 * t + n, :])
                        ins.then_inc(y_ev, 1)
            dve.wait_ge(f_gg, 1)
            for t in range(TT):
                dve.wait_ge(f_ssq, t + 1)
                if t:
                    rms(ssq[3], D).then_inc(f_aff, 1)
                tt(yacc[t][:, :], yacc[t][:, :], ps[:, 0:4, :].rearrange("p a n -> p (a n)"), ALU.mult
                   ).then_inc(y_gated, 1)
            dve.wait_ge(f_root, 1)
            link(nc.vector.reciprocal(rst[3], rst[3]))
            dve.wait_ge(x1_ld, 16)
            dve.wait_ge(y_gated, TT)
            for t in range(TT):
                stt(xs[:, t, :], yacc[t][:, :], rst[3][:, t:t + 1], xs[:, t, :], ALU.mult, ALU.add).then_inc(f_out, 1)


def kernel(**inputs):
    import concourse.bacc as bacc
    from concourse.bass_utils import run_bass_kernel_spmd

    names = ["x", "c", "w_ada", "b_ada", "g_pre_mix", "w_in", "g_q_lat", "w_uq", "g_kv_lat", "w_ukv", "g_out_mla",
             "g_out_moba", "w_out", "g_post_mix", "g_pre_ffn", "w_peer_q", "sub_keys_1", "sub_keys_2", "u_experts",
             "v_experts", "g_post_ffn"]
    nc = bacc.Bacc("TRN2", target_bir_lowering=False, num_devices=1)
    arrays = {name: np.ascontiguousarray(inputs[name]) for name in names}
    arrays["const_per"], arrays["const_front"] = tables()
    args = {name: nc.dram_tensor(name, a.shape, F32, kind="ExternalInput").ap() for name, a in arrays.items()}
    out = nc.dram_tensor("out", (1, T, D), F32, kind="ExternalOutput").ap()
    build(nc, **args, out=out)
    r = run_bass_kernel_spmd(nc, [arrays], core_ids=[0])
    return r.results[0]["out"]
```
